# Optimizing a Trainium2 kernel written in Bass

```python
import math
import jax, jax.numpy as jnp
from jax import lax
import numpy as np

D_MODEL = 1024
BATCH = 1
SEQ = 256
DEPTH = 2

N_EVEN = (DEPTH + 1) // 2
N_ODD = DEPTH // 2
PLE_DIM = 256
EPS = 1e-6

A_HEADS = 4
A_DK = 128
A_DV = 128
A_WIDTH = A_HEADS * A_DV
A_CHUNK = 64
A_CONV = 4
B_HEADS = 8
B_DH = 64
B_WIDTH = B_HEADS * B_DH
B_LATENT = 128
IDX_HEADS = 8
IDX_DIM = 64
TOPK_MAX = 256
Q_BLOCK = 128
REL_BUCKETS = 32
REL_MAX_DIST = 128
MIX_WIDTH = A_WIDTH + B_WIDTH
IN_SIZES = (A_HEADS * A_DK, A_HEADS * A_DK, A_HEADS * A_DV, A_WIDTH, A_HEADS, A_HEADS,
            B_WIDTH, B_LATENT, IDX_HEADS * IDX_DIM, IDX_DIM, IDX_HEADS)
IN_OFFSETS = tuple(int(v) for v in np.cumsum(IN_SIZES)[:-1])
D_IN_EVEN = int(sum(IN_SIZES))
POOL_WINDOWS = (2, 4, 8, 16)
POOL_GROUP = D_MODEL // len(POOL_WINDOWS)
D_FF = 3584
N_EXPERTS = 8
TOP_K_EXPERTS = 2

kernel_name = 'hybrid_mlstm_dsa_pool_moe'

def rmsnorm(x, g):
    xf = x.astype(jnp.float32)
    y = xf * lax.rsqrt(jnp.mean(xf * xf, axis=-1, keepdims=True) + EPS)
    return (y * g.astype(jnp.float32)).astype(x.dtype)

def causal_dwconv(x, w):
    k = w.shape[0]
    return lax.conv_general_dilated(x, w[:, None, :].astype(x.dtype), window_strides=(1,),
                                    padding=[(k - 1, 0)], dimension_numbers=('NWC', 'WIO', 'NWC'),
                                    feature_group_count=x.shape[-1])

def mlstm_chunkwise(q, k, v, log_i, log_f):
    b, h, s, dk = q.shape
    dv = v.shape[-1]
    nc = s // A_CHUNK

    def to_chunks(a):
        return jnp.moveaxis(a.reshape(b, h, nc, A_CHUNK, *a.shape[3:]), 2, 0)

    causal = jnp.tril(jnp.ones((A_CHUNK, A_CHUNK), dtype=bool))

    def step(carry, inp):
        c_state, n_state, m_state = carry
        qq, kk, vv, ii, ff = inp
        bcum = jnp.cumsum(ff, axis=-1)
        dmat = bcum[..., :, None] - bcum[..., None, :] + ii[..., None, :]
        dmat = jnp.where(causal, dmat, -jnp.inf)
        inter = bcum + m_state[..., None]
        m_t = jnp.maximum(inter, jnp.max(dmat, axis=-1))
        w_intra = jnp.exp(dmat - m_t[..., None])
        w_inter = jnp.exp(inter - m_t)
        scores = jnp.einsum('bhtd,bhsd->bhts', qq, kk) * w_intra
        num = (jnp.einsum('bhts,bhsv->bhtv', scores, vv)
               + w_inter[..., None] * jnp.einsum('bhtd,bhdv->bhtv', qq, c_state))
        den = jnp.sum(scores, axis=-1) + w_inter * jnp.einsum('bhtd,bhd->bht', qq, n_state)
        h_out = num / jnp.maximum(jnp.abs(den), jnp.exp(-m_t))[..., None]
        b_last = bcum[..., -1]
        g = b_last[..., None] - bcum + ii
        m_new = jnp.maximum(b_last + m_state, jnp.max(g, axis=-1))
        decay = jnp.exp(b_last + m_state - m_new)
        wk = jnp.exp(g - m_new[..., None])
        c_new = decay[..., None, None] * c_state + jnp.einsum('bhs,bhsd,bhsv->bhdv', wk, kk, vv)
        n_new = decay[..., None] * n_state + jnp.einsum('bhs,bhsd->bhd', wk, kk)
        return (c_new, n_new, m_new), h_out

    init = (jnp.zeros((b, h, dk, dv), jnp.float32), jnp.zeros((b, h, dk), jnp.float32),
            jnp.zeros((b, h), jnp.float32))
    _, hs = lax.scan(step, init, tuple(map(to_chunks, (q, k, v, log_i, log_f))))
    return jnp.moveaxis(hs, 0, 2).reshape(b, h, s, dv)

def t5_bucket(dist):
    max_exact = REL_BUCKETS // 2
    logd = jnp.log(jnp.maximum(dist, 1).astype(jnp.float32) / max_exact)
    large = max_exact + (logd / math.log(REL_MAX_DIST / max_exact) * (REL_BUCKETS - max_exact)).astype(jnp.int32)
    large = jnp.minimum(large, REL_BUCKETS - 1)
    return jnp.where(dist < max_exact, dist, large)

def dsa_attention(q, k, c, q_idx, k_idx, w_idx, w_uv, rel_bias):
    b, s = q.shape[0], q.shape[1]
    topk = min(TOPK_MAX, s // 4)
    nb = s // Q_BLOCK
    key_pos = jnp.arange(s)
    scale = B_DH ** -0.5
    gather = jax.vmap(lambda a, i: a[i])

    def blocks(a):
        return jnp.moveaxis(a.reshape(b, nb, Q_BLOCK, *a.shape[2:]), 1, 0)

    def one_block(args):
        qb, qib, wb, t0 = args
        t = t0 + jnp.arange(Q_BLOCK)
        isc = jax.nn.relu(jnp.einsum('bqhd,bsd->bqhs', qib, k_idx).astype(jnp.float32))
        isc = jnp.einsum('bqhs,bqh->bqs', isc, wb.astype(jnp.float32))
        isc = jnp.where(key_pos[None, None, :] <= t[None, :, None], isc, -jnp.inf)
        _, idx = lax.top_k(isc, topk)
        valid = idx <= t[None, :, None]
        k_sel = gather(k, idx)
        c_sel = gather(c, idx)
        logits = jnp.einsum('bqhd,bqkd->bhqk', qb, k_sel).astype(jnp.float32) * scale
        bucket = t5_bucket(jnp.maximum(t[None, :, None] - idx, 0))
        logits = logits + jnp.moveaxis(rel_bias[bucket], -1, 1).astype(jnp.float32)
        logits = jnp.where(valid[:, None], logits, -jnp.inf)
        probs = jax.nn.softmax(logits, axis=-1).astype(c.dtype)
        o_lat = jnp.einsum('bhqk,bqkc->bqhc', probs, c_sel)
        return jnp.einsum('bqhc,hcd->bqhd', o_lat, w_uv)

    t0s = jnp.arange(nb, dtype=jnp.int32) * Q_BLOCK
    out = lax.map(one_block, (blocks(q), blocks(q_idx), blocks(w_idx), t0s))
    return jnp.moveaxis(out, 0, 1).reshape(b, s, B_WIDTH)

def even_mixer(y, w_in, b_gate, conv_w, g_h, g_q, g_k, g_kv, w_uk, w_uv, w_out, rel_bias):
    b, s, _ = y.shape
    proj = y @ w_in
    aq, ak, av, ao, ai, af, bq, bc, bqi, bki, bwi = jnp.split(proj, IN_OFFSETS, axis=-1)
    qk = jax.nn.silu(causal_dwconv(jnp.concatenate([aq, ak], axis=-1), conv_w))
    aq, ak = jnp.split(qk, 2, axis=-1)

    def heads(a, nh):
        return a.reshape(b, s, nh, -1).transpose(0, 2, 1, 3).astype(jnp.float32)

    qa = heads(aq, A_HEADS)
    ka = heads(ak, A_HEADS) * (A_DK ** -0.5)
    va = heads(av, A_HEADS)
    log_i = (ai + b_gate[:A_HEADS]).astype(jnp.float32).transpose(0, 2, 1)
    log_f = jax.nn.log_sigmoid((af + b_gate[A_HEADS:]).astype(jnp.float32)).transpose(0, 2, 1)
    h_a = mlstm_chunkwise(qa, ka, va, log_i, log_f)
    h_a = rmsnorm(h_a, g_h.reshape(A_HEADS, 1, A_DV))
    h_a = h_a.transpose(0, 2, 1, 3).reshape(b, s, A_WIDTH).astype(y.dtype) * jax.nn.sigmoid(ao)
    qb = rmsnorm(bq.reshape(b, s, B_HEADS, B_DH), g_q)
    lat = rmsnorm(bc, g_kv)
    kb = rmsnorm(lat @ w_uk, g_k)
    h_b = dsa_attention(qb, kb, lat, bqi.reshape(b, s, IDX_HEADS, IDX_DIM), bki, bwi, w_uv, rel_bias)
    return jnp.concatenate([h_a, h_b], axis=-1) @ w_out

def pool_mixer(y, w_pool, scale):
    b, s, d = y.shape
    yf = y.astype(jnp.float32)
    cs0 = jnp.pad(jnp.cumsum(yf, axis=1), ((0, 0), (1, 0), (0, 0)))
    pos = jnp.arange(1, s + 1, dtype=jnp.float32)[None, :, None]
    outs = []
    for g, win in enumerate(POOL_WINDOWS):
        sl = slice(g * POOL_GROUP, (g + 1) * POOL_GROUP)
        c = cs0[:, :, sl]
        lower = jnp.pad(c, ((0, 0), (win - 1, 0), (0, 0)))[:, :s]
        mean = (c[:, 1:] - lower) / jnp.minimum(pos, win)
        pooled = (mean - yf[:, :, sl]).astype(y.dtype)
        outs.append(pooled @ w_pool[g])
    return jnp.concatenate(outs, axis=-1) * scale

def swiglu(y, wg, wu, wd):
    return (jax.nn.silu(y @ wg) * (y @ wu)) @ wd

def moe(y, w_router, b_router, wg, wu, wd):
    logits = (y @ w_router).astype(jnp.float32) + b_router.astype(jnp.float32)
    top_v, top_i = lax.top_k(logits, TOP_K_EXPERTS)
    gates = jax.nn.softmax(top_v, axis=-1)
    combine = jnp.sum(jax.nn.one_hot(top_i, N_EXPERTS, dtype=jnp.float32) * gates[..., None], axis=-2)
    out = jnp.zeros_like(y)
    for e in range(N_EXPERTS):
        out = out + combine[..., e:e + 1].astype(y.dtype) * swiglu(y, wg[e], wu[e], wd[e])
    return out

def setup_inputs(seed: int = 0) -> dict:
    key = jax.random.key(seed)
    ks = iter(jax.random.split(key, 40))

    def nrm(shape, scale):
        return jax.random.normal(next(ks), shape, jnp.float32) * scale

    def gain(shape):
        return 1.0 + nrm(shape, 0.1)

    return {
        'x': nrm((BATCH, SEQ, D_MODEL), 1.0),
        'p': nrm((DEPTH, BATCH, SEQ, PLE_DIM), 1.0),
        'norm_mix': gain((DEPTH, D_MODEL)),
        'norm_ffn': gain((DEPTH, D_MODEL)),
        'w_in_e': nrm((N_EVEN, D_MODEL, D_IN_EVEN), D_MODEL ** -0.5),
        'b_gate_e': jnp.concatenate([nrm((N_EVEN, A_HEADS), 0.1), 3.0 + nrm((N_EVEN, A_HEADS), 0.5)], axis=-1),
        'conv_a': nrm((N_EVEN, A_CONV, 2 * A_HEADS * A_DK), A_CONV ** -0.5),
        'norm_h_a': gain((N_EVEN, A_WIDTH)),
        'norm_q_b': gain((N_EVEN, B_DH)),
        'norm_k_b': gain((N_EVEN, B_DH)),
        'norm_kv_b': gain((N_EVEN, B_LATENT)),
        'w_uk_b': nrm((N_EVEN, B_LATENT, B_DH), B_LATENT ** -0.5),
        'w_uv_b': nrm((N_EVEN, B_HEADS, B_LATENT, B_DH), B_LATENT ** -0.5),
        'w_out_e': nrm((N_EVEN, MIX_WIDTH, D_MODEL), MIX_WIDTH ** -0.5),
        'rel_bias': nrm((REL_BUCKETS, B_HEADS), 0.5),
        'w_pool': nrm((N_ODD, len(POOL_WINDOWS), POOL_GROUP, POOL_GROUP), POOL_GROUP ** -0.5),
        'scale_pool': gain((N_ODD, D_MODEL)),
        'w_gate_d': nrm((N_EVEN, D_MODEL, D_FF), D_MODEL ** -0.5),
        'w_up_d': nrm((N_EVEN, D_MODEL, D_FF), D_MODEL ** -0.5),
        'w_down_d': nrm((N_EVEN, D_FF, D_MODEL), D_FF ** -0.5),
        'w_router': nrm((N_ODD, D_MODEL, N_EXPERTS), D_MODEL ** -0.5),
        'b_router': nrm((N_ODD, N_EXPERTS), 0.01),
        'w_gate_m': nrm((N_ODD, N_EXPERTS, D_MODEL, D_FF), D_MODEL ** -0.5),
        'w_up_m': nrm((N_ODD, N_EXPERTS, D_MODEL, D_FF), D_MODEL ** -0.5),
        'w_down_m': nrm((N_ODD, N_EXPERTS, D_FF, D_MODEL), D_FF ** -0.5),
        'w_ple': nrm((DEPTH, PLE_DIM, D_MODEL), PLE_DIM ** -0.5),
        'w_ple_gate': nrm((DEPTH, D_MODEL, D_MODEL), D_MODEL ** -0.5),
        'norm_ple': gain((DEPTH, D_MODEL)),
    }

def reference(x, p, norm_mix, norm_ffn, w_in_e, b_gate_e, conv_a, norm_h_a, norm_q_b, norm_k_b,
              norm_kv_b, w_uk_b, w_uv_b, w_out_e, rel_bias, w_pool, scale_pool, w_gate_d, w_up_d,
              w_down_d, w_router, b_router, w_gate_m, w_up_m, w_down_m, w_ple, w_ple_gate, norm_ple):
    h = x
    for i in range(DEPTH):
        y = rmsnorm(h, norm_mix[i])
        if i % 2 == 0:
            e = i // 2
            h = h + even_mixer(y, w_in_e[e], b_gate_e[e], conv_a[e], norm_h_a[e], norm_q_b[e],
                               norm_k_b[e], norm_kv_b[e], w_uk_b[e], w_uv_b[e], w_out_e[e], rel_bias)
            y = rmsnorm(h, norm_ffn[i])
            h = h + swiglu(y, w_gate_d[e], w_up_d[e], w_down_d[e])
        else:
            o = i // 2
            h = h + pool_mixer(y, w_pool[o], scale_pool[o])
            y = rmsnorm(h, norm_ffn[i])
            h = h + moe(y, w_router[o], b_router[o], w_gate_m[o], w_up_m[o], w_down_m[o])
        gate = jax.nn.sigmoid(rmsnorm(h, norm_ple[i]) @ w_ple_gate[i])
        h = h + (p[i] @ w_ple[i]) * gate
    return h


_drawn_inputs = setup_inputs


def setup_inputs(seed=0):
    import zlib

    import numpy as np

    out = dict(_drawn_inputs(seed))
    spreads = {}
    factors = {'b_router': 2.944}
    for name, (base, spread) in spreads.items():
        noise = np.random.default_rng([zlib.crc32(name.encode()), seed]).standard_normal(out[name].shape)
        drawn = base * np.exp(spread * noise) if base else spread * noise
        out[name] = __import__('jax').numpy.asarray(drawn.astype(out[name].dtype))
    for name, factor in factors.items():
        out[name] = (out[name] * factor).astype(out[name].dtype)
    return out
```

```python
import math

import numpy as np
import concourse.bass as bass
from concourse import mybir

F32 = mybir.dt.float32
F32R = mybir.dt.float32r
I32 = mybir.dt.int32
U32 = mybir.dt.uint32
ALU = mybir.AluOpType
ACT = mybir.ActivationFunctionType
AX_X = mybir.AxisListType.X

P = 128
D = 1024
KD = D // P
SEQ = 256
T = SEQ // P
EPS = 1e-6
A_HEADS, A_DK = 4, 128
B_HEADS, B_DH, B_LATENT = 8, 64, 128
TOPK = 64
BUCKETS, MAX_DIST = 32, 128
OFF_AQ, OFF_AV, OFF_AO, OFF_AI, OFF_AF = 0, 1024, 1536, 2048, 2052
OFF_BQ, OFF_BC, OFF_QI, OFF_KI, OFF_WI, D_IN = 2056, 2568, 2696, 3208, 3272, 3280
CONV = 4
WINDOWS = (2, 4, 8, 16)
F_FF = 3584
N_EXP = 8
PLE = 256
FC = 512
N_CH = F_FF // FC
NEG = -1e30
ACAUSAL, TAKEN = -3.0e38, -3.3e38
BIAS_W = 384

UNITS = [("U", 0), ("G", 0)]
for _c in range(1, N_CH):
    UNITS += [("U", _c), ("G", _c), ("D", _c - 1)]
UNITS.append(("D", N_CH - 1))
N_UNITS = len(UNITS)
AT = {u: n for n, u in enumerate(UNITS)}
RING = 3
QUARTERS = 4
assert N_UNITS % RING == 0


class Signal:

    def __init__(self, nc, name):
        self.sem, self.base, self.name = nc.alloc_semaphore(name), 0, name

    def by(self, ins, n=1):
        return ins.then_inc(self.sem, n)

    def wait(self, eng, n):
        eng.wait_ge(self.sem, n + self.base)

    def past(self, n):
        self.base += n


def constants():
    d = np.arange(SEQ)
    exact = BUCKETS // 2
    log = np.log(np.maximum(d, 1).astype(np.float32) / np.float32(exact)) / np.float32(math.log(MAX_DIST / exact))
    large = np.minimum(exact + (log * (BUCKETS - exact)).astype(np.int32), BUCKETS - 1)
    bucket = np.where(d < exact, d, large)
    bias_onehot = np.zeros((BUCKETS, BIAS_W), np.float32)
    for j in range(SEQ):
        bias_onehot[bucket[SEQ - 1 - j], j] = 1.0
    select = np.zeros((A_HEADS, A_HEADS * P), np.float32)
    for hd in range(A_HEADS):
        select[hd, hd * P:(hd + 1) * P] = 1.0
    halves = np.zeros((P, 2), np.float32)
    halves[:B_DH, 0] = 1.0
    halves[B_DH:, 1] = 1.0
    pos = np.arange(1, SEQ + 1, dtype=np.float32)
    inv = np.stack([np.float32(1.0) / np.minimum(pos, np.float32(w)) for w in WINDOWS])
    return {
        "c_ident": np.eye(P, dtype=np.float32),
        "c_before": np.triu(np.ones((P, P), np.float32), 1),
        "c_bias": bias_onehot,
        "c_select": select,
        "c_halves": halves,
        "c_invpos": inv.astype(np.float32),
        "c_iota": np.arange(P, dtype=np.float32)[None, :],
    }


def build(nc, a, out, stop=None):
    limit = nc.sbuf_usable_end
    bottom = -(-nc.sbuf_base // 64) * 64
    at = [bottom]

    def place(name, shape, dtype=F32, offset=None):
        n = int(np.prod(shape[1:])) * 4
        if offset is None:
            offset, at[0] = at[0], at[0] + -(-n // 64) * 64
        assert offset % 4 == 0 and offset + n <= limit, (name, offset, n, limit)
        return nc.alloc_sbuf_tensor_at(name, tuple(shape), dtype, offset=offset)

    def region(size):
        o = at[0]
        at[0] += size
        assert at[0] <= limit, (at[0], limit)
        return o

    def inside(base, size):
        o = [base]

        def put(name, shape, dtype=F32):
            n = -(-int(np.prod(shape[1:])) * 4 // 64) * 64
            t = place(name, shape, dtype, offset=o[0])
            o[0] += n
            assert o[0] <= base + size, (name, o[0] - base, size)
            return t
        return put

    h = place("h", (P, T, D))
    ident = place("ident", (P, P))
    before = place("before", (P, P))
    ones = place("ones", (P, P))
    gains = place("gains", (P, P))
    stat = place("stat", (P, 64))
    bias_i = place("bias_i", (A_HEADS, 1))
    bias_f = place("bias_f", (A_HEADS, 1))
    eps_col = place("eps_col", (P, 1))
    one_col = place("one_col", (P, 1))
    over_at = region(64)
    y = place("y", (P, T, D))

    ffn_small = region(16384 + 3 * 2048 + 3 * 2048 + 2 * 4096)
    put = inside(ffn_small, 16384 + 6 * 2048 + 2 * 4096)
    x_hi = put("x_hi", (P, KD, SEQ), F32R)
    x_lo = put("x_lo", (P, KD, SEQ), F32R)
    hid = [put(f"hid{t}", (P, FC)) for t in range(T)]
    hidT_hi = [put(f"hidT_hi{t}", (P, 4, P), F32R) for t in range(T)]
    hidT_lo = [put(f"hidT_lo{t}", (P, 4, P), F32R) for t in range(T)]
    slot_out = put("slot_out", (P, D))
    z_free_at = ffn_small + 16384 + 6 * 2048 + 4096
    UNIT_B = 16384
    ring_raw = region(RING * UNIT_B)
    ring_split = region(2 * RING * UNIT_B)
    raw = [place(f"raw{s}", (P, 4096), offset=ring_raw + s * UNIT_B) for s in range(RING)]
    w_hi = [place(f"w_hi{s}", (P, 4096), F32R, offset=ring_split + 2 * s * UNIT_B) for s in range(RING)]
    w_lo = [place(f"w_lo{s}", (P, 4096), F32R, offset=ring_split + (2 * s + 1) * UNIT_B) for s in range(RING)]
    arena, arena_n = ring_raw, 3 * RING * UNIT_B

    ps = nc.alloc_psum_tensor("ps", (P, 8, 512), F32)

    names = {}

    def sig(name):
        if name not in names:
            names[name] = Signal(nc, name)
        return names[name]

    def finished(**counts):
        for name, n in counts.items():
            sig(name).past(n)

    def linker(eng, name):
        s = sig(name)
        count = [0]

        def link(ins):
            count[0] += 1
            ins.then_inc(s.sem, 1)
            eng.wait_ge(s.sem, s.base + count[0])

        link.end = lambda: s.past(count[0])
        return link

    ROW_MIX, ROW_FFN, ROW_PLE, ROW_CONV, ROW_GQ, ROW_GK = 0, 16, 32, 48, 80, 81
    N_ROWS = 82

    w_in = place("w_in", (P, KD, D_IN), offset=arena)
    W_IN_B = KD * D_IN * 4
    t1 = inside(arena + W_IN_B, arena_n - W_IN_B)
    qk = t1("qk", (P, 8, SEQ))
    v_ones = t1("v_ones", (P, T, A_HEADS, 129))
    ao = t1("ao", (P, T, 512))
    qi = t1("qi", (P, 4, SEQ))
    bqT = t1("bqT", (P, 4, SEQ))
    ki2 = t1("ki2", (P, SEQ))
    bc = t1("bc", (P, T, B_LATENT))
    wi = t1("wi", (P, T, 8))
    gate_i = t1("gate_i", (A_HEADS, SEQ))
    gate_f = t1("gate_f", (A_HEADS, SEQ))
    t2 = inside(ffn_small, 16384 + 6 * 2048 + 2 * 4096)
    yT = t2("yT_mix", (P, KD, SEQ))
    conv_in = t2("conv_in", (P, 8, CONV - 1 + SEQ))
    bias_toe = t2("bias_toe", (P, B_HEADS, SEQ))
    params = t2("params", (P, P))
    gh_b = t2("gh_b", (P, 512))
    gkv_b = t2("gkv_b", (P, B_LATENT))
    assert nc is not None
    rel8 = place("rel8", (BUCKETS, B_HEADS), offset=ring_split + 5 * UNIT_B - 64 * 4)

    t3 = inside(arena, W_IN_B)
    w_uk = t3("w_uk", (P, B_DH))
    w_uv = t3("w_uv", (P, B_HEADS, B_DH))
    w_o = t3("w_o", (P, KD, D))
    sel_h = t3("sel_h", (A_HEADS, A_HEADS * P))
    halves = t3("halves", (P, 2))
    hcat = t3("hcat", (P, T, D))
    g1 = t3("g1", (A_HEADS, SEQ))
    g2 = t3("g2", (A_HEADS, SEQ))
    g3 = t3("g3", (A_HEADS, SEQ))
    g4 = t3("g4", (A_HEADS, SEQ))
    cols = t3("cols", (P, T, 8))
    wT = t3("wT", (P, A_HEADS, 384))
    small = t3("small", (P, 128))
    kb2 = t3("kb2", (P, T, P))
    kbT = t3("kbT", (P, SEQ))
    lat = t3("lat", (P, T, B_LATENT))
    latT = t3("latT", (P, SEQ))
    vu = t3("vu", (P, T, 512))
    isc = t3("isc", (P, SEQ))
    top8 = t3("top8", (P, 8))
    big = t3("big", (P, B_HEADS, SEQ))
    t3b = inside(ffn_small, 16384)
    probT = t3b("probT", (P, 16, P))
    hT = t3b("hcatT", (P, KD, SEQ))

    scratch_b = nc.dram_tensor("bias_scratch", [P * B_HEADS * BIAS_W], F32)
    t4 = inside(arena, 65536)
    bias_rows = t4("bias_rows", (P, B_HEADS, BIAS_W))
    rel_wide = t4("rel_wide", (BUCKETS, B_HEADS, P))
    bias_oh = t4("bias_oh", (BUCKETS, BIAS_W))

    w_in_v = a["w_in_e"][0].rearrange("(k p) n -> p k n", p=P)
    IN_GROUPS = [(0, 512), (512, 1024), (2048, 2056), (1024, 1536), (1536, 2048), (2056, 2568), (2696, 3280), (2568, 2696)]

    def dve_const(e, link):
        link(e.memset(ones[:, :], 1.0))
        link(e.memset(eps_col[:, :], EPS))
        link(e.memset(one_col[:, :], 1.0))

    with nc.Block() as block:
        @block.sync
        def _(e):
            s = sig("param_loaded")
            for t in range(T):
                s.by(e.dma_start(h[:, t, :], a["x"][0, t * P:(t + 1) * P, :]), 16)
            s.by(e.dma_start(ident[:, :], a["c_ident"]), 16)
            s.by(e.dma_start(before[:, :], a["c_before"]), 16)
            for row, name in ((ROW_MIX, "norm_mix"), (ROW_FFN, "norm_ffn"), (ROW_PLE, "norm_ple")):
                s.by(e.dma_start(params[row:row + 16, :], a[name].rearrange("l (k p) -> (l k) p", p=P)), 16)
            s.by(e.dma_start(params[ROW_CONV:ROW_CONV + 32, :], a["conv_a"][0].rearrange("j (k p) -> (j k) p", p=P)), 16)
            for row, name in ((ROW_GQ, "norm_q_b"), (ROW_GK, "norm_k_b")):
                for half in range(2):
                    s.by(e.dma_start(params[row:row + 1, half * B_DH:(half + 1) * B_DH], a[name]), 16)
            s.by(e.dma_start(rel8[:, :], a["rel_bias"]), 16)
            s.by(e.dma_start(bias_oh[:, :], a["c_bias"]), 16)
            b8 = a["b_gate_e"].rearrange("a (g n) -> g n a", g=2)
            s.by(e.dma_start(bias_i[:, :], b8[0]), 16)
            s.by(e.dma_start(bias_f[:, :], b8[1]), 16)
            s.by(e.dma_start(gh_b[:, :], a["norm_h_a"].partition_broadcast(P)[:, 0, :]), 16)
            s.by(e.dma_start(gkv_b[:, :], a["norm_kv_b"].partition_broadcast(P)[:, 0, :]), 16)
            sig("bias_rows").wait(e, B_HEADS)
            sig("bias_out").by(e.dma_start(scratch_b[:].rearrange("(p x) -> p x", p=P),
                                           bias_rows[:, :, :].rearrange("p a b -> p (a b)")), 16)
            sig("bias_out").wait(e, 16)
            x = B_HEADS * BIAS_W - 1
            skewed = scratch_b[P - 1:P - 1 + P * x].rearrange("(p x) -> p x", x=x)
            for hd in range(B_HEADS):
                sig("bias_in").by(e.dma_start(bias_toe[:, hd, :], skewed[:, hd * BIAS_W:hd * BIAS_W + SEQ]), 16)
            sig("bias_in").wait(e, 16 * B_HEADS)

        @block.vector
        def _(e):
            link = linker(e, "dve_step")
            dve_const(e, link)
            link(e.memset(conv_in[:, :, 0:CONV - 1], 0.0))
            sig("param_loaded").wait(e, 16 * N_PARAM_DMAS)
            sig("rel_wide").by(e.tensor_copy(rel_wide[:, :, :], rel8[:, :].unsqueeze(2).to_broadcast([BUCKETS, B_HEADS, P])))
            sig("params_T").wait(e, 1)
            e.tensor_copy(gains[:, 0:N_ROWS], ps[:, 0, 0:N_ROWS]).then_inc(sig("gains").sem, 1)
            link.end()

        @block.tensor
        def _(e):
            sig("param_loaded").wait(e, 16 * N_PARAM_DMAS)
            sig("params_T").by(e.transpose(ps[:, 0, 0:N_ROWS], params[0:N_ROWS, :], ident[0:N_ROWS, 0:N_ROWS]))
            sig("rel_wide").wait(e, 1)
            sig("gains").wait(e, 1)
            for hd in range(B_HEADS):
                sig("bias_mm").by(e.matmul(ps[:, hd, 0:BIAS_W], rel_wide[:, hd, :], bias_oh[:, :], start=True, stop=True))

        @block.scalar
        def _(e):
            for hd in range(B_HEADS):
                sig("bias_mm").wait(e, hd + 1)
                sig("bias_rows").by(e.copy(bias_rows[:, hd, :], ps[:, hd, 0:BIAS_W]))
    finished(param_loaded=16 * N_PARAM_DMAS)

    def norm_T(row, split, yT=None, want_y=False, load=None):
        with nc.Block() as block:
            if load is not None:
                @block.sync
                def _(e):
                    load(e)

            @block.scalar
            def _(e):
                for t in range(T):
                    sig("squares").by(e.activation(y[:, t, :], h[:, t, :], ACT.Square, accum_out=stat[:, t:t + 1]))
                sig("squares").wait(e, T)
                sig("rms").by(e.activation(stat[:, 2:4], stat[:, 0:2], ACT.Sqrt, bias=eps_col[:, :], scale=1.0 / D))
                if not split:
                    for b in range(4):
                        sig("y_T").wait(e, b + 1)
                        for k in (2 * b, 2 * b + 1):
                            j = k % 2
                            ins = e.activation(yT[:, k, :], ps[:, b, j * SEQ:(j + 1) * SEQ], ACT.Copy,
                                               scale=gains[:, row + k:row + k + 1])
                        sig("yT_hi").by(ins)
                else:
                    for b in range(4):
                        sig("y_T").wait(e, b + 1)
                        for k in (2 * b, 2 * b + 1):
                            j = k % 2
                            ins = e.activation(x_hi[:, k, :], ps[:, b, j * SEQ:(j + 1) * SEQ], ACT.Copy,
                                               scale=gains[:, row + k:row + k + 1])
                        sig("yT_hi").by(ins)

            @block.vector
            def _(e):
                link = linker(e, "dve_step")
                sig("rms").wait(e, 1)
                link(e.reciprocal(stat[:, 4:6], stat[:, 2:4]))
                for t in range(T):
                    sig("y_ready").by(e.tensor_scalar(y[:, t, :], h[:, t, :], stat[:, 4 + t:5 + t], None, ALU.mult))
                if split:
                    for b in range(4):
                        sig("yT_hi").wait(e, b + 1)
                        for k in (2 * b, 2 * b + 1):
                            j = k % 2
                            e.scalar_tensor_tensor(out=x_lo[:, k, :], in0=ps[:, b, j * SEQ:(j + 1) * SEQ],
                                                   scalar=gains[:, row + k:row + k + 1],
                                                   in1=x_hi[:, k, :].bitcast(F32), op0=ALU.mult, op1=ALU.subtract)
                link.end()

            @block.tensor
            def _(e):
                sig("y_ready").wait(e, T)
                for b in range(4):
                    for k in (2 * b, 2 * b + 1):
                        for t in range(T):
                            o = (k % 2) * SEQ + t * P
                            ins = e.transpose(ps[:, b, o:o + P], y[:, t, k * P:(k + 1) * P], ident[:, :])
                    sig("y_T").by(ins)
        finished(squares=T, rms=1, y_ready=T, y_T=4, yT_hi=4)

    def load_w_in(e):
        for n, (lo, hi) in enumerate(IN_GROUPS):
            sig(f"w_in{n}").by(e.dma_start(w_in[:, :, lo:hi], w_in_v[:, :, lo:hi]), 16)

    norm_T(ROW_MIX, False, yT=yT, load=load_w_in)

    def dump():
        with nc.Block() as block:
            @block.sync
            def _(e):
                for t in range(T):
                    sig("out").by(e.dma_start(out[0, t * P:(t + 1) * P, :], h[:, t, :]), 16)
                sig("out").wait(e, 16 * T)

    with nc.Block() as block:
        @block.tensor
        def _(e):
            n = [0]

            def bank(group):
                b = n[0]
                sig(f"w_in{group}").wait(e, 16)
                if b >= 8:
                    sig("proj_out").wait(e, b - 7)
                n[0] += 1
                return b % 8

            def by_channel(b, col, pair, width=P, part=0):
                for k in range(KD):
                    ins = e.matmul(ps[part:part + width, b, pair * SEQ:(pair + 1) * SEQ], w_in[:, k, col:col + width],
                                   yT[:, k, :], start=(k == 0), stop=(k == KD - 1))
                return ins

            def by_token(b, t, col, width, at=0):
                for k in range(KD):
                    ins = e.matmul(ps[:, b, at:at + width], yT[:, k, t * P:(t + 1) * P], w_in[:, k, col:col + width],
                                   start=(k == 0), stop=(k == KD - 1))
                return ins

            for m in range(4):
                b = bank(m // 2)
                by_channel(b, OFF_AQ + 2 * m * P, 0)
                sig("proj_mm").by(by_channel(b, OFF_AQ + (2 * m + 1) * P, 1))
            b = bank(2)
            by_channel(b, OFF_AI, 0, A_HEADS)
            sig("proj_mm").by(by_channel(b, OFF_AF, 1, A_HEADS))
            for g, col in ((3, OFF_AV), (4, OFF_AO)):
                for t in range(T):
                    b = bank(g)
                    sig("proj_mm").by(by_token(b, t, col, 512))
            for g, col in ((5, OFF_BQ), (6, OFF_QI)):
                for m in range(2):
                    b = bank(g)
                    by_channel(b, col + 2 * m * P, 0)
                    sig("proj_mm").by(by_channel(b, col + (2 * m + 1) * P, 1))
            b = bank(6)
            by_channel(b, OFF_KI, 0, B_DH, 0)
            sig("proj_mm").by(by_channel(b, OFF_KI, 0, B_DH, B_DH))
            for t in range(T):
                b = bank(7)
                by_token(b, t, OFF_BC, B_LATENT)
                sig("proj_mm").by(by_token(b, t, OFF_WI, 8, B_LATENT))

        @block.scalar
        def _(e):
            n = [0]

            def nxt():
                n[0] += 1
                sig("proj_mm").wait(e, n[0])
                return (n[0] - 1) % 8

            for m in range(4):
                b = nxt()
                sig("proj_out").by(e.copy(conv_in[:, 2 * m:2 * m + 2, CONV - 1:],
                                          ps[:, b, :].rearrange("p (j s) -> p j s", j=2)))
            b = nxt()
            e.activation(gate_i[:, :], ps[0:A_HEADS, b, 0:SEQ], ACT.Identity, bias=bias_i[:, :])
            sig("proj_out").by(e.activation(gate_f[:, :], ps[0:A_HEADS, b, SEQ:2 * SEQ], ACT.Identity, bias=bias_f[:, :]))
            for t in range(T):
                b = nxt()
                sig("proj_out").by(e.copy(v_ones[:, t, :, 0:P], ps[:, b, :].rearrange("p (h d) -> p h d", h=A_HEADS)))
            for t in range(T):
                b = nxt()
                sig("proj_out").by(e.activation(ao[:, t, :], ps[:, b, :], ACT.Sigmoid))
            for dst in (bqT, qi):
                for m in range(2):
                    b = nxt()
                    sig("proj_out").by(e.copy(dst[:, 2 * m:2 * m + 2, :], ps[:, b, :].rearrange("p (j s) -> p j s", j=2)))
            b = nxt()
            sig("proj_out").by(e.copy(ki2[:, :], ps[:, b, 0:SEQ]))
            for t in range(T):
                b = nxt()
                e.copy(bc[:, t, :], ps[:, b, 0:B_LATENT])
                sig("proj_out").by(e.copy(wi[:, t, :], ps[:, b, B_LATENT:B_LATENT + 8]))
            for c in range(8):
                sig("conv").wait(e, c + 1)
                e.activation(qk[:, c, :], qk[:, c, :], ACT.Silu)

        @block.vector
        def _(e):
            link = linker(e, "dve_step")
            e.memset(v_ones[:, :, :, P:P + 1], 1.0)
            for c in range(8):
                sig("proj_out").wait(e, c // 2 + 1)
                w = lambda j: gains[:, ROW_CONV + 8 * j + c:ROW_CONV + 8 * j + c + 1]
                link(e.tensor_scalar(qk[:, c, :], conv_in[:, c, 0:SEQ], w(0), None, ALU.mult))
                for j in range(1, CONV):
                    ins = e.scalar_tensor_tensor(out=qk[:, c, :], in0=conv_in[:, c, j:j + SEQ], scalar=w(j),
                                                 in1=qk[:, c, :], op0=ALU.mult, op1=ALU.add)
                    if j < CONV - 1:
                        link(ins)
                sig("conv").by(ins)
            link.end()
    finished(proj_mm=16, proj_out=16, conv=8)

    with nc.Block() as block:
        @block.sync
        def _(e):
            s = sig("mix_loaded")
            s.by(e.dma_start(sel_h[:, :], a["c_select"]), 16)
            s.by(e.dma_start(w_uk[:, :], a["w_uk_b"][0]), 16)
            s.by(e.dma_start(w_uv[:, :, :], a["w_uv_b"][0].rearrange("h c d -> c h d")), 16)
            s.by(e.dma_start(halves[:, :], a["c_halves"]), 16)
            s.by(e.dma_start(w_o[:, :, :], a["w_out_e"][0].rearrange("(k p) n -> p k n", p=P)), 16)
            s.wait(e, 16 * 5)

        @block.vector
        def _(e):
            link = linker(e, "dve_step")
            sig("absf").by(e.scalar_tensor_tensor(out=g1[:, :], in0=gate_f[:, :], scalar=-1.0, in1=gate_f[:, :],
                                                  op0=ALU.mult, op1=ALU.max))
            sig("softplus").wait(e, 1)
            link(e.scalar_tensor_tensor(out=g2[:, :], in0=gate_f[:, :], scalar=0.0, in1=g1[:, :],
                                        op0=ALU.min, op1=ALU.subtract))
            one_row = wT[0:A_HEADS, 0, 0:SEQ]
            link(e.memset(one_row, 1.0))
            link(e.tensor_tensor_scan(g3[:, :], one_row, g2[:, :], 0.0, ALU.mult, ALU.add))
            link(e.tensor_tensor(g1[:, :], gate_i[:, :], g3[:, :], ALU.subtract))
            link(e.tensor_tensor_scan(g2[:, :], one_row, g1[:, :], 0.0, ALU.mult, ALU.max))
            sig("gate_rows").by(e.scalar_tensor_tensor(out=g4[:, :], in0=g3[:, :], scalar=-1.0, in1=g2[:, :],
                                                       op0=ALU.mult, op1=ALU.subtract))
            for hd in range(A_HEADS):
                sig("qk_mm").wait(e, hd + 1)
                sig("w_masked").wait(e, 1)
                sig("scores").by(e.scalar_tensor_tensor(out=wT[:, hd, :], in0=ps[:, 4 + hd, 0:384], scalar=A_DK ** -0.5,
                                                        in1=wT[:, hd, :], op0=ALU.mult, op1=ALU.mult))
            den, rden = small[:, 0:8], small[:, 8:16]
            for t in range(T):
                link(e.tensor_tensor(ao[:, t, :], ao[:, t, :], gh_b[:, :], ALU.mult))
            sig("num_mm").wait(e, 1)
            for t in range(T):
                for g in range(2):
                    link(e.tensor_copy(small[:, 4 * t + 2 * g:4 * t + 2 * g + 2],
                                       ps[:, 2 * t + g, 0:258].rearrange("p (h d) -> p h d", h=2)[:, :, 128]))
            link(e.scalar_tensor_tensor(out=rden, in0=den, scalar=-1.0, in1=den, op0=ALU.mult, op1=ALU.max))
            link(e.tensor_tensor(rden, rden, small[:, 16:24], ALU.max))
            link(e.reciprocal(den, rden))
            for t in range(T):
                for hd in range(A_HEADS):
                    o = (hd % 2) * 129
                    ins = e.tensor_scalar(hcat[:, t, hd * P:(hd + 1) * P], ps[:, 2 * t + hd // 2, o:o + P],
                                          small[:, 4 * t + hd:4 * t + hd + 1], None, ALU.mult)
                    sig("h_raw").by(ins)
            sig("h_rms").wait(e, 1)
            link(e.reciprocal(small[:, 32:40], small[:, 24:32]))
            for t in range(T):
                for hd in range(A_HEADS):
                    c = slice(hd * P, (hd + 1) * P)
                    e.scalar_tensor_tensor(out=hcat[:, t, c], in0=hcat[:, t, c], scalar=small[:, 32 + 4 * t + hd:33 + 4 * t + hd],
                                           in1=ao[:, t, c], op0=ALU.mult, op1=ALU.mult)
            link.end()

        @block.scalar
        def _(e):
            link = linker(e, "act_step")
            sig("absf").wait(e, 1)
            link(e.activation(g1[:, :], g1[:, :], ACT.Exp, scale=-1.0))
            sig("softplus").by(e.activation(g1[:, :], g1[:, :], ACT.Ln, bias=one_col[0:A_HEADS, :]))
            sig("gate_cols").wait(e, 1)
            link(e.copy(cols[:, :, :], ps[:, 0, 0:16].rearrange("p (t n) -> p t n", t=T)))
            e.activation(small[:, 16:24].rearrange("p (t n) -> p t n", t=T), cols[:, :, 4:8], ACT.Exp)
            for hd in range(A_HEADS):
                mB = ps[:, 1 + hd // 2, (hd % 2) * SEQ:(hd % 2 + 1) * SEQ]
                e.activation(wT[:, hd, 0:SEQ], mB, ACT.Exp, bias=cols[:, 0, hd:hd + 1], scale=-1.0)
                ins = e.activation(wT[:, hd, SEQ:384], mB[:, P:SEQ], ACT.Exp, bias=cols[:, 1, hd:hd + 1], scale=-1.0)
            sig("w_exp").by(ins)
            for t in range(T):
                for hd in range(A_HEADS):
                    sig("h_raw").wait(e, 4 * t + hd + 1)
                    ins = e.activation(big[:, hd, 0:P], hcat[:, t, hd * P:(hd + 1) * P], ACT.Square,
                                       accum_out=small[:, 24 + 4 * t + hd:25 + 4 * t + hd])
                    if hd < A_HEADS:
                        link(ins)
            sig("h_rms").by(e.activation(small[:, 24:32], small[:, 24:32], ACT.Sqrt, bias=eps_col[:, :], scale=1.0 / P))
            link.end()

        @block.gpsimd
        def _(e):
            sig("w_exp").wait(e, 1)
            e.affine_select(out=wT[:, :, 0:P], in_=wT[:, :, 0:P], pattern=[[0, A_HEADS], [1, P]],
                            compare_op=ALU.is_ge, fill=0.0, base=0, channel_multiplier=-1)
            sig("w_masked").by(e.affine_select(out=wT[:, :, SEQ:384], in_=wT[:, :, SEQ:384], pattern=[[0, A_HEADS], [1, P]],
                                               compare_op=ALU.is_ge, fill=0.0, base=0, channel_multiplier=-1))

        @block.tensor
        def _(e):
            for hd in range(A_HEADS):
                e.matmul(ps[:, 4 + hd, 0:SEQ], qk[:, 4 + hd, 0:P], qk[:, hd, :], start=True, stop=True)
                sig("qk_mm").by(e.matmul(ps[:, 4 + hd, SEQ:384], qk[:, 4 + hd, P:SEQ], qk[:, hd, P:SEQ], start=True, stop=True))
            sig("gate_rows").wait(e, 1)
            sig("mix_loaded").wait(e, 16 * 5)
            for t in range(T):
                e.transpose(ps[:, 0, 8 * t:8 * t + 4], g1[:, t * P:(t + 1) * P], ident[0:A_HEADS, 0:A_HEADS])
                e.transpose(ps[:, 0, 8 * t + 4:8 * t + 8], g4[:, t * P:(t + 1) * P], ident[0:A_HEADS, 0:A_HEADS])
            for hd in range(A_HEADS):
                ins = e.matmul(ps[:, 1 + hd // 2, (hd % 2) * SEQ:(hd % 2 + 1) * SEQ], sel_h[:, hd * P:(hd + 1) * P],
                               g2[:, :], start=True, stop=True)
            sig("gate_cols").by(ins)
            sig("scores").wait(e, A_HEADS)
            for t in range(T):
                for hd in range(A_HEADS):
                    o = (hd % 2) * 129
                    dst = ps[:, 2 * t + hd // 2, o:o + 129]
                    if t == 0:
                        ins = e.matmul(dst, wT[:, hd, 0:P], v_ones[:, 0, hd, :], start=True, stop=True)
                    else:
                        e.matmul(dst, wT[:, hd, P:SEQ], v_ones[:, 0, hd, :], start=True, stop=False)
                        ins = e.matmul(dst, wT[:, hd, SEQ:384], v_ones[:, 1, hd, :], start=False, stop=True)
            sig("num_mm").by(ins)

    def bank_of(hd):
        return 2 * (hd // 4) + hd % 2, (hd // 2 % 2) * SEQ

    GQK = stat[:, 8:9]
    rstd_q = small[:, 48:64]
    with nc.Block() as block:
        @block.scalar
        def _(e):
            link = linker(e, "act_step")
            for t in range(T):
                link(e.activation(big[:, 0, 0:B_LATENT], bc[:, t, :], ACT.Square, accum_out=small[:, t:t + 1]))
            sig("lat_rms").by(e.activation(small[:, 2:4], small[:, 0:2], ACT.Sqrt, bias=eps_col[:, :], scale=1.0 / B_LATENT))
            sig("q_sq").by(e.activation(big[:, 4:8, :], bqT[:, :, :], ACT.Square))
            sig("latT_mm").wait(e, 1)
            sig("latT").by(e.copy(latT[:, :], ps[:, 0, 0:SEQ]))
            sig("uv_mm").wait(e, 1)
            for t in range(T):
                link(e.activation(big[:, 0, 0:B_DH], ps[:, 1, t * B_DH:(t + 1) * B_DH], ACT.Square, accum_out=small[:, 8 + t:9 + t]))
                e.copy(vu[:, t, :], ps[:, 2 + t, :])
            sig("k_rms").by(e.activation(small[:, 10:12], small[:, 8:10], ACT.Sqrt, bias=eps_col[:, :], scale=1.0 / B_DH))
            sig("q_rms").by(e.activation(small[:, 32:48], ps[:, 4, 0:16], ACT.Sqrt, bias=eps_col[:, :], scale=1.0 / B_DH))
            sig("kbT_mm").wait(e, 1)
            sig("kbT").by(e.activation(kbT[:, :], ps[:, 5, 0:SEQ], ACT.Copy, scale=GQK))
            for t in range(T):
                S = P * (t + 1)
                for b in range(4):
                    sig("idx_mm").wait(e, 2 * t + b // 2 + 1)
                    hd = 4 * (b // 2) + b % 2
                    sig("idx_relu").by(e.activation(big[:, hd:hd + 3:2, 0:S],
                                                    ps[:, b, :].rearrange("p (j s) -> p j s", j=2)[:, :, 0:S], ACT.Relu))
                for hd in range(B_HEADS):
                    sig("nmax").wait(e, t + 1)
                    ins = e.activation(big[:, hd, 0:S], big[:, hd, 0:S], ACT.Exp, bias=small[:, 64 + hd:65 + hd],
                                       accum_out=small[:, 72 + hd:73 + hd])
                sig("probs").by(ins)
                for g in range(2 * (t + 1)):
                    sig("probT_mm").wait(e, 2 * t + g + 1)
                    sig("probT").by(e.copy(probT[:, 4 * g:4 * g + 4, :], ps[:, g, :].rearrange("p (j s) -> p j s", j=4)))
            link.end()

        @block.vector
        def _(e):
            link = linker(e, "dve_step")
            sig("lat_rms").wait(e, 1)
            link(e.reciprocal(small[:, 4:6], small[:, 2:4]))
            for t in range(T):
                ins = e.scalar_tensor_tensor(out=lat[:, t, :], in0=bc[:, t, :], scalar=small[:, 4 + t:5 + t],
                                             in1=gkv_b[:, :], op0=ALU.mult, op1=ALU.mult)
            sig("lat").by(ins)
            link(e.scalar_tensor_tensor(out=GQK, in0=gains[:, ROW_GQ:ROW_GQ + 1], scalar=B_DH ** -0.5,
                                        in1=gains[:, ROW_GK:ROW_GK + 1], op0=ALU.mult, op1=ALU.mult))
            sig("k_rms").wait(e, 1)
            link(e.reciprocal(small[:, 12:14], small[:, 10:12]))
            for t in range(T):
                for half in range(2):
                    ins = e.tensor_scalar(kb2[:, t, half * B_DH:(half + 1) * B_DH], ps[:, 1, t * B_DH:(t + 1) * B_DH],
                                          small[:, 12 + t:13 + t], None, ALU.mult)
            sig("kb").by(ins)
            sig("q_rms").wait(e, 1)
            link(e.reciprocal(rstd_q, small[:, 32:48]))
            for t in range(T):
                S = P * (t + 1)
                for hd in range(B_HEADS):
                    sig("idx_relu").wait(e, 4 * t + bank_of(hd)[0] + 1)
                    w = wi[:, t, hd:hd + 1]
                    if hd == 0:
                        ins = e.tensor_scalar(isc[:, 0:S], big[:, 0, 0:S], w, None, ALU.mult)
                    else:
                        ins = e.scalar_tensor_tensor(out=isc[:, 0:S], in0=big[:, hd, 0:S], scalar=w, in1=isc[:, 0:S],
                                                     op0=ALU.mult, op1=ALU.add)
                    link(ins)
                sig("isc").by(e.nop())
                sig("isc_masked").wait(e, t + 1)
                for _r in range(TOPK // 8):
                    link(e.max(top8[:, :], isc[:, 0:S]))
                    link(e.match_replace(isc[:, 0:S], top8[:, :], isc[:, 0:S], TAKEN))
                sig("taken").by(e.tensor_scalar(isc[:, 0:S], isc[:, 0:S], (ACAUSAL + TAKEN) / 2, NEG, ALU.is_gt, ALU.mult))
                for hd in range(B_HEADS):
                    b, c = bank_of(hd)
                    sig("logit_mm").wait(e, 2 * t + hd // 4 + 1)
                    link(e.scalar_tensor_tensor(out=big[:, hd, 0:S],
                                                in0=ps[:, 4 + b, c:c + S],
                                                scalar=rstd_q[:, 8 * t + hd:8 * t + hd + 1],
                                                in1=bias_toe[:, hd, SEQ - S:SEQ], op0=ALU.mult, op1=ALU.add))
                sig("sel_masked").wait(e, t + 1)
                link(e.tensor_tensor(big[:, :, 0:S], big[:, :, 0:S], isc[:, 0:S].unsqueeze(1).to_broadcast([P, B_HEADS, S]), ALU.add))
                sig("nmax").by(e.tensor_reduce(small[:, 64:72], big[:, :, 0:S], AX_X, ALU.max, negate=True))
                sig("probs").wait(e, t + 1)
                link(e.reciprocal(small[:, 80:88], small[:, 72:80]))
                sig("pv_mm").wait(e, t + 1)
                sig("attn_out").by(e.tensor_tensor(hcat[:, t, 512:1024].rearrange("p (h d) -> p h d", h=B_HEADS),
                                                   ps[:, 7, :].rearrange("p (h d) -> p h d", h=B_HEADS),
                                                   small[:, 80:88].unsqueeze(2).to_broadcast([P, B_HEADS, B_DH]), ALU.mult))
            link.end()

        @block.gpsimd
        def _(e):
            for t in range(T):
                S = P * (t + 1)
                sig("isc").wait(e, t + 1)
                sig("isc_masked").by(e.affine_select(out=isc[:, 0:S], in_=isc[:, 0:S], pattern=[[-1, S]],
                                                     compare_op=ALU.is_ge, fill=ACAUSAL, base=t * P, channel_multiplier=1))
                sig("taken").wait(e, t + 1)
                sig("sel_masked").by(e.affine_select(out=isc[:, 0:S], in_=isc[:, 0:S], pattern=[[-1, S]],
                                                     compare_op=ALU.is_ge, fill=NEG, base=t * P, channel_multiplier=1))

        @block.tensor
        def _(e):
            sig("lat").wait(e, 1)
            for t in range(T):
                ins = e.transpose(ps[:, 0, t * P:(t + 1) * P], lat[:, t, :], ident[:, :])
            sig("latT_mm").by(ins)
            sig("q_sq").wait(e, 1)
            for t in range(T):
                for j in range(4):
                    ins = e.matmul(ps[:, 4, 8 * t + 2 * j:8 * t + 2 * j + 2], big[:, 4 + j, t * P:(t + 1) * P], halves[:, :],
                                   start=True, stop=True)
            sig("latT").wait(e, 1)
            for t in range(T):
                e.matmul(ps[:, 1, t * B_DH:(t + 1) * B_DH], latT[:, t * P:(t + 1) * P], w_uk[:, :], start=True, stop=True)
                ins = e.matmul(ps[:, 2 + t, :], latT[:, t * P:(t + 1) * P], w_uv[:, :, :].rearrange("p h d -> p (h d)"),
                               start=True, stop=True)
            sig("uv_mm").by(ins)
            sig("kb").wait(e, 1)
            for t in range(T):
                ins = e.transpose(ps[:, 5, t * P:(t + 1) * P], kb2[:, t, :], ident[:, :])
            sig("kbT_mm").by(ins)
            sig("kbT").wait(e, 1)
            for t in range(T):
                S = P * (t + 1)
                if t == 1:
                    sig("attn_out").wait(e, 1)
                for hd in range(B_HEADS):
                    b, c = bank_of(hd)
                    part = slice((hd % 2) * B_DH, (hd % 2 + 1) * B_DH)
                    ins = e.matmul(ps[:, b, c:c + S], qi[part, hd // 2, t * P:(t + 1) * P], ki2[part, 0:S],
                                   start=True, stop=True)
                    if hd % 4 == 3:
                        sig("idx_mm").by(ins)
                for hd in range(B_HEADS):
                    b, c = bank_of(hd)
                    part = slice((hd % 2) * B_DH, (hd % 2 + 1) * B_DH)
                    ins = e.matmul(ps[:, 4 + b, c:c + S], bqT[part, hd // 2, t * P:(t + 1) * P], kbT[part, 0:S],
                                   start=True, stop=True)
                    if hd % 4 == 3:
                        sig("logit_mm").by(ins)
                sig("probs").wait(e, t + 1)
                blocks = [(hd, s) for hd in range(B_HEADS) for s in range(t + 1)]
                for n, (hd, s) in enumerate(blocks):
                    ins = e.transpose(ps[:, n // 4, (n % 4) * P:(n % 4 + 1) * P], big[:, hd, s * P:(s + 1) * P], ident[:, :])
                    if n % 4 == 3:
                        sig("probT_mm").by(ins)
                for n, (hd, s) in enumerate(blocks):
                    sig("probT").wait(e, 2 * t + n // 4 + 1)
                    ins = e.matmul(ps[:, 7, hd * B_DH:(hd + 1) * B_DH], probT[:, n, :], vu[:, s, hd * B_DH:(hd + 1) * B_DH],
                                   start=(s == 0), stop=(s == t))
                sig("pv_mm").by(ins)

    def add_product(xT, w, k_n):
        def pe(e):
            for t in range(T):
                for n in range(2):
                    for k in range(k_n):
                        ins = e.matmul(ps[:, 4 + 2 * t + n, :], xT[:, k, t * P:(t + 1) * P], w[:, k, n * 512:(n + 1) * 512],
                                       start=(k == 0), stop=(k == k_n - 1))
                    sig("product").by(ins)

        def dve(e):
            for t in range(T):
                for n in range(2):
                    c = slice(n * 512, (n + 1) * 512)
                    sig("product").wait(e, 2 * t + n + 1)
                    e.tensor_tensor(h[:, t, c], h[:, t, c], ps[:, 4 + 2 * t + n, :], ALU.add)
        return pe, dve

    with nc.Block() as block:
        pe_add, dve_add = add_product(hT, w_o, KD)

        @block.tensor
        def _(e):
            for b in range(4):
                for k in (2 * b, 2 * b + 1):
                    for t in range(T):
                        o = (k % 2) * SEQ + t * P
                        ins = e.transpose(ps[:, b, o:o + P], hcat[:, t, k * P:(k + 1) * P], ident[:, :])
                sig("hcat_T").by(ins)
            sig("hT").wait(e, 4)
            pe_add(e)

        @block.scalar
        def _(e):
            for b in range(4):
                sig("hcat_T").wait(e, b + 1)
                sig("hT").by(e.copy(hT[:, 2 * b:2 * b + 2, :], ps[:, b, :].rearrange("p (j s) -> p j s", j=2)))

        @block.vector
        def _(e):
            dve_add(e)
    finished(product=4)
    if stop == "mix0":
        return dump()

    Q = N_UNITS * QUARTERS
    CH = N_CH

    def swiglu(weights, tag, moe=None):
        tiles = T if moe is None else 1
        bU, bG, bZ = ([0, 1], [2, 3], [4, 6]) if moe is None else ([0], [1], [2])
        names = ["raw0", "raw1", "raw2", "split_hi", "split_lo", "unit_used", "silu", "hid", "hid_T", "hidT_hi",
                 "hidT_lo", "acc_out"]
        if moe is not None:
            names += ["pick", "gathered", "x_hi", "x_lo", "back", "back_T", "backT", "scatter", "scattered", "acc_cleared"]
        sem = {k: nc.alloc_semaphore(f"{tag}_{k}") for k in names}
        first = sem
        second = None if moe is None else {k: nc.alloc_semaphore(f"{tag}_more_{k}") for k in names}

        hidden_after = {min(AT[("G", c)] + 2, N_UNITS - 1): c for c in range(CH)}
        transposed_after = {min(AT[("G", c)] + 3, N_UNITS - 1): c for c in range(CH)}

        def split_lo_at(i, n, q=QUARTERS - 1):
            return i * Q + (RING + n) * QUARTERS + q + 1

        def unit_used_at(i, n):
            return i * N_UNITS + RING + n + 1

        def chunk_at(i, c, t=None):
            return i * (CH * tiles) + c * tiles + (tiles if t is None else t + 1)

        def slot(n):
            return n % RING

        def load_units(e, i):
            for n, (kind, c) in enumerate(UNITS):
                w = weights[kind] if moe is None else weights[kind][i]
                if kind == "D":
                    src = w[c * FC:(c + 1) * FC, :].rearrange("(j p) n -> p j n", p=P)
                    dst = raw[slot(n)][:, :].rearrange("p (j n) -> p j n", j=4)
                else:
                    src = w[:, c * FC:(c + 1) * FC].rearrange("(k p) n -> p k n", p=P)
                    dst = raw[slot(n)][:, :].rearrange("p (k n) -> p k n", k=KD)
                e.wait_ge(sem["split_lo"], split_lo_at(i, n - RING))
                e.dma_start(dst, src).then_inc(sem[f"raw{slot(n)}"], 16)

        def split_hi(e, i, n):
            e.wait_ge(sem[f"raw{slot(n)}"], i * (16 * N_UNITS // RING) + 16 * (n // RING + 1))
            e.wait_ge(sem["unit_used"], unit_used_at(i, n - RING))
            for q in range(QUARTERS):
                c = slice(q * 1024, (q + 1) * 1024)
                e.copy(w_hi[slot(n)][:, c], raw[slot(n)][:, c]).then_inc(sem["split_hi"], 1)

        def split_lo(e, i, n):
            for q in range(QUARTERS):
                c = slice(q * 1024, (q + 1) * 1024)
                e.wait_ge(sem["split_hi"], i * Q + n * QUARTERS + q + 1)
                e.tensor_tensor(w_lo[slot(n)][:, c], raw[slot(n)][:, c], w_hi[slot(n)][:, c].bitcast(F32),
                                ALU.subtract).then_inc(sem["split_lo"], 1)

        def three_passes(e, dst, xh, xl, wh, wl, first, last):
            e.matmul(dst, xh, wh, start=first, stop=False)
            e.matmul(dst, xh, wl, start=False, stop=False)
            return e.matmul(dst, xl, wh, start=False, stop=last)

        def unit_product(e, i, n):
            kind, c = UNITS[n]
            if kind == "U" and c > 0:
                e.wait_ge(sem["hid"], chunk_at(i, c - 1))
            if kind == "G" and c > 0:
                e.wait_ge(sem["hidT_lo"], chunk_at(i, c - 1))
            if kind == "D":
                e.wait_ge(sem["hidT_lo"], chunk_at(i, c))
                if c == 0 and moe is not None:
                    e.wait_ge(sem["acc_out"], i + 1)
            wh, wl = w_hi[slot(n)], w_lo[slot(n)]
            for t in range(tiles):
                for q in range(QUARTERS):
                    if t == 0:
                        e.wait_ge(sem["split_lo"], split_lo_at(i, n, q))
                    for m in range(2):
                        cols_ = slice((2 * q + m) * 512, (2 * q + m + 1) * 512)
                        if kind == "D":
                            ins = three_passes(e, ps[:, bZ[t] + m, :], hidT_hi[t][:, q, :], hidT_lo[t][:, q, :],
                                               wh[:, cols_], wl[:, cols_], c == 0 and q == 0, c == CH - 1 and q == QUARTERS - 1)
                        else:
                            k = 2 * q + m
                            ins = three_passes(e, ps[:, (bU if kind == "U" else bG)[t], :],
                                               x_hi[:, k, t * P:(t + 1) * P], x_lo[:, k, t * P:(t + 1) * P],
                                               wh[:, cols_], wl[:, cols_], k == 0, k == KD - 1)
            ins.then_inc(sem["unit_used"], 1)

        def transpose_hidden(e, i, c):
            for t in range(tiles):
                e.wait_ge(sem["hid"], chunk_at(i, c, t))
                for j in range(4):
                    ins = e.transpose(ps[:, bG[t], j * P:(j + 1) * P], hid[t][:, j * P:(j + 1) * P], ident[:, :])
                ins.then_inc(sem["hid_T"], 1)

        def silu(e, i, c):
            e.wait_ge(sem["unit_used"], unit_used_at(i, AT[("G", c)]))
            for t in range(tiles):
                e.activation(hid[t][:, :], ps[:, bG[t], :], ACT.Silu).then_inc(sem["silu"], 1)

        def hidden(e, i, c):
            for t in range(tiles):
                e.wait_ge(sem["silu"], chunk_at(i, c, t))
                e.tensor_tensor(hid[t][:, :], hid[t][:, :], ps[:, bU[t], :], ALU.mult).then_inc(sem["hid"], 1)

        def hiddenT_hi(e, i, c):
            for t in range(tiles):
                e.wait_ge(sem["hid_T"], chunk_at(i, c, t))
                e.copy(hidT_hi[t][:, :, :], ps[:, bG[t], :].rearrange("p (j s) -> p j s", j=4)).then_inc(sem["hidT_hi"], 1)

        def hiddenT_lo(e, i, c):
            for t in range(tiles):
                e.wait_ge(sem["hidT_hi"], chunk_at(i, c, t))
                e.tensor_tensor(hidT_lo[t][:, :, :], ps[:, bG[t], :].rearrange("p (j s) -> p j s", j=4),
                                hidT_hi[t][:, :, :].bitcast(F32), ALU.subtract).then_inc(sem["hidT_lo"], 1)

        def pick_for(e, col):
            for t in range(T):
                e.tensor_scalar(pick[:, t, :], iota[:, :], rank[:, t, col], None, ALU.is_equal).then_inc(sem["pick"], 1)

        def back_for(e, col):
            for t in range(T):
                e.tensor_scalar(back[:, t, :], iota[:, :], rank[:, t, col], gate[:, t, col], ALU.is_equal,
                                ALU.mult).then_inc(sem["back"], 1)

        def transpose_back(e, i):
            e.wait_ge(sem["back"], (i + 1) * T)
            for t in range(T):
                ins = e.transpose(ps[:, 6, t * P:(t + 1) * P], back[:, t, :], ident[:, :])
            ins.then_inc(sem["back_T"], 1)

        def leave(e, i):
            e.wait_ge(sem["unit_used"], unit_used_at(i, -1))
            e.copy(slot_out[:, :].rearrange("p (n c) -> p n c", n=2), ps[:, 2:4, :]).then_inc(sem["acc_out"], 1)
            e.wait_ge(sem["back_T"], i + 1)
            e.copy(backT[:, :], ps[:, 6, 0:SEQ]).then_inc(sem["backT"], 1)

        def scatter(e, i):
            e.wait_ge(sem["acc_out"], i + 1)
            e.wait_ge(sem["backT"], i + 1)
            for t in range(T):
                for n in range(2):
                    ins = e.matmul(ps[:, 4 + 2 * t + n, :], backT[:, t * P:(t + 1) * P], slot_out[:, n * 512:(n + 1) * 512],
                                   start=True, stop=True)
            ins.then_inc(sem["scatter"], 1)

        def add_scattered(e, i):
            e.wait_ge(sem["scatter"], i + 1)
            for t in range(T):
                e.tensor_tensor(h[:, t, :].rearrange("p (n c) -> p n c", n=2), h[:, t, :].rearrange("p (n c) -> p n c", n=2),
                                ps[:, 4 + 2 * t:6 + 2 * t, :], ALU.add).then_inc(sem["scattered"], 1)

        def gather(e, i):
            e.wait_ge(sem["pick"], (i + 1) * T)
            for k in range(KD):
                for t in range(T):
                    ins = e.matmul(ps[:, 4 + k // 4, (k % 4) * P:(k % 4 + 1) * P], y[:, t, k * P:(k + 1) * P], pick[:, t, :],
                                   start=(t == 0), stop=(t == T - 1))
            ins.then_inc(sem["gathered"], 1)

        def gathered_hi(e, i):
            e.wait_ge(sem["gathered"], i + 1)
            for b in range(2):
                e.copy(x_hi[:, 4 * b:4 * b + 4, 0:P], ps[:, 4 + b, :].rearrange("p (k s) -> p k s", k=4)).then_inc(sem["x_hi"], 1)

        def gathered_lo(e, i):
            for b in range(2):
                e.wait_ge(sem["x_hi"], 2 * i + b + 1)
                e.tensor_tensor(x_lo[:, 4 * b:4 * b + 4, 0:P], ps[:, 4 + b, :].rearrange("p (k s) -> p k s", k=4),
                                x_hi[:, 4 * b:4 * b + 4, 0:P].bitcast(F32), ALU.subtract).then_inc(sem["x_lo"], 1)

        def run(e, turn):
            if moe is None:
                turn(0)
            else:
                with e.Fori(0, N_EXP) as i:
                    turn(i)

        if moe is not None:
            pick, back, backT, rank, gate, iota, over = moe

        def sync_pass(e):
            run(e, lambda i: load_units(e, i))

        def scalar_pass(e):
            def turn(i):
                for n in range(N_UNITS):
                    split_hi(e, i, n)
                    if n == 0 and moe is not None:
                        leave(e, i)
                    if n in hidden_after:
                        silu(e, i, hidden_after[n])
                    if n in transposed_after:
                        hiddenT_hi(e, i, transposed_after[n])
                if moe is not None:
                    gathered_hi(e, i + 1)
            if moe is not None:
                e.wait_ge(sem["acc_cleared"], 1)
                gathered_hi(e, 0)
            run(e, turn)
            if moe is not None:
                leave(e, N_EXP)

        def vector_pass(e):
            def turn(i):
                if moe is not None:
                    back_for(e, bass.ds(i, 1))
                for n in range(N_UNITS):
                    split_lo(e, i, n)
                    if n in hidden_after:
                        hidden(e, i, hidden_after[n])
                        if n == AT[("G", 0)] + 2 and moe is not None:
                            add_scattered(e, i)
                            pick_for(e, bass.ds(i + 2, 1))
                    if n in transposed_after:
                        hiddenT_lo(e, i, transposed_after[n])
                if moe is not None:
                    gathered_lo(e, i + 1)
            e.nop().then_inc(sem["split_lo"], RING * QUARTERS)
            if moe is not None:
                pick_for(e, slice(1, 2))
                e.memset(ps[:, 2:4, :], 0.0).then_inc(sem["acc_cleared"], 1)
                gathered_lo(e, 0)
            run(e, turn)
            if moe is None:
                e.wait_ge(sem["unit_used"], unit_used_at(0, N_UNITS - 1))
                for t in range(T):
                    e.tensor_tensor(h[:, t, :].rearrange("p (n c) -> p n c", n=2), h[:, t, :].rearrange("p (n c) -> p n c", n=2),
                                    ps[:, bZ[t]:bZ[t] + 2, :], ALU.add)
            else:
                back_for(e, slice(N_EXP, N_EXP + 1))
                add_scattered(e, N_EXP)

        def tensor_pass(e):
            def turn(i):
                if moe is not None:
                    transpose_back(e, i)
                    e.wait_ge(sem["x_lo"], 2 * i + 2)
                for n, (kind, c) in enumerate(UNITS):
                    if n == N_UNITS - 1 and moe is not None:
                        e.wait_ge(sem["scattered"], (i + 1) * T)
                        gather(e, i + 1)
                    unit_product(e, i, n)
                    if (kind, c) == ("G", 0) and moe is not None:
                        scatter(e, i)
                    if (kind, c) == ("U", 1):
                        transpose_hidden(e, i, 0)
                    if kind == "D" and c < CH - 1:
                        transpose_hidden(e, i, c + 1)
            e.nop().then_inc(sem["unit_used"], RING)
            if moe is not None:
                gather(e, 0)
            run(e, turn)
            if moe is not None:
                transpose_back(e, N_EXP)
                scatter(e, N_EXP)

        def passes(e, one_pass, between=None):
            nonlocal sem
            sem = first
            one_pass(e)
            if moe is None:
                return
            crowded = e.value_load(over[0:1, 0:1], min_val=0, max_val=1)
            with e.If(crowded > 0):
                e.wait_ge(first["scattered"], (N_EXP + 1) * T)
                if between is not None:
                    between()
                sem = second
                one_pass(e)
            sem = first

        with nc.Block() as block:
            @block.sync
            def _(e):
                passes(e, sync_pass)

            @block.scalar
            def _(e):
                passes(e, scalar_pass)

            @block.vector
            def _(e):
                def next_slots():
                    e.tensor_scalar(rank[:, :, :], rank[:, :, :], -float(P), None, ALU.add).then_inc(first["acc_cleared"], 1)
                    e.wait_ge(first["acc_cleared"], 2)
                passes(e, vector_pass, next_slots)

            @block.tensor
            def _(e):
                passes(e, tensor_pass)

    norm_T(ROW_FFN, True)
    swiglu({"U": a["w_up_d"][0], "G": a["w_gate_d"][0], "D": a["w_down_d"][0]}, "dense")
    if stop == "ffn0":
        return dump()

    def embed(layer):
        t5 = inside(arena, arena_n)
        tag = f"ple{layer}"
        w_g = t5(f"w_g_{tag}", (P, KD, D))
        w_p = t5(f"w_p_{tag}", (P, 2, D))
        p_in = t5(f"p_in_{tag}", (P, T, PLE))
        pT = t5(f"pT_{tag}", (P, 2, SEQ))
        sg = t5(f"sg_{tag}", (P, 4, 512))
        xT = inside(ffn_small, 16384)(f"xT_{tag}", (P, KD, SEQ))

        def load(e):
            s = sig("embed_loaded")
            s.by(e.dma_start(p_in[:, :, :], a["p"][layer, 0].rearrange("(t p) n -> p t n", p=P)), 16)
            s.by(e.dma_start(w_p[:, :, :], a["w_ple"][layer].rearrange("(k p) n -> p k n", p=P)), 16)
            s.by(e.dma_start(w_g[:, :, :], a["w_ple_gate"][layer].rearrange("(k p) n -> p k n", p=P)), 16)

        norm_T(ROW_PLE + KD * layer, False, yT=xT, load=load)
        with nc.Block() as block:
            @block.tensor
            def _(e):
                sig("embed_loaded").wait(e, 48)
                for k in range(2):
                    for t in range(T):
                        ins = e.transpose(ps[:, 0, k * SEQ + t * P:k * SEQ + (t + 1) * P], p_in[:, t, k * P:(k + 1) * P], ident[:, :])
                sig("p_T").by(ins)
                for t in range(T):
                    for n in range(2):
                        for k in range(KD):
                            ins = e.matmul(ps[:, 4 + 2 * t + n, :], xT[:, k, t * P:(t + 1) * P], w_g[:, k, n * 512:(n + 1) * 512],
                                           start=(k == 0), stop=(k == KD - 1))
                        sig("gate_mm").by(ins)
                sig("pT").wait(e, 1)
                for t in range(T):
                    for n in range(2):
                        for k in range(2):
                            ins = e.matmul(ps[:, 2 * t + n, :], pT[:, k, t * P:(t + 1) * P], w_p[:, k, n * 512:(n + 1) * 512],
                                           start=(k == 0), stop=(k == 1))
                        sig("emb_mm").by(ins)

            @block.scalar
            def _(e):
                sig("p_T").wait(e, 1)
                sig("pT").by(e.copy(pT[:, :, :], ps[:, 0, :].rearrange("p (k s) -> p k s", k=2)))
                for b in range(4):
                    sig("gate_mm").wait(e, b + 1)
                    sig("gate_sig").by(e.activation(sg[:, b, :], ps[:, 4 + b, :], ACT.Sigmoid))

            @block.vector
            def _(e):
                for b in range(4):
                    sig("emb_mm").wait(e, b + 1)
                    sig("gate_sig").wait(e, b + 1)
                    sig("gated").by(e.tensor_tensor(sg[:, b, :], sg[:, b, :], ps[:, b, :], ALU.mult))
                for b in range(4):
                    sig("gated").wait(e, b + 1)
                    c = slice((b % 2) * 512, (b % 2 + 1) * 512)
                    e.tensor_tensor(h[:, b // 2, c], h[:, b // 2, c], sg[:, b, :], ALU.add)
        finished(embed_loaded=48, p_T=1, gate_mm=4, pT=1, emb_mm=4, gate_sig=4, gated=4)

    embed(0)
    if stop == "ple0":
        return dump()

    PAD = max(WINDOWS)
    t6 = inside(arena, arena_n)
    w_pool = t6("w_pool", (P, 4, 2, 256))
    scale_b = t6("scale_b", (P, D))
    inv_pos = t6("inv_pos", (P, 4, SEQ))
    win = [t6(f"win{n}", (P, KD, PAD + SEQ)) for n in range(3)]
    pooled = t6("pooled", (P, KD, SEQ))

    def load_pool(e):
        s = sig("pool_loaded")
        for g in range(4):
            s.by(e.dma_start(w_pool[:, g, :, :], a["w_pool"][0, g].rearrange("(k p) n -> p k n", p=P)), 16)
        s.by(e.dma_start(scale_b[:, :], a["scale_pool"].partition_broadcast(P)[:, 0, :]), 16)
        s.by(e.dma_start(inv_pos[:, :, :], a["c_invpos"].partition_broadcast(P)), 16)

    norm_T(ROW_MIX + KD, False, yT=yT, load=load_pool)
    with nc.Block() as block:
        @block.vector
        def _(e):
            link = linker(e, "dve_step")
            for w in win:
                link(e.memset(w[:, :, 0:PAD], 0.0))
            link(e.tensor_copy(win[0][:, :, PAD:], yT[:, :, :]))
            sig("pool_loaded").wait(e, 16 * 6)
            src = 0
            for g in range(4):
                step, dst = 1 << g, 1 + g % 2
                link(e.tensor_tensor(win[dst][:, 2 * g:, PAD:], win[src][:, 2 * g:, PAD:],
                                     win[src][:, 2 * g:, PAD - step:PAD + SEQ - step], ALU.add))
                link(e.tensor_tensor(pooled[:, 2 * g:2 * g + 2, :], win[dst][:, 2 * g:2 * g + 2, PAD:],
                                     inv_pos[:, g, :].unsqueeze(1).to_broadcast([P, 2, SEQ]), ALU.mult))
                sig("pooled").by(e.tensor_tensor(pooled[:, 2 * g:2 * g + 2, :], pooled[:, 2 * g:2 * g + 2, :],
                                                 yT[:, 2 * g:2 * g + 2, :], ALU.subtract))
                src = dst
            for b in range(4):
                c = slice((b % 2) * 512, (b % 2 + 1) * 512)
                sig("pool_mm").wait(e, b + 1)
                link(e.tensor_tensor(y[:, b // 2, c], ps[:, 4 + b, :], scale_b[:, c], ALU.mult))
                e.tensor_tensor(h[:, b // 2, c], h[:, b // 2, c], y[:, b // 2, c], ALU.add)
            link.end()

        @block.tensor
        def _(e):
            for t in range(T):
                for g in range(4):
                    sig("pooled").wait(e, g + 1)
                    for k in range(2):
                        ins = e.matmul(ps[:, 4 + 2 * t + g // 2, (g % 2) * 256:(g % 2 + 1) * 256],
                                       pooled[:, 2 * g + k, t * P:(t + 1) * P], w_pool[:, g, k, :],
                                       start=(k == 0), stop=(k == 1))
                    if g % 2:
                        sig("pool_mm").by(ins)
    if stop == "mix1":
        return dump()

    t7 = inside(z_free_at, 4096)
    pick = t7("pick", (P, T, P))
    back = t7("back", (P, T, P))
    backT = t7("backT", (P, SEQ))
    rank = t7("rank", (P, T, N_EXP + 2))
    gate = t7("gate", (P, T, N_EXP + 2))
    iota = t7("iota", (P, P))
    t8 = inside(arena, arena_n)
    w_r = t8("w_r", (P, KD, N_EXP))
    b_r = t8("b_r", (P, N_EXP))
    g_b = t8("g_b", (P, D))
    logit = t8("logit", (P, T, N_EXP))
    top_v = t8("top_v", (P, T, 8))
    top_i = t8("top_i", (P, T, 8), U32)
    top_f = t8("top_f", (P, T, 8))
    sc = t8("sc", (P, T, 8))
    oh = t8("oh", (P, T, 2, N_EXP))
    chosen = t8("chosen", (P, T, N_EXP))
    most = t8("most", (P, 1))
    over = place("over", (P, 1), I32, offset=over_at)

    def load_router(e):
        s = sig("router_loaded")
        s.by(e.dma_start(w_r[:, :, :], a["w_router"][0].rearrange("(k p) n -> p k n", p=P)), 16)
        s.by(e.dma_start(b_r[:, :], a["b_router"].partition_broadcast(P)[:, 0, :]), 16)
        s.by(e.dma_start(g_b[:, :], a["norm_ffn"][1:2].partition_broadcast(P)[:, 0, :]), 16)
        s.by(e.dma_start(iota[:, :], a["c_iota"].partition_broadcast(P)[:, 0, :]), 16)

    norm_T(ROW_FFN + KD, False, yT=yT, load=load_router)
    with nc.Block() as block:
        @block.tensor
        def _(e):
            sig("router_loaded").wait(e, 64)
            for t in range(T):
                for k in range(KD):
                    ins = e.matmul(ps[:, t, 0:N_EXP], yT[:, k, t * P:(t + 1) * P], w_r[:, k, :],
                                   start=(k == 0), stop=(k == KD - 1))
                sig("logit").by(ins)
            sig("chosen").wait(e, T)
            e.matmul(ps[:, 2, 0:N_EXP], before[:, :], chosen[:, 0, :], start=True, stop=True)
            e.matmul(ps[:, 3, 0:N_EXP], ones[:, :], chosen[:, 0, :], start=True, stop=False)
            e.matmul(ps[:, 3, 0:N_EXP], before[:, :], chosen[:, 1, :], start=False, stop=True)
            e.matmul(ps[:, 4, 0:N_EXP], ones[:, :], chosen[:, 0, :], start=True, stop=False)
            sig("ranks").by(e.matmul(ps[:, 4, 0:N_EXP], ones[:, :], chosen[:, 1, :], start=False, stop=True))

        @block.scalar
        def _(e):
            sig("gap").wait(e, 1)
            sig("gap_exp").by(e.activation(sc[:, :, 1], sc[:, :, 0], ACT.Exp))

        @block.vector
        def _(e):
            link = linker(e, "dve_step")
            sig("router_loaded").wait(e, 64)
            link(e.memset(rank[:, :, :], -1.0))
            link(e.memset(gate[:, :, :], 0.0))
            for t in range(T):
                sig("logit").wait(e, t + 1)
                link(e.tensor_tensor(logit[:, t, :], ps[:, t, 0:N_EXP], b_r[:, :], ALU.add))
                link(e.max(top_v[:, t, :], logit[:, t, :]))
                link(e.max_index(top_i[:, t, :], top_v[:, t, :], logit[:, t, :]))
            link(e.tensor_copy(top_f[:, :, :], top_i[:, :, :]))
            sig("gap").by(e.tensor_tensor(sc[:, :, 0], top_v[:, :, 1], top_v[:, :, 0], ALU.subtract))
            for t in range(T):
                for j in range(2):
                    link(e.tensor_scalar(oh[:, t, j, :], iota[:, 0:N_EXP], top_f[:, t, j:j + 1], None, ALU.is_equal))
                sig("chosen").by(e.tensor_tensor(chosen[:, t, :], oh[:, t, 0, :], oh[:, t, 1, :], ALU.add))
            sig("gap_exp").wait(e, 1)
            link(e.tensor_scalar(sc[:, :, 2], sc[:, :, 1], 1.0, None, ALU.add))
            link(e.reciprocal(sc[:, :, 3], sc[:, :, 2]))
            link(e.tensor_tensor(sc[:, :, 4], sc[:, :, 3], sc[:, :, 1], ALU.mult))
            sig("ranks").wait(e, 1)
            for t in range(T):
                e1 = slice(1, N_EXP + 1)
                link(e.tensor_scalar(gate[:, t, e1], oh[:, t, 0, :], sc[:, t, 3:4], None, ALU.mult))
                link(e.scalar_tensor_tensor(out=gate[:, t, e1], in0=oh[:, t, 1, :], scalar=sc[:, t, 4:5], in1=gate[:, t, e1],
                                            op0=ALU.mult, op1=ALU.add))
                link(e.scalar_tensor_tensor(out=rank[:, t, e1], in0=ps[:, 2 + t, 0:N_EXP], scalar=1.0, in1=chosen[:, t, :],
                                            op0=ALU.add, op1=ALU.mult))
                link(e.tensor_scalar(rank[:, t, e1], rank[:, t, e1], -1.0, None, ALU.add))
            link(e.tensor_reduce(most[:, :], ps[:, 4, 0:N_EXP], AX_X, ALU.max))
            link(e.tensor_scalar(over[:, :], most[:, :], float(P), None, ALU.is_gt))
            for t in range(T):
                e.tensor_tensor(y[:, t, :], y[:, t, :], g_b[:, :], ALU.mult)
            link.end()

    w_moe = {"U": a["w_up_m"][0], "G": a["w_gate_m"][0], "D": a["w_down_m"][0]}
    moe_small = (pick, back, backT, rank, gate, iota, over)
    swiglu(w_moe, "moe", moe_small)
    if stop == "ffn1":
        return dump()
    embed(1)
    dump()


N_PARAM_DMAS = 2 + 2 + 3 + 1 + 4 + 2 + 2 + 2

_INS = ['x', 'p', 'norm_mix', 'norm_ffn', 'w_in_e', 'b_gate_e', 'conv_a', 'norm_h_a', 'norm_q_b', 'norm_k_b',
        'norm_kv_b', 'w_uk_b', 'w_uv_b', 'w_out_e', 'rel_bias', 'w_pool', 'scale_pool', 'w_gate_d', 'w_up_d',
        'w_down_d', 'w_router', 'b_router', 'w_gate_m', 'w_up_m', 'w_down_m', 'w_ple', 'w_ple_gate', 'norm_ple']


def kernel(**inputs):
    import numpy as _np
    import concourse.bacc as _bacc
    from concourse import mybir as _mybir
    from concourse.bass_utils import run_bass_kernel_spmd as _run

    nc = _bacc.Bacc("TRN2", target_bir_lowering=False, num_devices=1)
    arrays, args = {}, {}
    given = {name: _np.ascontiguousarray(inputs[name]) for name in _INS}
    given.update(constants())
    for name, v in given.items():
        arrays[f"in_{name}"] = v
        args[name] = nc.dram_tensor(f"in_{name}", v.shape, _mybir.dt.from_np(v.dtype), kind="ExternalInput").ap()
    out = nc.dram_tensor("out_0", (1, SEQ, D), _mybir.dt.float32, kind="ExternalOutput").ap()
    build(nc, args, out)
    r = _run(nc, [arrays], core_ids=[0])
    return r.results[0]["out_0"]
```

```python
import math

import numpy as np
import concourse.bass as bass
from concourse import mybir

F32 = mybir.dt.float32
F32R = mybir.dt.float32r
I32 = mybir.dt.int32
U32 = mybir.dt.uint32
ALU = mybir.AluOpType
ACT = mybir.ActivationFunctionType
AX_X = mybir.AxisListType.X

P = 128
D = 1024
KD = D // P
SEQ = 256
T = SEQ // P
EPS = 1e-6
A_HEADS, A_DK = 4, 128
B_HEADS, B_DH, B_LATENT = 8, 64, 128
TOPK = 64
BUCKETS, MAX_DIST = 32, 128
OFF_AQ, OFF_AV, OFF_AO, OFF_AI, OFF_AF = 0, 1024, 1536, 2048, 2052
OFF_BQ, OFF_BC, OFF_QI, OFF_KI, OFF_WI, D_IN = 2056, 2568, 2696, 3208, 3272, 3280
CONV = 4
WINDOWS = (2, 4, 8, 16)
F_FF = 3584
N_EXP = 8
N_LAYERS = 2
PLE = 256
FC = 512
N_CH = F_FF // FC
NEG = -1e30
ACAUSAL, TAKEN = -3.0e38, -3.3e38
BIAS_W = 384

UNITS = [("U", 0), ("G", 0)]
for _c in range(1, N_CH):
    UNITS += [("U", _c), ("G", _c), ("D", _c - 1)]
UNITS.append(("D", N_CH - 1))
N_UNITS = len(UNITS)
AT = {u: n for n, u in enumerate(UNITS)}
RING = 3
QUARTERS = 4
assert N_UNITS % RING == 0


class Signal:

    def __init__(self, nc, name):
        self.sem, self.base, self.name = nc.alloc_semaphore(name), 0, name

    def at(self, n):
        return n + self.base

    def past(self, n):
        self.base += n


def constants():
    d = np.arange(SEQ)
    exact = BUCKETS // 2
    log = np.log(np.maximum(d, 1).astype(np.float32) / np.float32(exact)) / np.float32(math.log(MAX_DIST / exact))
    large = np.minimum(exact + (log * (BUCKETS - exact)).astype(np.int32), BUCKETS - 1)
    bucket = np.where(d < exact, d, large)
    bias_onehot = np.zeros((BUCKETS, BIAS_W), np.float32)
    for j in range(SEQ):
        bias_onehot[bucket[SEQ - 1 - j], j] = 1.0
    select = np.zeros((A_HEADS, A_HEADS * P), np.float32)
    for hd in range(A_HEADS):
        select[hd, hd * P:(hd + 1) * P] = 1.0
    halves = np.zeros((P, 2), np.float32)
    halves[:B_DH, 0] = 1.0
    halves[B_DH:, 1] = 1.0
    pos = np.arange(1, SEQ + 1, dtype=np.float32)
    inv = np.stack([np.float32(1.0) / np.minimum(pos, np.float32(w)) for w in WINDOWS])
    return {
        "c_ident": np.eye(P, dtype=np.float32),
        "c_before": np.triu(np.ones((P, P), np.float32), 1),
        "c_bias": bias_onehot,
        "c_select": select,
        "c_halves": halves,
        "c_invpos": inv.astype(np.float32),
        "c_iota": np.arange(P, dtype=np.float32)[None, :],
    }


def build(nc, a, out, stop=None):
    limit = nc.sbuf_usable_end
    bottom = -(-nc.sbuf_base // 64) * 64
    at = [bottom]

    def place(name, shape, dtype=F32, offset=None):
        n = int(np.prod(shape[1:])) * 4
        if offset is None:
            offset, at[0] = at[0], at[0] + -(-n // 64) * 64
        assert offset % 4 == 0 and offset + n <= limit, (name, offset, n, limit)
        return nc.alloc_sbuf_tensor_at(name, tuple(shape), dtype, offset=offset)

    def region(size):
        o = at[0]
        at[0] += size
        assert at[0] <= limit, (at[0], limit)
        return o

    def inside(base, size):
        o = [base]

        def put(name, shape, dtype=F32):
            n = -(-int(np.prod(shape[1:])) * 4 // 64) * 64
            t = place(name, shape, dtype, offset=o[0])
            o[0] += n
            assert o[0] <= base + size, (name, o[0] - base, size)
            return t
        put.next = lambda: o[0]
        return put

    h = place("h", (P, T, D))
    ident = place("ident", (P, P))
    before = place("before", (P, P))
    ones = place("ones", (P, P))
    gains = place("gains", (P, P))
    stat = place("stat", (P, 64))
    bias_i = place("bias_i", (A_HEADS, 1))
    bias_f = place("bias_f", (A_HEADS, 1))
    eps_col = place("eps_col", (P, 1))
    one_col = place("one_col", (P, 1))
    over_at = region(64)
    y = place("y", (P, T, D))

    ffn_small = region(16384 + 3 * 2048 + 3 * 2048 + 2 * 4096)
    put = inside(ffn_small, 16384 + 6 * 2048 + 2 * 4096)
    x_hi = put("x_hi", (P, KD, SEQ), F32R)
    x_lo = put("x_lo", (P, KD, SEQ), F32R)
    hid = [put(f"hid{t}", (P, FC)) for t in range(T)]
    hidT_hi = [put(f"hidT_hi{t}", (P, 4, P), F32R) for t in range(T)]
    hidT_lo = [put(f"hidT_lo{t}", (P, 4, P), F32R) for t in range(T)]
    slot_out = put("slot_out", (P, D))
    z_free_at = ffn_small + 16384 + 6 * 2048 + 4096
    UNIT_B = 16384
    ring_raw = region(RING * UNIT_B)
    ring_split = region(2 * RING * UNIT_B)
    raw = [place(f"raw{s}", (P, 4096), offset=ring_raw + s * UNIT_B) for s in range(RING)]
    w_hi = [place(f"w_hi{s}", (P, 4096), F32R, offset=ring_split + 2 * s * UNIT_B) for s in range(RING)]
    w_lo = [place(f"w_lo{s}", (P, 4096), F32R, offset=ring_split + (2 * s + 1) * UNIT_B) for s in range(RING)]
    arena, arena_n = ring_raw, 3 * RING * UNIT_B

    ps = nc.alloc_psum_tensor("ps", (P, 8, 512), F32)

    names = {}

    def sig(name):
        if name not in names:
            names[name] = Signal(nc, name)
        return names[name]

    def finished(**counts):
        for name, n in counts.items():
            sig(name).past(n)

    def linker(eng, name):
        s = sig(name)
        count = [0]

        def link(ins):
            count[0] += 1
            ins.then_inc(s.sem, 1)
            eng.wait_ge(s.sem, s.base + count[0])

        link.end = lambda: s.past(count[0])
        return link

    ROW_MIX, ROW_FFN, ROW_PLE, ROW_CONV, ROW_GQ, ROW_GK = 0, 16, 32, 48, 80, 81
    N_ROWS = 82

    LIN = 2048
    MIX_RAW, MIX_SPLIT = 3, 3
    mix_at = arena + (MIX_RAW + 2 * MIX_SPLIT) * LIN * 4
    t1 = inside(mix_at, arena + arena_n - mix_at)
    qk = t1("qk", (P, 8, SEQ))
    v_ones = t1("v_ones", (P, T, A_HEADS, 129))
    ao = t1("ao", (P, T, 512))
    qi = t1("qi", (P, 4, SEQ))
    bqT = t1("bqT", (P, 4, SEQ))
    NARROW = B_LATENT + B_DH + 8 + 2 * A_HEADS
    narrow = t1("narrow", (P, T, NARROW))
    bc, ki, wi = narrow[:, :, 0:B_LATENT], narrow[:, :, B_LATENT:B_LATENT + B_DH], narrow[:, :, B_LATENT + B_DH:NARROW - 2 * A_HEADS]
    ki_twice = t1("ki_twice", (P, T, 2, B_DH))
    ki2 = t1("ki2", (P, SEQ))
    gate_i = t1("gate_i", (A_HEADS, SEQ))
    gate_f = t1("gate_f", (A_HEADS, SEQ))
    w_uk = t1("w_uk", (P, B_DH))
    w_uv = t1("w_uv", (P, B_HEADS, B_DH))
    sel_h = t1("sel_h", (A_HEADS, A_HEADS * P))
    halves = t1("halves", (P, 2))
    g1 = t1("g1", (A_HEADS, SEQ))
    g2 = t1("g2", (A_HEADS, SEQ))
    g3 = t1("g3", (A_HEADS, SEQ))
    g4 = t1("g4", (A_HEADS, SEQ))
    cols = t1("cols", (P, T, 8))
    WT_AT = t1.next()
    wT = t1("wT", (P, A_HEADS, 384))
    small = t1("small", (P, 96))
    msmall = t1("msmall", (P, 48))
    kb2 = t1("kb2", (P, T, P))
    kbT = t1("kbT", (P, SEQ))
    lat = t1("lat", (P, T, B_LATENT))
    latT = t1("latT", (P, SEQ))
    vu = t1("vu", (P, T, 512))
    isc = t1("isc", (P, SEQ))
    top8 = t1("top8", (P, 8))
    most_mask = t1("most_mask", (P, P))
    neg_mask = t1("neg_mask", (P, P))
    rel8 = t1("rel8", (BUCKETS, B_HEADS))
    bias_rows = place("bias_rows", (P, B_HEADS, BIAS_W), offset=t1.next())
    big = t1("big", (P, B_HEADS, SEQ))
    probT = t1("probT", (P, 16, P))
    rel_wide = place("rel_wide", (BUCKETS, B_HEADS, P), offset=WT_AT)
    bias_oh = place("bias_oh", (BUCKETS, BIAS_W), offset=WT_AT + B_HEADS * P * 4)
    t2 = inside(ffn_small + 16384, 6 * 2048 + 2 * 4096)
    conv_in = t2("conv_in", (P, 8, CONV - 1 + SEQ))
    bias_toe = t2("bias_toe", (P, B_HEADS, SEQ))
    params = t2("params", (P, P))
    gh_b = t2("gh_b", (P, 512))
    gkv_b = t2("gkv_b", (P, B_LATENT))
    yT = place("yT", (P, KD, SEQ), offset=ffn_small)
    hcat = y
    scratch_b = nc.dram_tensor("bias_scratch", [P * B_HEADS * BIAS_W], F32)
    w_in_v = a["w_in_e"][0].rearrange("(k p) n -> p k n", p=P)
    w_out_v = a["w_out_e"][0].rearrange("(k p) n -> p k n", p=P)

    def dve_const(e, link):
        link(e.memset(ones[:, :], 1.0))
        link(e.memset(eps_col[:, :], EPS))
        link(e.memset(one_col[:, :], 1.0))

    HALVES = 2

    class Stream:

        def __init__(self, tag, n_raw, raw_at, n_split, split_at):
            self.n_raw, self.n_split = n_raw, n_split
            b = LIN * 4
            self.raw = [place(f"{tag}_raw{s}", (P, LIN), offset=raw_at + s * b) for s in range(n_raw)]
            self.hi = [place(f"{tag}_hi{s}", (P, LIN), F32R, offset=split_at + 2 * s * b) for s in range(n_split)]
            self.lo = [place(f"{tag}_lo{s}", (P, LIN), F32R, offset=split_at + (2 * s + 1) * b) for s in range(n_split)]
            self.landed = [sig(f"w_landed{s}") for s in range(n_raw)]
            self.hi_made, self.lo_made, self.used = sig("w_hi_made"), sig("w_lo_made"), sig("w_used")
            self.dmas = {}
            self.shape = {}

        def load(self, e, n, parts):
            if n >= self.n_raw:
                e.wait_ge(self.lo_made.sem, self.lo_made.at((n - self.n_raw + 1) * HALVES))
            for lo, hi, src, k in parts:
                dst = self.raw[n % self.n_raw][:, :].rearrange("p (k n) -> p k n", k=k)[:, :, lo:hi]
                e.dma_start(dst, src).then_inc(self.landed[n % self.n_raw].sem, 16)

        def halves(self, n):
            k, w = self.shape.get(n, (KD, 256))
            for q in range(HALVES):
                yield [x[:, :].rearrange("p (k n) -> p k n", k=k)[:, q * k // 2:(q + 1) * k // 2, 0:w]
                       for x in (self.raw[n % self.n_raw], self.hi[n % self.n_split], self.lo[n % self.n_split])]

        def make_hi(self, e, n):
            s = n % self.n_raw
            e.wait_ge(self.landed[s].sem, self.landed[s].at(16 * sum(self.dmas.get(m, 1) for m in range(s, n + 1, self.n_raw))))
            if n >= self.n_split:
                e.wait_ge(self.used.sem, self.used.at(n - self.n_split + 1))
            for raw_, hi, _ in self.halves(n):
                e.copy(hi, raw_).then_inc(self.hi_made.sem, 1)

        def make_lo(self, e, n):
            for q, (raw_, hi, lo) in enumerate(self.halves(n)):
                e.wait_ge(self.hi_made.sem, self.hi_made.at(n * HALVES + q + 1))
                e.tensor_tensor(lo, raw_, hi.bitcast(F32), ALU.subtract).then_inc(self.lo_made.sem, 1)

        def over(self, units):
            for s in range(self.n_raw):
                self.landed[s].past(16 * sum(self.dmas.get(m, 1) for m in range(s, units, self.n_raw)))
            self.hi_made.past(units * HALVES)
            self.lo_made.past(units * HALVES)
            self.used.past(units)

        def half_ready(self, e, n, q):
            e.wait_ge(self.lo_made.sem, self.lo_made.at(n * HALVES + q + 1))

        def parts(self, n, k):
            return [w[n % self.n_split][:, :].rearrange("p (k n) -> p k n", k=k) for w in (self.hi, self.lo)]

        def by_token(self, e, n, bank, width=256, stride=256):
            wh, wl = self.parts(n, KD)
            for t in range(T):
                for k in range(KD):
                    if t == 0 and k % 4 == 0:
                        self.half_ready(e, n, k // 4)
                    tok = slice(t * P, (t + 1) * P)
                    dst = ps[:, bank, t * stride:t * stride + width]
                    ins = three_passes(e, dst, x_hi[:, k, tok], x_lo[:, k, tok], wh[:, k, 0:width], wl[:, k, 0:width],
                                       k == 0, k == KD - 1)
            ins.then_inc(self.used.sem, 1)
            return ins

        def by_channel(self, e, n, bank):
            wh, wl = self.parts(n, KD)
            for j in range(2):
                for k in range(KD):
                    if j == 0 and k % 4 == 0:
                        self.half_ready(e, n, k // 4)
                    ch = slice(j * P, (j + 1) * P)
                    ins = three_passes(e, ps[:, bank, j * SEQ:(j + 1) * SEQ], wh[:, k, ch], wl[:, k, ch],
                                       x_hi[:, k, :], x_lo[:, k, :], k == 0, k == KD - 1)
            ins.then_inc(self.used.sem, 1)

    def three_passes(e, dst, xh, xl, wh, wl, first, last):
        e.matmul(dst, xh, wh, start=first, stop=False)
        e.matmul(dst, xh, wl, start=False, stop=False)
        return e.matmul(dst, xl, wh, start=False, stop=last)

    def norm_T(row, split, yT=None, want_y=False, load=None):
        with nc.Block() as block:
            if load is not None:
                @block.sync
                def _(e):
                    load(e)

            @block.scalar
            def _(e):
                for t in range(T):
                    e.activation(y[:, t, :], h[:, t, :], ACT.Square, accum_out=stat[:, t:t + 1]).then_inc(sig("squares").sem, 1)
                e.wait_ge(sig("squares").sem, sig("squares").at(T))
                e.activation(stat[:, 2:4], stat[:, 0:2], ACT.Sqrt, bias=eps_col[:, :], scale=1.0 / D).then_inc(sig("rms").sem, 1)
                if not split:
                    for b in range(4):
                        e.wait_ge(sig("y_T").sem, sig("y_T").at(b + 1))
                        for k in (2 * b, 2 * b + 1):
                            j = k % 2
                            ins = e.activation(yT[:, k, :], ps[:, b, j * SEQ:(j + 1) * SEQ], ACT.Copy,
                                               scale=gains[:, row + k:row + k + 1])
                        ins.then_inc(sig("yT_hi").sem, 1)
                else:
                    for b in range(4):
                        e.wait_ge(sig("y_T").sem, sig("y_T").at(b + 1))
                        for k in (2 * b, 2 * b + 1):
                            j = k % 2
                            ins = e.activation(x_hi[:, k, :], ps[:, b, j * SEQ:(j + 1) * SEQ], ACT.Copy,
                                               scale=gains[:, row + k:row + k + 1])
                        ins.then_inc(sig("yT_hi").sem, 1)

            @block.vector
            def _(e):
                link = linker(e, "dve_step")
                e.wait_ge(sig("rms").sem, sig("rms").at(1))
                link(e.reciprocal(stat[:, 4:6], stat[:, 2:4]))
                for t in range(T):
                    e.tensor_scalar(y[:, t, :], h[:, t, :], stat[:, 4 + t:5 + t], None, ALU.mult).then_inc(sig("y_ready").sem, 1)
                if split:
                    for b in range(4):
                        e.wait_ge(sig("yT_hi").sem, sig("yT_hi").at(b + 1))
                        for k in (2 * b, 2 * b + 1):
                            j = k % 2
                            e.scalar_tensor_tensor(out=x_lo[:, k, :], in0=ps[:, b, j * SEQ:(j + 1) * SEQ],
                                                   scalar=gains[:, row + k:row + k + 1],
                                                   in1=x_hi[:, k, :].bitcast(F32), op0=ALU.mult, op1=ALU.subtract)
                link.end()

            @block.tensor
            def _(e):
                e.wait_ge(sig("y_ready").sem, sig("y_ready").at(T))
                for b in range(4):
                    for k in (2 * b, 2 * b + 1):
                        for t in range(T):
                            o = (k % 2) * SEQ + t * P
                            ins = e.transpose(ps[:, b, o:o + P], y[:, t, k * P:(k + 1) * P], ident[:, :])
                    ins.then_inc(sig("y_T").sem, 1)
        finished(squares=T, rms=1, y_ready=T, y_T=4, yT_hi=4)

    def dump():
        with nc.Block() as block:
            @block.sync
            def _(e):
                for t in range(T):
                    e.dma_start(out[0, t * P:(t + 1) * P, :], h[:, t, :]).then_inc(sig("out").sem, 16)
                e.wait_ge(sig("out").sem, sig("out").at(16 * T))

    QI, BQ, AQ, AV, AO, WO, MIX_UNITS = 1, 3, 5, 9, 11, 13, 17
    mix = Stream("mix", MIX_RAW, arena, MIX_SPLIT, arena + MIX_RAW * LIN * 4)
    mix.shape[0], mix.dmas[0] = (KD, NARROW), 3
    column = {}
    for first_unit, n_units, off in ((QI, 2, OFF_QI), (BQ, 2, OFF_BQ), (AQ, 4, OFF_AQ), (AV, 2, OFF_AV), (AO, 2, OFF_AO)):
        for j in range(n_units):
            column[first_unit + j] = off + 256 * j

    def load_mix_unit(e, n):
        if n == 0:
            mix.load(e, 0, [(0, B_LATENT, w_in_v[:, :, OFF_BC:OFF_BC + B_LATENT], KD),
                            (B_LATENT, B_LATENT + B_DH + 8, w_in_v[:, :, OFF_KI:D_IN], KD),
                            (B_LATENT + B_DH + 8, NARROW, w_in_v[:, :, OFF_AI:OFF_AI + 8], KD)])
        elif n < WO:
            mix.load(e, n, [(0, 256, w_in_v[:, :, column[n]:column[n] + 256], KD)])
        else:
            mix.load(e, n, [(0, 256, w_out_v[:, :, (n - WO) * 256:(n - WO + 1) * 256], KD)])

    def bank_of(hd):
        return 2 * (hd // 4) + hd % 2, (hd // 2 % 2) * SEQ

    GQK = stat[:, 8:9]
    rstd_q = small[:, 48:64]
    den, rden = msmall[:, 0:8], msmall[:, 8:16]
    q_sq = y[:, :, 0:512].rearrange("p t (j s) -> p t j s", j=2)
    N_PARAM_DMAS = 3 + 1 + 4 + 2 + 2
    PV = 2

    with nc.Block() as block:
        @block.sync
        def _(e):
            for t in range(T):
                e.dma_start(h[:, t, :], a["x"][0, t * P:(t + 1) * P, :]).then_inc(sig("x_loaded").sem, 16)
            e.dma_start(ident[:, :], a["c_ident"]).then_inc(sig("ident_loaded").sem, 16)
            s = sig("param_loaded")
            for row, name in ((ROW_MIX, "norm_mix"), (ROW_FFN, "norm_ffn"), (ROW_PLE, "norm_ple")):
                e.dma_start(params[row:row + 16, :], a[name].rearrange("l (k p) -> (l k) p", p=P)).then_inc(s.sem, 16)
            e.dma_start(params[ROW_CONV:ROW_CONV + 32, :],
                        a["conv_a"][0].rearrange("j (k p) -> (j k) p", p=P)).then_inc(s.sem, 16)
            for row, name in ((ROW_GQ, "norm_q_b"), (ROW_GK, "norm_k_b")):
                for half in range(2):
                    e.dma_start(params[row:row + 1, half * B_DH:(half + 1) * B_DH], a[name]).then_inc(s.sem, 16)
            e.dma_start(rel8[:, :], a["rel_bias"]).then_inc(s.sem, 16)
            e.dma_start(bias_oh[:, :], a["c_bias"]).then_inc(s.sem, 16)
            b8 = a["b_gate_e"].rearrange("a (g n) -> g n a", g=2)
            e.dma_start(bias_i[:, :], b8[0]).then_inc(s.sem, 16)
            e.dma_start(bias_f[:, :], b8[1]).then_inc(s.sem, 16)
            for n in range(3):
                load_mix_unit(e, n)
            s = sig("mix_loaded")
            e.dma_start(gkv_b[:, :], a["norm_kv_b"].partition_broadcast(P)[:, 0, :]).then_inc(s.sem, 16)
            e.dma_start(w_uk[:, :], a["w_uk_b"][0]).then_inc(s.sem, 16)
            e.dma_start(w_uv[:, :, :], a["w_uv_b"][0].rearrange("h c d -> c h d")).then_inc(s.sem, 16)
            e.dma_start(halves[:, :], a["c_halves"]).then_inc(s.sem, 16)
            e.dma_start(sel_h[:, :], a["c_select"]).then_inc(s.sem, 16)
            e.dma_start(gh_b[:, :], a["norm_h_a"].partition_broadcast(P)[:, 0, :]).then_inc(s.sem, 16)
            e.dma_start(before[:, :], a["c_before"]).then_inc(s.sem, 16)
            load_mix_unit(e, 3)
            load_mix_unit(e, 4)
            e.wait_ge(sig("bias_rows").sem, sig("bias_rows").at(B_HEADS))
            e.dma_start(scratch_b[:].rearrange("(p x) -> p x", p=P),
                        bias_rows[:, :, :].rearrange("p a b -> p (a b)")).then_inc(sig("bias_out").sem, 16)
            load_mix_unit(e, 5)
            e.wait_ge(sig("bias_out").sem, sig("bias_out").at(16))
            x = B_HEADS * BIAS_W - 1
            skewed = scratch_b[P - 1:P - 1 + P * x].rearrange("(p x) -> p x", x=x)
            for hd in range(B_HEADS):
                e.dma_start(bias_toe[:, hd, :], skewed[:, hd * BIAS_W:hd * BIAS_W + SEQ]).then_inc(sig("bias_in").sem, 16)
            for n in range(6, MIX_UNITS):
                load_mix_unit(e, n)

        @block.gpsimd
        def _(e):
            link = linker(e, "pool_step")
            link(e.memset(most_mask[:, :], -ACAUSAL))
            link(e.memset(neg_mask[:, :], 0.0))
            for m, fill in ((most_mask, ACAUSAL), (neg_mask, NEG)):
                e.affine_select(out=m[:, :], in_=m[:, :], pattern=[[-1, P]], compare_op=ALU.is_ge, fill=fill,
                                base=0, channel_multiplier=1).then_inc(sig("masks").sem, 1)
            e.wait_ge(sig("w_exp").sem, sig("w_exp").at(A_HEADS))
            for c in (0, SEQ):
                e.affine_select(out=wT[:, :, c:c + P], in_=wT[:, :, c:c + P], pattern=[[0, A_HEADS], [1, P]],
                                compare_op=ALU.is_ge, fill=0.0, base=0, channel_multiplier=-1).then_inc(sig("w_masked").sem, 1)
            link.end()

        @block.scalar
        def _(e):
            for t in range(T):
                e.wait_ge(sig("x_loaded").sem, sig("x_loaded").at(16 * T))
                e.activation(y[:, t, :], h[:, t, :], ACT.Square, accum_out=stat[:, t:t + 1]).then_inc(sig("squares").sem, 1)
            e.wait_ge(sig("squares").sem, sig("squares").at(T))
            e.wait_ge(sig("consts").sem, sig("consts").at(1))
            e.activation(stat[:, 2:4], stat[:, 0:2], ACT.Sqrt, bias=eps_col[:, :], scale=1.0 / D).then_inc(sig("rms").sem, 1)
            e.wait_ge(sig("gains").sem, sig("gains").at(1))
            for b in range(4):
                e.wait_ge(sig("y_T").sem, sig("y_T").at(b + 1))
                for k in (2 * b, 2 * b + 1):
                    ins = e.activation(x_hi[:, k, :], ps[:, 2 + b, (k % 2) * SEQ:(k % 2 + 1) * SEQ], ACT.Copy,
                                       scale=gains[:, ROW_MIX + k:ROW_MIX + k + 1])
                ins.then_inc(sig("yT_hi").sem, 1)
            for n in range(3):
                mix.make_hi(e, n)

            def projected(n):
                e.wait_ge(mix.used.sem, mix.used.at(n + 1))
                return ps[:, n % 2, :]

            def relu_index(t):
                for b in range(4):
                    e.wait_ge(sig("idx_mm").sem, sig("idx_mm").at(2 * t + b // 2 + 1))
                    hd = 4 * (b // 2) + b % 2
                    e.activation(big[:, hd:hd + 3:2, 0:P * (t + 1)],
                                 ps[:, 4 + b, :].rearrange("p (j s) -> p j s", j=2)[:, :, 0:P * (t + 1)],
                                 ACT.Relu).then_inc(sig("idx_relu").sem, 1)

            def probabilities(t):
                S = P * (t + 1)
                e.wait_ge(sig("nmax").sem, sig("nmax").at(t + 1))
                for hd in range(B_HEADS):
                    ins = e.activation(big[:, hd, 0:S], big[:, hd, 0:S], ACT.Exp, bias=small[:, 64 + hd:65 + hd],
                                       accum_out=small[:, 72 + hd:73 + hd])
                ins.then_inc(sig("probs").sem, 1)

            def probabilities_T(t):
                for g in range(2 * (t + 1)):
                    e.wait_ge(sig("probT_mm").sem, sig("probT_mm").at(2 * t + g + 1))
                    e.copy(probT[:, 4 * g:4 * g + 4, :],
                           ps[:, 4 + g, :].rearrange("p (j s) -> p j s", j=4)).then_inc(sig("probT").sem, 1)

            def silu(chunks):
                for c in chunks:
                    e.wait_ge(sig("conv").sem, sig("conv").at(c + 1))
                    e.activation(qk[:, c, :], qk[:, c, :], ACT.Silu).then_inc(sig("qk").sem, 1)

            def decay_weights(heads):
                for hd in heads:
                    e.wait_ge(sig("mB_mm").sem, sig("mB_mm").at(hd // 2 * 2 + 2))
                    mB = ps[:, 2, (hd % 2) * SEQ:(hd % 2 + 1) * SEQ]
                    e.activation(wT[:, hd, 0:SEQ], mB, ACT.Exp, bias=cols[:, 0, hd:hd + 1], scale=-1.0)
                    e.activation(wT[:, hd, SEQ:384], mB[:, P:SEQ], ACT.Exp, bias=cols[:, 1, hd:hd + 1],
                                 scale=-1.0).then_inc(sig("w_exp").sem, 1)

            p = projected(0)
            e.copy(narrow[:, :, :], p.rearrange("p (t n) -> p t n", t=T)[:, :, 0:NARROW]).then_inc(sig("proj_out").sem, 1)
            e.wait_ge(sig("proj_out").sem, sig("proj_out").at(1))
            for t in range(T):
                e.activation(isc[:, t * P:(t + 1) * P], bc[:, t, :], ACT.Square,
                             accum_out=small[:, t:t + 1]).then_inc(sig("lat_sq").sem, 1)
            e.wait_ge(sig("lat_sq").sem, sig("lat_sq").at(T))
            e.activation(small[:, 2:4], small[:, 0:2], ACT.Sqrt, bias=eps_col[:, :],
                         scale=1.0 / B_LATENT).then_inc(sig("lat_rms").sem, 1)
            for hd in range(4):
                e.wait_ge(sig("bias_mm").sem, sig("bias_mm").at(hd + 1))
                e.copy(bias_rows[:, hd, :], ps[:, 4 + hd, 0:BIAS_W]).then_inc(sig("bias_rows").sem, 1)
            mix.make_hi(e, 3)
            p = projected(1)
            e.copy(qi[:, 0:2, :], p.rearrange("p (j s) -> p j s", j=2)).then_inc(sig("proj_out").sem, 1)
            e.wait_ge(sig("kiT_mm").sem, sig("kiT_mm").at(1))
            e.copy(ki2[:, :], ps[:, 2, 0:SEQ]).then_inc(sig("ki2").sem, 1)
            e.wait_ge(sig("latT_mm").sem, sig("latT_mm").at(1))
            e.copy(latT[:, :], ps[:, 3, 0:SEQ]).then_inc(sig("latT").sem, 1)
            for hd in range(4, B_HEADS):
                e.wait_ge(sig("bias_mm").sem, sig("bias_mm").at(hd + 1))
                e.copy(bias_rows[:, hd, :], ps[:, hd, 0:BIAS_W]).then_inc(sig("bias_rows").sem, 1)
            mix.make_hi(e, 4)
            p = projected(2)
            e.copy(qi[:, 2:4, :], p.rearrange("p (j s) -> p j s", j=2)).then_inc(sig("proj_out").sem, 1)
            e.wait_ge(sig("uv_mm").sem, sig("uv_mm").at(1))
            for t in range(T):
                e.activation(isc[:, t * B_DH:(t + 1) * B_DH], ps[:, 3, SEQ + t * B_DH:SEQ + (t + 1) * B_DH], ACT.Square,
                             accum_out=small[:, 8 + t:9 + t]).then_inc(sig("k_sq").sem, 1)
            e.wait_ge(sig("k_sq").sem, sig("k_sq").at(T))
            e.activation(small[:, 10:12], small[:, 8:10], ACT.Sqrt, bias=eps_col[:, :],
                         scale=1.0 / B_DH).then_inc(sig("k_rms").sem, 1)
            for t in range(T):
                e.copy(vu[:, t, :], ps[:, 4 + t, :]).then_inc(sig("vu").sem, 1)
            e.wait_ge(sig("gates_mm").sem, sig("gates_mm").at(1))
            e.activation(gate_f[:, :], ps[0:A_HEADS, 2, SEQ:2 * SEQ], ACT.Identity, bias=bias_f[:, :]).then_inc(sig("gate_in").sem, 1)
            e.activation(gate_i[:, :], ps[0:A_HEADS, 2, 0:SEQ], ACT.Identity, bias=bias_i[:, :]).then_inc(sig("gate_in").sem, 1)
            mix.make_hi(e, 5)
            p = projected(3)
            e.copy(bqT[:, 0:2, :], p.rearrange("p (j s) -> p j s", j=2)).then_inc(sig("proj_out").sem, 1)
            e.wait_ge(sig("bias_out").sem, sig("bias_out").at(16))
            relu_index(0)
            e.wait_ge(sig("kbT_mm").sem, sig("kbT_mm").at(1))
            e.activation(kbT[:, :], ps[:, 3, 0:SEQ], ACT.Copy, scale=GQK).then_inc(sig("kbT").sem, 1)
            mix.make_hi(e, 6)
            e.wait_ge(sig("absf").sem, sig("absf").at(1))
            e.activation(g1[:, :], g1[:, :], ACT.Exp, scale=-1.0).then_inc(sig("exp_f").sem, 1)
            e.wait_ge(sig("exp_f").sem, sig("exp_f").at(1))
            e.activation(g1[:, :], g1[:, :], ACT.Ln, bias=one_col[0:A_HEADS, :]).then_inc(sig("softplus").sem, 1)
            p = projected(4)
            e.copy(bqT[:, 2:4, :], p.rearrange("p (j s) -> p j s", j=2)).then_inc(sig("proj_out").sem, 1)
            mix.make_hi(e, 7)
            e.wait_ge(sig("proj_out").sem, sig("proj_out").at(5))
            e.activation(q_sq, bqT[:, :, :].rearrange("p (t j) s -> p t j s", j=2), ACT.Square).then_inc(sig("q_sq").sem, 1)
            p = projected(5)
            e.copy(conv_in[:, 0:2, CONV - 1:], p.rearrange("p (j s) -> p j s", j=2)).then_inc(sig("proj_out").sem, 1)
            mix.make_hi(e, 8)
            e.wait_ge(sig("gate_cols").sem, sig("gate_cols").at(1))
            e.activation(small[:, 32:48], ps[:, 3, 384:400], ACT.Sqrt, bias=eps_col[:, :],
                         scale=1.0 / B_DH).then_inc(sig("q_rms").sem, 1)
            e.copy(cols[:, :, :], ps[:, 3, 400:416].rearrange("p (t n) -> p t n", t=T)).then_inc(sig("cols").sem, 1)
            e.wait_ge(sig("cols").sem, sig("cols").at(1))
            e.activation(msmall[:, 16:24].rearrange("p (h t) -> p t h", t=T), cols[:, :, 4:8], ACT.Exp)
            decay_weights((0, 1))
            p = projected(6)
            e.copy(conv_in[:, 2:4, CONV - 1:], p.rearrange("p (j s) -> p j s", j=2)).then_inc(sig("proj_out").sem, 1)
            mix.make_hi(e, 9)
            probabilities(0)
            p = projected(7)
            e.copy(conv_in[:, 4:6, CONV - 1:], p.rearrange("p (j s) -> p j s", j=2)).then_inc(sig("proj_out").sem, 1)
            mix.make_hi(e, 10)
            decay_weights((2, 3))
            probabilities_T(0)
            p = projected(8)
            e.copy(conv_in[:, 6:8, CONV - 1:], p.rearrange("p (j s) -> p j s", j=2)).then_inc(sig("proj_out").sem, 1)
            mix.make_hi(e, 11)
            relu_index(1)
            for n in (9, 10):
                p = projected(n)
                for t in range(T):
                    ins = e.copy(v_ones[:, t, 2 * (n - AV):2 * (n - AV) + 2, 0:P], p[:, t * SEQ:(t + 1) * SEQ].rearrange("p (h d) -> p h d", h=2))
                ins.then_inc(sig("proj_out").sem, 1)
                mix.make_hi(e, n + 3)
            silu(range(8))
            for n in (11, 12):
                p = projected(n)
                e.activation(ao[:, :, (n - AO) * 256:(n - AO + 1) * 256], p.rearrange("p (t n) -> p t n", t=T),
                             ACT.Sigmoid).then_inc(sig("proj_out").sem, 1)
                mix.make_hi(e, n + 3)
            probabilities(1)
            for hd in range(A_HEADS):
                e.wait_ge(sig("h_raw").sem, sig("h_raw").at(hd + 1))
                for t in range(T):
                    e.activation(wT[:, hd, t * P:(t + 1) * P], hcat[:, t, hd * P:(hd + 1) * P], ACT.Square,
                                 accum_out=msmall[:, 24 + 2 * hd + t:25 + 2 * hd + t]).then_inc(sig("h_sq").sem, 1)
            e.wait_ge(sig("h_sq").sem, sig("h_sq").at(8))
            e.activation(msmall[:, 32:40], msmall[:, 24:32], ACT.Sqrt, bias=eps_col[:, :], scale=1.0 / P).then_inc(sig("h_rms").sem, 1)
            probabilities_T(1)
            for b in range(4):
                e.wait_ge(sig("hcat_T").sem, sig("hcat_T").at(b + 1))
                bank = (0, 1, 5, 6)[b]
                e.copy(x_hi[:, 2 * b:2 * b + 2, :], ps[:, bank, :].rearrange("p (j s) -> p j s", j=2)).then_inc(sig("hT_hi").sem, 1)
            mix.make_hi(e, 16)

        @block.vector
        def _(e):
            link = linker(e, "dve_step")
            link(e.memset(ones[:, :], 1.0))
            link(e.memset(one_col[:, :], 1.0))
            e.memset(eps_col[:, :], EPS).then_inc(sig("consts").sem, 1)
            link(e.memset(conv_in[:, :, 0:CONV - 1], 0.0))
            link(e.memset(v_ones[:, :, :, P:P + 1], 1.0))
            e.wait_ge(sig("rms").sem, sig("rms").at(1))
            link(e.reciprocal(stat[:, 4:6], stat[:, 2:4]))
            for t in range(T):
                e.tensor_scalar(y[:, t, :], h[:, t, :], stat[:, 4 + t:5 + t], None, ALU.mult).then_inc(sig("y_ready").sem, 1)
            e.wait_ge(sig("params_T").sem, sig("params_T").at(1))
            e.tensor_copy(gains[:, 0:N_ROWS], ps[:, 6, 0:N_ROWS]).then_inc(sig("gains").sem, 1)
            e.tensor_copy(rel_wide[:, :, :], rel8[:, :].unsqueeze(2).to_broadcast([BUCKETS, B_HEADS, P])).then_inc(sig("rel_wide").sem, 1)
            for b in range(4):
                e.wait_ge(sig("yT_hi").sem, sig("yT_hi").at(b + 1))
                for k in (2 * b, 2 * b + 1):
                    ins = e.scalar_tensor_tensor(out=x_lo[:, k, :], in0=ps[:, 2 + b, (k % 2) * SEQ:(k % 2 + 1) * SEQ],
                                                 scalar=gains[:, ROW_MIX + k:ROW_MIX + k + 1],
                                                 in1=x_hi[:, k, :].bitcast(F32), op0=ALU.mult, op1=ALU.subtract)
                ins.then_inc(sig("yT_lo").sem, 1)
            for n in range(3):
                mix.make_lo(e, n)
            link(e.scalar_tensor_tensor(out=GQK, in0=gains[:, ROW_GQ:ROW_GQ + 1], scalar=B_DH ** -0.5,
                                        in1=gains[:, ROW_GK:ROW_GK + 1], op0=ALU.mult, op1=ALU.mult))
            e.wait_ge(sig("proj_out").sem, sig("proj_out").at(1))
            e.tensor_copy(ki_twice[:, :, :, :], ki.unsqueeze(2).to_broadcast([P, T, 2, B_DH])).then_inc(sig("ki_twice").sem, 1)
            e.wait_ge(sig("mix_loaded").sem, sig("mix_loaded").at(16 * 7))
            e.wait_ge(sig("lat_rms").sem, sig("lat_rms").at(1))
            link(e.reciprocal(small[:, 4:6], small[:, 2:4]))
            for t in range(T):
                ins = e.scalar_tensor_tensor(out=lat[:, t, :], in0=bc[:, t, :], scalar=small[:, 4 + t:5 + t],
                                             in1=gkv_b[:, :], op0=ALU.mult, op1=ALU.mult)
            ins.then_inc(sig("lat").sem, 1)
            mix.make_lo(e, 3)
            mix.make_lo(e, 4)
            e.wait_ge(sig("k_rms").sem, sig("k_rms").at(1))
            link(e.reciprocal(small[:, 12:14], small[:, 10:12]))
            for t in range(T):
                for half in range(2):
                    ins = e.tensor_scalar(kb2[:, t, half * B_DH:(half + 1) * B_DH], ps[:, 3, SEQ + t * B_DH:SEQ + (t + 1) * B_DH],
                                          small[:, 12 + t:13 + t], None, ALU.mult)
            ins.then_inc(sig("kb").sem, 1)
            e.wait_ge(sig("gate_in").sem, sig("gate_in").at(2))
            e.scalar_tensor_tensor(out=g1[:, :], in0=gate_f[:, :], scalar=-1.0, in1=gate_f[:, :],
                                   op0=ALU.mult, op1=ALU.max).then_inc(sig("absf").sem, 1)
            mix.make_lo(e, 5)
            mix.make_lo(e, 6)

            def top_keys(t):
                S = P * (t + 1)
                last = slice(S - P, S)
                for hd in range(B_HEADS):
                    e.wait_ge(sig("idx_relu").sem, sig("idx_relu").at(4 * t + bank_of(hd)[0] + 1))
                    w = wi[:, t, hd:hd + 1]
                    if hd == 0:
                        ins = e.tensor_scalar(isc[:, 0:S], big[:, 0, 0:S], w, None, ALU.mult)
                    else:
                        ins = e.scalar_tensor_tensor(out=isc[:, 0:S], in0=big[:, hd, 0:S], scalar=w, in1=isc[:, 0:S],
                                                     op0=ALU.mult, op1=ALU.add)
                    link(ins)
                e.wait_ge(sig("masks").sem, sig("masks").at(2))
                link(e.tensor_tensor(isc[:, last], isc[:, last], most_mask[:, :], ALU.min))
                for _r in range(TOPK // 8):
                    link(e.max(top8[:, :], isc[:, 0:S]))
                    link(e.match_replace(isc[:, 0:S], top8[:, :], isc[:, 0:S], TAKEN))
                link(e.tensor_scalar(isc[:, 0:S], isc[:, 0:S], (ACAUSAL + TAKEN) / 2, NEG, ALU.is_gt, ALU.mult))
                link(e.tensor_tensor(isc[:, last], isc[:, last], neg_mask[:, :], ALU.min))

            def masked_logits(t):
                S = P * (t + 1)
                for hd in range(B_HEADS):
                    b, c = bank_of(hd)
                    e.wait_ge(sig("logit_mm").sem, sig("logit_mm").at(2 * t + hd // 4 + 1))
                    link(e.scalar_tensor_tensor(out=big[:, hd, 0:S], in0=ps[:, 4 + b, c:c + S],
                                                scalar=rstd_q[:, 8 * t + hd:8 * t + hd + 1],
                                                in1=bias_toe[:, hd, SEQ - S:SEQ], op0=ALU.mult, op1=ALU.add))
                link(e.tensor_tensor(big[:, :, 0:S], big[:, :, 0:S], isc[:, 0:S].unsqueeze(1).to_broadcast([P, B_HEADS, S]), ALU.add))
                e.tensor_reduce(small[:, 64:72], big[:, :, 0:S], AX_X, ALU.max, negate=True).then_inc(sig("nmax").sem, 1)

            def attention_out(t):
                e.wait_ge(sig("probs").sem, sig("probs").at(t + 1))
                link(e.reciprocal(small[:, 80:88], small[:, 72:80]))
                e.wait_ge(sig("pv_mm").sem, sig("pv_mm").at(t + 1))
                e.tensor_tensor(hcat[:, t, 512:1024].rearrange("p (h d) -> p h d", h=B_HEADS),
                                ps[:, PV, :].rearrange("p (h d) -> p h d", h=B_HEADS),
                                small[:, 80:88].unsqueeze(2).to_broadcast([P, B_HEADS, B_DH]),
                                ALU.mult).then_inc(sig("attn_out").sem, 1)

            def conv(chunks):
                for c in chunks:
                    e.wait_ge(sig("proj_out").sem, sig("proj_out").at(AQ + c // 2 + 1))
                    w = lambda j: gains[:, ROW_CONV + 8 * j + c:ROW_CONV + 8 * j + c + 1]
                    link(e.tensor_scalar(qk[:, c, :], conv_in[:, c, 0:SEQ], w(0), None, ALU.mult))
                    for j in range(1, CONV):
                        ins = e.scalar_tensor_tensor(out=qk[:, c, :], in0=conv_in[:, c, j:j + SEQ], scalar=w(j),
                                                     in1=qk[:, c, :], op0=ALU.mult, op1=ALU.add)
                        if j < CONV - 1:
                            link(ins)
                    ins.then_inc(sig("conv").sem, 1)

            e.wait_ge(sig("softplus").sem, sig("softplus").at(1))
            link(e.scalar_tensor_tensor(out=g2[:, :], in0=gate_f[:, :], scalar=0.0, in1=g1[:, :], op0=ALU.min, op1=ALU.subtract))
            e.wait_ge(sig("bias_mm").sem, sig("bias_mm").at(B_HEADS))
            one_row = wT[0:A_HEADS, 0, 0:SEQ]
            link(e.memset(one_row, 1.0))
            link(e.tensor_tensor_scan(g3[:, :], one_row, g2[:, :], 0.0, ALU.mult, ALU.add))
            link(e.tensor_tensor(g1[:, :], gate_i[:, :], g3[:, :], ALU.subtract))
            link(e.tensor_tensor_scan(g2[:, :], one_row, g1[:, :], 0.0, ALU.mult, ALU.max))
            e.scalar_tensor_tensor(out=g4[:, :], in0=g3[:, :], scalar=-1.0, in1=g2[:, :],
                                   op0=ALU.mult, op1=ALU.subtract).then_inc(sig("gate_rows").sem, 1)
            mix.make_lo(e, 7)
            top_keys(0)
            mix.make_lo(e, 8)
            e.wait_ge(sig("q_rms").sem, sig("q_rms").at(1))
            link(e.reciprocal(rstd_q, small[:, 32:48]))
            e.wait_ge(sig("bias_in").sem, sig("bias_in").at(16 * B_HEADS))
            masked_logits(0)
            mix.make_lo(e, 9)
            conv((0, 1))
            mix.make_lo(e, 10)
            conv((2, 3))
            mix.make_lo(e, 11)
            attention_out(0)
            conv((4, 5))
            top_keys(1)
            mix.make_lo(e, 12)
            conv((6, 7))
            mix.make_lo(e, 13)
            masked_logits(1)
            mix.make_lo(e, 14)
            mix.make_lo(e, 15)
            for t in range(T):
                e.wait_ge(sig("proj_out").sem, sig("proj_out").at(WO))
                link(e.tensor_tensor(ao[:, t, :], ao[:, t, :], gh_b[:, :], ALU.mult))
            e.wait_ge(sig("w_masked").sem, sig("w_masked").at(2))
            for g in range(2):
                for hd in (2 * g, 2 * g + 1):
                    e.wait_ge(sig("qk_mm").sem, sig("qk_mm").at(hd + 1))
                    e.scalar_tensor_tensor(out=wT[:, hd, :], in0=ps[:, hd % 2, 0:384], scalar=A_DK ** -0.5,
                                           in1=wT[:, hd, :], op0=ALU.mult, op1=ALU.mult).then_inc(sig("scores").sem, 1)
                e.wait_ge(sig("num_mm").sem, sig("num_mm").at(2 * g + 2))
                d4, r4 = den[:, 4 * g:4 * g + 4], rden[:, 4 * g:4 * g + 4]
                link(e.tensor_copy(d4.rearrange("p (h t) -> p h t", t=T),
                                   ps[:, 0:2, 0:258].rearrange("p h (t d) -> p h t d", t=T)[:, :, :, P]))
                link(e.scalar_tensor_tensor(out=r4, in0=d4, scalar=-1.0, in1=d4, op0=ALU.mult, op1=ALU.max))
                link(e.tensor_tensor(r4, r4, msmall[:, 16 + 4 * g:20 + 4 * g], ALU.max))
                link(e.reciprocal(d4, r4))
                for hd in (2 * g, 2 * g + 1):
                    for t in range(T):
                        ins = e.tensor_scalar(hcat[:, t, hd * P:(hd + 1) * P], ps[:, hd % 2, t * 129:t * 129 + P],
                                              den[:, 2 * hd + t:2 * hd + t + 1], None, ALU.mult)
                    ins.then_inc(sig("h_raw").sem, 1)
            e.wait_ge(sig("h_rms").sem, sig("h_rms").at(1))
            link(e.reciprocal(msmall[:, 40:48], msmall[:, 32:40]))
            for hd in range(A_HEADS):
                for t in range(T):
                    c = slice(hd * P, (hd + 1) * P)
                    ins = e.scalar_tensor_tensor(out=hcat[:, t, c], in0=hcat[:, t, c], scalar=msmall[:, 40 + 2 * hd + t:41 + 2 * hd + t],
                                                 in1=ao[:, t, c], op0=ALU.mult, op1=ALU.mult)
                ins.then_inc(sig("h_out").sem, 1)
            attention_out(1)
            for b in range(4):
                e.wait_ge(sig("hT_hi").sem, sig("hT_hi").at(b + 1))
                bank = (0, 1, 5, 6)[b]
                e.tensor_tensor(x_lo[:, 2 * b:2 * b + 2, :], ps[:, bank, :].rearrange("p (j s) -> p j s", j=2),
                                x_hi[:, 2 * b:2 * b + 2, :].bitcast(F32), ALU.subtract).then_inc(sig("hT_lo").sem, 1)
            mix.make_lo(e, 16)
            for n in range(WO, MIX_UNITS):
                e.wait_ge(mix.used.sem, mix.used.at(n + 1))
                c = slice((n - WO) * 256, (n - WO + 1) * 256)
                e.tensor_tensor(h[:, :, c], h[:, :, c], ps[:, (3, 7, 2, 4)[n - WO], :].rearrange("p (t n) -> p t n", t=T), ALU.add)
            link.end()

        @block.tensor
        def _(e):
            e.wait_ge(sig("ident_loaded").sem, sig("ident_loaded").at(16))
            e.wait_ge(sig("param_loaded").sem, sig("param_loaded").at(16 * N_PARAM_DMAS))
            e.transpose(ps[:, 6, 0:N_ROWS], params[0:N_ROWS, :], ident[0:N_ROWS, 0:N_ROWS]).then_inc(sig("params_T").sem, 1)
            e.wait_ge(sig("y_ready").sem, sig("y_ready").at(T))
            for b in range(4):
                for k in (2 * b, 2 * b + 1):
                    for t in range(T):
                        o = (k % 2) * SEQ + t * P
                        ins = e.transpose(ps[:, 2 + b, o:o + P], y[:, t, k * P:(k + 1) * P], ident[:, :])
                ins.then_inc(sig("y_T").sem, 1)

            def project(n):
                if n >= 2:
                    e.wait_ge(sig("proj_out").sem, sig("proj_out").at(n - 1))
                if n == 0:
                    mix.by_token(e, 0, 0, width=NARROW)
                elif n < AV:
                    mix.by_channel(e, n, n % 2)
                else:
                    mix.by_token(e, n, n % 2)

            def bias_table(heads):
                for hd in heads:
                    e.matmul(ps[:, 4 + hd % 4, 0:BIAS_W], rel_wide[:, hd, :], bias_oh[:, :], start=True,
                             stop=True).then_inc(sig("bias_mm").sem, 1)

            def index_scores(t):
                S = P * (t + 1)
                for hd in range(B_HEADS):
                    b, c = bank_of(hd)
                    part = slice((hd % 2) * B_DH, (hd % 2 + 1) * B_DH)
                    ins = e.matmul(ps[:, 4 + b, c:c + S], qi[part, hd // 2, t * P:(t + 1) * P], ki2[part, 0:S],
                                   start=True, stop=True)
                    if hd % 4 == 3:
                        ins.then_inc(sig("idx_mm").sem, 1)

            def logits(t):
                S = P * (t + 1)
                e.wait_ge(sig("idx_relu").sem, sig("idx_relu").at(4 * t + 4))
                for hd in range(B_HEADS):
                    b, c = bank_of(hd)
                    part = slice((hd % 2) * B_DH, (hd % 2 + 1) * B_DH)
                    ins = e.matmul(ps[:, 4 + b, c:c + S], bqT[part, hd // 2, t * P:(t + 1) * P], kbT[part, 0:S],
                                   start=True, stop=True)
                    if hd % 4 == 3:
                        ins.then_inc(sig("logit_mm").sem, 1)

            def probabilities_T(t):
                e.wait_ge(sig("probs").sem, sig("probs").at(t + 1))
                for n in range(8 * (t + 1)):
                    hd, k = n // (t + 1), n % (t + 1)
                    ins = e.transpose(ps[:, 4 + n // 4, (n % 4) * P:(n % 4 + 1) * P], big[:, hd, k * P:(k + 1) * P], ident[:, :])
                    if n % 4 == 3:
                        ins.then_inc(sig("probT_mm").sem, 1)

            def attend(t):
                for n in range(8 * (t + 1)):
                    hd, k = n // (t + 1), n % (t + 1)
                    if n % 4 == 0:
                        e.wait_ge(sig("probT").sem, sig("probT").at(2 * t + n // 4 + 1))
                    ins = e.matmul(ps[:, PV, hd * B_DH:(hd + 1) * B_DH], probT[:, n, :], vu[:, k, hd * B_DH:(hd + 1) * B_DH],
                                   start=(k == 0), stop=(k == t))
                ins.then_inc(sig("pv_mm").sem, 1)

            e.wait_ge(sig("yT_lo").sem, sig("yT_lo").at(4))
            project(0)
            e.wait_ge(sig("rel_wide").sem, sig("rel_wide").at(1))
            bias_table(range(4))
            project(1)
            e.wait_ge(sig("ki_twice").sem, sig("ki_twice").at(1))
            for t in range(T):
                ins = e.transpose(ps[:, 2, t * P:(t + 1) * P], ki_twice[:, t, :, :].rearrange("p g d -> p (g d)"), ident[:, :])
            ins.then_inc(sig("kiT_mm").sem, 1)
            e.wait_ge(sig("lat").sem, sig("lat").at(1))
            for t in range(T):
                ins = e.transpose(ps[:, 3, t * P:(t + 1) * P], lat[:, t, :], ident[:, :])
            ins.then_inc(sig("latT_mm").sem, 1)
            e.wait_ge(sig("bias_rows").sem, sig("bias_rows").at(4))
            bias_table(range(4, B_HEADS))
            project(2)
            e.wait_ge(sig("latT").sem, sig("latT").at(1))
            e.wait_ge(sig("bias_rows").sem, sig("bias_rows").at(6))
            for t in range(T):
                e.matmul(ps[:, 3, SEQ + t * B_DH:SEQ + (t + 1) * B_DH], latT[:, t * P:(t + 1) * P], w_uk[:, :], start=True, stop=True)
                ins = e.matmul(ps[:, 4 + t, :], latT[:, t * P:(t + 1) * P], w_uv[:, :, :].rearrange("p h d -> p (h d)"),
                               start=True, stop=True)
            ins.then_inc(sig("uv_mm").sem, 1)
            e.wait_ge(sig("ki2").sem, sig("ki2").at(1))
            for g in range(2):
                for t in range(T):
                    c = NARROW - 2 * A_HEADS + g * A_HEADS
                    ins = e.transpose(ps[0:A_HEADS, 2, g * SEQ + t * P:g * SEQ + (t + 1) * P], narrow[:, t, c:c + A_HEADS], ident[:, :])
            ins.then_inc(sig("gates_mm").sem, 1)
            project(3)
            e.wait_ge(sig("bias_rows").sem, sig("bias_rows").at(B_HEADS))
            e.wait_ge(sig("vu").sem, sig("vu").at(T))
            index_scores(0)
            e.wait_ge(sig("kb").sem, sig("kb").at(1))
            for t in range(T):
                ins = e.transpose(ps[:, 3, t * P:(t + 1) * P], kb2[:, t, :], ident[:, :])
            ins.then_inc(sig("kbT_mm").sem, 1)
            project(4)
            project(5)
            e.wait_ge(sig("q_sq").sem, sig("q_sq").at(1))
            for t in range(T):
                for j in range(4):
                    o = 384 + 8 * t + 2 * j
                    e.matmul(ps[:, 3, o:o + 2], q_sq[:, j // 2, j % 2, t * P:(t + 1) * P], halves[:, :], start=True, stop=True)
            e.wait_ge(sig("gate_rows").sem, sig("gate_rows").at(1))
            for t in range(T):
                o = 400 + 8 * t
                e.transpose(ps[:, 3, o:o + 4], g1[:, t * P:(t + 1) * P], ident[0:A_HEADS, 0:A_HEADS])
                ins = e.transpose(ps[:, 3, o + 4:o + 8], g4[:, t * P:(t + 1) * P], ident[0:A_HEADS, 0:A_HEADS])
            ins.then_inc(sig("gate_cols").sem, 1)
            for hd in (0, 1):
                e.matmul(ps[:, 2, hd * SEQ:(hd + 1) * SEQ], sel_h[:, hd * P:(hd + 1) * P], g2[:, :], start=True,
                         stop=True).then_inc(sig("mB_mm").sem, 1)
            logits(0)
            project(6)
            e.wait_ge(sig("w_exp").sem, sig("w_exp").at(2))
            for hd in (2, 3):
                e.matmul(ps[:, 2, (hd - 2) * SEQ:(hd - 1) * SEQ], sel_h[:, hd * P:(hd + 1) * P], g2[:, :], start=True,
                         stop=True).then_inc(sig("mB_mm").sem, 1)
            project(7)
            probabilities_T(0)
            project(8)
            e.wait_ge(sig("w_exp").sem, sig("w_exp").at(A_HEADS))
            attend(0)
            index_scores(1)
            project(9)
            logits(1)
            for n in range(10, WO):
                project(n)
            for g in range(2):
                for hd in (2 * g, 2 * g + 1):
                    e.wait_ge(sig("qk").sem, sig("qk").at(8))
                    if g == 0:
                        e.wait_ge(sig("proj_out").sem, sig("proj_out").at(WO))
                    else:
                        e.wait_ge(sig("h_raw").sem, sig("h_raw").at(hd - 1))
                    e.matmul(ps[:, hd % 2, 0:SEQ], qk[:, 4 + hd, 0:P], qk[:, hd, :], start=True, stop=True)
                    e.matmul(ps[:, hd % 2, SEQ:384], qk[:, 4 + hd, P:SEQ], qk[:, hd, P:SEQ], start=True,
                             stop=True).then_inc(sig("qk_mm").sem, 1)
                for hd in (2 * g, 2 * g + 1):
                    e.wait_ge(sig("scores").sem, sig("scores").at(hd + 1))
                    e.matmul(ps[:, hd % 2, 0:129], wT[:, hd, 0:P], v_ones[:, 0, hd, :], start=True, stop=True)
                    e.matmul(ps[:, hd % 2, 129:258], wT[:, hd, P:SEQ], v_ones[:, 0, hd, :], start=True, stop=False)
                    e.matmul(ps[:, hd % 2, 129:258], wT[:, hd, SEQ:384], v_ones[:, 1, hd, :], start=False,
                             stop=True).then_inc(sig("num_mm").sem, 1)
            probabilities_T(1)
            e.wait_ge(sig("attn_out").sem, sig("attn_out").at(1))
            attend(1)
            for b in range(4):
                bank = (0, 1, 5, 6)[b]
                for k in (2 * b, 2 * b + 1):
                    if b < 2:
                        e.wait_ge(sig("h_out").sem, sig("h_out").at(k + 1))
                    else:
                        e.wait_ge(sig("attn_out").sem, sig("attn_out").at(T))
                    for t in range(T):
                        o = (k % 2) * SEQ + t * P
                        ins = e.transpose(ps[:, bank, o:o + P], hcat[:, t, k * P:(k + 1) * P], ident[:, :])
                ins.then_inc(sig("hcat_T").sem, 1)
            e.wait_ge(sig("hT_lo").sem, sig("hT_lo").at(4))
            for n in range(WO, MIX_UNITS):
                mix.by_token(e, n, (3, 7, 2, 4)[n - WO])
    mix.over(MIX_UNITS)
    finished(squares=T, rms=1, y_ready=T, y_T=4, yT_hi=4, yT_lo=4)
    if stop == "mix0":
        return dump()

    def embed(layer):
        tag = f"ple{layer}"
        ws = Stream(tag, 5, ring_raw, 2, ring_split)
        ws.shape[0] = (2, D)
        t5 = inside(ring_split + 4 * LIN * 4, 2 * RING * UNIT_B - 4 * LIN * 4)
        p_in = t5(f"p_in_{tag}", (P, T, PLE))
        p_hi = t5(f"p_hi_{tag}", (P, 2, SEQ), F32R)
        p_lo = t5(f"p_lo_{tag}", (P, 2, SEQ), F32R)
        emb = t5(f"emb_{tag}", (P, T, D))
        sg = t5(f"sg_{tag}", (P, 4, 512))
        row = ROW_PLE + KD * layer

        def load(e, free=None):
            for n in range(5):
                if free is not None:
                    free(n)
                if n == 0:
                    ws.load(e, 0, [(0, D, a["w_ple"][layer].rearrange("(k p) n -> p k n", p=P), 2)])
                else:
                    ws.load(e, n, [(0, 256, a["w_ple_gate"][layer][:, (n - 1) * 256:n * 256].rearrange("(k p) n -> p k n", p=P), KD)])

        def launch():
            with nc.Block() as block:
                @block.sync
                def _(e):
                    e.dma_start(p_in[:, :, :], a["p"][layer, 0].rearrange("(t p) n -> p t n", p=P)).then_inc(sig("p_loaded").sem, 16)
                    if layer == N_LAYERS - 1:
                        for b in range(4):
                            e.wait_ge(sig("embedded").sem, sig("embedded").at(2 * b + 2))
                            e.dma_start(out[0, :, b * 256:(b + 1) * 256].rearrange("(t p) n -> p t n", p=P),
                                        h[:, :, b * 256:(b + 1) * 256]).then_inc(sig("out").sem, 16)
                        e.wait_ge(sig("out").sem, sig("out").at(64))

                @block.scalar
                def _(e):
                    for t in range(T):
                        e.activation(y[:, t, :], h[:, t, :], ACT.Square, accum_out=stat[:, t:t + 1]).then_inc(sig("squares").sem, 1)
                    e.wait_ge(sig("squares").sem, sig("squares").at(T))
                    e.activation(stat[:, 2:4], stat[:, 0:2], ACT.Sqrt, bias=eps_col[:, :], scale=1.0 / D).then_inc(sig("rms").sem, 1)
                    ws.make_hi(e, 0)
                    e.wait_ge(sig("p_T").sem, sig("p_T").at(1))
                    e.copy(p_hi[:, :, :], ps[:, 4, :].rearrange("p (k s) -> p k s", k=2)).then_inc(sig("p_hi").sem, 1)
                    for b in range(4):
                        e.wait_ge(sig("y_T").sem, sig("y_T").at(b + 1))
                        for k in (2 * b, 2 * b + 1):
                            ins = e.activation(x_hi[:, k, :], ps[:, b, (k % 2) * SEQ:(k % 2 + 1) * SEQ], ACT.Copy,
                                               scale=gains[:, row + k:row + k + 1])
                        ins.then_inc(sig("yT_hi").sem, 1)
                    ws.make_hi(e, 1)
                    e.wait_ge(ws.used.sem, ws.used.at(1))
                    for t in range(T):
                        e.copy(emb[:, t, :].rearrange("p (n c) -> p n c", n=2), ps[:, 4 + 2 * t:6 + 2 * t, :]).then_inc(sig("emb").sem, 1)
                    for n in range(2, 5):
                        ws.make_hi(e, n)
                        e.wait_ge(ws.used.sem, ws.used.at(n))
                        e.activation(sg[:, n - 2, :], ps[:, n - 2, :], ACT.Sigmoid).then_inc(sig("gate_sig").sem, 1)
                    e.wait_ge(ws.used.sem, ws.used.at(5))
                    e.activation(sg[:, 3, :], ps[:, 3, :], ACT.Sigmoid).then_inc(sig("gate_sig").sem, 1)

                @block.vector
                def _(e):
                    link = linker(e, "dve_step")
                    e.wait_ge(sig("rms").sem, sig("rms").at(1))
                    link(e.reciprocal(stat[:, 4:6], stat[:, 2:4]))
                    for t in range(T):
                        e.tensor_scalar(y[:, t, :], h[:, t, :], stat[:, 4 + t:5 + t], None, ALU.mult).then_inc(sig("y_ready").sem, 1)
                    ws.make_lo(e, 0)
                    e.wait_ge(sig("p_hi").sem, sig("p_hi").at(1))
                    e.tensor_tensor(p_lo[:, :, :], ps[:, 4, :].rearrange("p (k s) -> p k s", k=2),
                                    p_hi[:, :, :].bitcast(F32), ALU.subtract).then_inc(sig("p_lo").sem, 1)
                    for b in range(4):
                        e.wait_ge(sig("yT_hi").sem, sig("yT_hi").at(b + 1))
                        for k in (2 * b, 2 * b + 1):
                            ins = e.scalar_tensor_tensor(out=x_lo[:, k, :], in0=ps[:, b, (k % 2) * SEQ:(k % 2 + 1) * SEQ],
                                                         scalar=gains[:, row + k:row + k + 1],
                                                         in1=x_hi[:, k, :].bitcast(F32), op0=ALU.mult, op1=ALU.subtract)
                        ins.then_inc(sig("yT_lo").sem, 1)
                    for n in range(1, 5):
                        ws.make_lo(e, n)
                    for b in range(4):
                        e.wait_ge(sig("gate_sig").sem, sig("gate_sig").at(b + 1))
                        e.wait_ge(sig("emb").sem, sig("emb").at(T))
                        c = slice(b * 256, (b + 1) * 256)
                        link(e.tensor_tensor(sg[:, b, :].rearrange("p (t n) -> p t n", t=T),
                                             sg[:, b, :].rearrange("p (t n) -> p t n", t=T), emb[:, :, c], ALU.mult))
                        e.tensor_tensor(h[:, :, c], h[:, :, c], sg[:, b, :].rearrange("p (t n) -> p t n", t=T),
                                        ALU.add).then_inc(sig("embedded").sem, 2)
                    link.end()

                @block.tensor
                def _(e):
                    e.wait_ge(sig("p_loaded").sem, sig("p_loaded").at(16))
                    for k in range(2):
                        for t in range(T):
                            ins = e.transpose(ps[:, 4, k * SEQ + t * P:k * SEQ + (t + 1) * P], p_in[:, t, k * P:(k + 1) * P],
                                              ident[:, :])
                    ins.then_inc(sig("p_T").sem, 1)
                    e.wait_ge(sig("y_ready").sem, sig("y_ready").at(T))
                    for b in range(4):
                        for k in (2 * b, 2 * b + 1):
                            for t in range(T):
                                o = (k % 2) * SEQ + t * P
                                ins = e.transpose(ps[:, b, o:o + P], y[:, t, k * P:(k + 1) * P], ident[:, :])
                        ins.then_inc(sig("y_T").sem, 1)
                    e.wait_ge(sig("p_lo").sem, sig("p_lo").at(1))
                    wh, wl = ws.parts(0, 2)
                    for t in range(T):
                        for n in range(2):
                            for k in range(2):
                                ws.half_ready(e, 0, k)
                                ins = three_passes(e, ps[:, 4 + 2 * t + n, :], p_hi[:, k, t * P:(t + 1) * P],
                                                   p_lo[:, k, t * P:(t + 1) * P], wh[:, k, n * 512:(n + 1) * 512],
                                                   wl[:, k, n * 512:(n + 1) * 512], k == 0, k == 1)
                    ins.then_inc(ws.used.sem, 1)
                    e.wait_ge(sig("yT_lo").sem, sig("yT_lo").at(4))
                    for n in range(1, 5):
                        ins = ws.by_token(e, n, n - 1)
            finished(squares=T, rms=1, y_ready=T, y_T=4, yT_hi=4, yT_lo=4, p_loaded=16, p_T=1, p_hi=1, p_lo=1, emb=T, gate_sig=4,
                     embedded=8)
            ws.over(5)
        return ws, load, launch

    Q = N_UNITS * QUARTERS
    CH = N_CH

    def swiglu(weights, tag, moe=None, load_next=None):
        tiles = T if moe is None else 1
        bU, bG, bZ = ([0, 1], [2, 3], [4, 6]) if moe is None else ([0], [1], [2])
        names = ["raw0", "raw1", "raw2", "split_hi", "split_lo", "unit_used", "silu", "hid", "hid_T", "hidT_hi",
                 "hidT_lo", "acc_out", "load_due"]
        if moe is not None:
            names += ["pick", "gathered", "x_hi", "x_lo", "back", "back_T", "backT", "scatter", "scattered", "acc_cleared"]
        sem = {k: sig(f"ffn_{k}") for k in names}
        first = sem
        second = None if moe is None else {k: sig(f"more_{k}") for k in names}

        hidden_after = {AT[("G", c)] + 2: c for c in range(CH)}
        transposed_after = {AT[("G", c)] + 3: c for c in range(CH)}

        def split_lo_at(i, n, q=QUARTERS - 1):
            return i * Q + n * QUARTERS + q + 1


        def unit_used_at(i, n):
            return i * N_UNITS + RING + n + 1

        def chunk_at(i, c, t=None):
            return i * (CH * tiles) + c * tiles + (tiles if t is None else t + 1)

        def slot(n):
            return n % RING

        def load_units(e, i, units):
            for n in units:
                kind, c = UNITS[n % N_UNITS]
                w = weights[kind] if moe is None else weights[kind][i + n // N_UNITS]
                if kind == "D":
                    src = w[c * FC:(c + 1) * FC, :].rearrange("(j p) n -> p j n", p=P)
                    dst = raw[slot(n)][:, :].rearrange("p (j n) -> p j n", j=4)
                else:
                    src = w[:, c * FC:(c + 1) * FC].rearrange("(k p) n -> p k n", p=P)
                    dst = raw[slot(n)][:, :].rearrange("p (k n) -> p k n", k=KD)
                if n >= RING:
                    e.wait_ge(sem["split_lo"].sem, sem["split_lo"].at(split_lo_at(i, n - RING)))
                    e.sem_inc(sem["load_due"].sem, 1)
                e.dma_start(dst, src).then_inc(sem[f"raw{slot(n)}"].sem, 16)

        def split_hi(e, i, n):
            e.wait_ge(sem[f"raw{slot(n)}"].sem, sem[f"raw{slot(n)}"].at(i * (16 * N_UNITS // RING) + 16 * (n // RING + 1)))
            e.wait_ge(sem["unit_used"].sem, sem["unit_used"].at(unit_used_at(i, n - RING)))
            for q in range(QUARTERS):
                c = slice(q * 1024, (q + 1) * 1024)
                e.copy(w_hi[slot(n)][:, c], raw[slot(n)][:, c]).then_inc(sem["split_hi"].sem, 1)

        def split_lo(e, i, n):
            for q in range(QUARTERS):
                c = slice(q * 1024, (q + 1) * 1024)
                e.wait_ge(sem["split_hi"].sem, sem["split_hi"].at(i * Q + n * QUARTERS + q + 1))
                e.tensor_tensor(w_lo[slot(n)][:, c], raw[slot(n)][:, c], w_hi[slot(n)][:, c].bitcast(F32),
                                ALU.subtract).then_inc(sem["split_lo"].sem, 1)

        def unit_product(e, i, n):
            kind, c = UNITS[n]
            if kind == "U" and c > 0:
                e.wait_ge(sem["hid"].sem, sem["hid"].at(chunk_at(i, c - 1)))
            if kind == "G" and c > 0:
                e.wait_ge(sem["hidT_lo"].sem, sem["hidT_lo"].at(chunk_at(i, c - 1)))
            if kind == "D":
                e.wait_ge(sem["hidT_lo"].sem, sem["hidT_lo"].at(chunk_at(i, c)))
                if c == 0 and moe is not None:
                    e.wait_ge(sem["acc_out"].sem, sem["acc_out"].at(i + 1))
            wh, wl = w_hi[slot(n)], w_lo[slot(n)]
            for t in range(tiles):
                for q in range(QUARTERS):
                    if t == 0:
                        e.wait_ge(sem["split_lo"].sem, sem["split_lo"].at(split_lo_at(i, n, q)))
                    for m in range(2):
                        cols_ = slice((2 * q + m) * 512, (2 * q + m + 1) * 512)
                        if kind == "D":
                            ins = three_passes(e, ps[:, bZ[t] + m, :], hidT_hi[t][:, q, :], hidT_lo[t][:, q, :],
                                               wh[:, cols_], wl[:, cols_], c == 0 and q == 0, c == CH - 1 and q == QUARTERS - 1)
                        else:
                            k = 2 * q + m
                            ins = three_passes(e, ps[:, (bU if kind == "U" else bG)[t], :],
                                               x_hi[:, k, t * P:(t + 1) * P], x_lo[:, k, t * P:(t + 1) * P],
                                               wh[:, cols_], wl[:, cols_], k == 0, k == KD - 1)
            ins.then_inc(sem["unit_used"].sem, 1)

        def transpose_hidden(e, i, c):
            for t in range(tiles):
                e.wait_ge(sem["hid"].sem, sem["hid"].at(chunk_at(i, c, t)))
                for j in range(4):
                    ins = e.transpose(ps[:, bG[t], j * P:(j + 1) * P], hid[t][:, j * P:(j + 1) * P], ident[:, :])
                ins.then_inc(sem["hid_T"].sem, 1)

        def silu(e, i, c):
            e.wait_ge(sem["unit_used"].sem, sem["unit_used"].at(unit_used_at(i, AT[("G", c)])))
            for t in range(tiles):
                e.activation(hid[t][:, :], ps[:, bG[t], :], ACT.Silu).then_inc(sem["silu"].sem, 1)

        def hidden(e, i, c):
            for t in range(tiles):
                e.wait_ge(sem["silu"].sem, sem["silu"].at(chunk_at(i, c, t)))
                e.tensor_tensor(hid[t][:, :], hid[t][:, :], ps[:, bU[t], :], ALU.mult).then_inc(sem["hid"].sem, 1)

        def hiddenT_hi(e, i, c):
            for t in range(tiles):
                e.wait_ge(sem["hid_T"].sem, sem["hid_T"].at(chunk_at(i, c, t)))
                e.copy(hidT_hi[t][:, :, :], ps[:, bG[t], :].rearrange("p (j s) -> p j s", j=4)).then_inc(sem["hidT_hi"].sem, 1)

        def hiddenT_lo(e, i, c):
            for t in range(tiles):
                e.wait_ge(sem["hidT_hi"].sem, sem["hidT_hi"].at(chunk_at(i, c, t)))
                e.tensor_tensor(hidT_lo[t][:, :, :], ps[:, bG[t], :].rearrange("p (j s) -> p j s", j=4),
                                hidT_hi[t][:, :, :].bitcast(F32), ALU.subtract).then_inc(sem["hidT_lo"].sem, 1)

        def pick_for(e, col):
            for t in range(T):
                e.tensor_scalar(pick[:, t, :], iota[:, :], rank[:, t, col], None, ALU.is_equal).then_inc(sem["pick"].sem, 1)

        def back_for(e, col):
            for t in range(T):
                e.tensor_scalar(back[:, t, :], iota[:, :], rank[:, t, col], gate[:, t, col], ALU.is_equal,
                                ALU.mult).then_inc(sem["back"].sem, 1)

        def transpose_back(e, i):
            e.wait_ge(sem["back"].sem, sem["back"].at((i + 1) * T))
            for t in range(T):
                ins = e.transpose(ps[:, 6, t * P:(t + 1) * P], back[:, t, :], ident[:, :])
            ins.then_inc(sem["back_T"].sem, 1)

        def leave(e, i):
            e.wait_ge(sem["unit_used"].sem, sem["unit_used"].at(unit_used_at(i, -1)))
            e.copy(slot_out[:, :].rearrange("p (n c) -> p n c", n=2), ps[:, 2:4, :]).then_inc(sem["acc_out"].sem, 1)
            e.wait_ge(sem["back_T"].sem, sem["back_T"].at(i + 1))
            e.copy(backT[:, :], ps[:, 6, 0:SEQ]).then_inc(sem["backT"].sem, 1)

        def scatter(e, i):
            e.wait_ge(sem["acc_out"].sem, sem["acc_out"].at(i + 1))
            e.wait_ge(sem["backT"].sem, sem["backT"].at(i + 1))
            for t in range(T):
                for n in range(2):
                    ins = e.matmul(ps[:, 4 + 2 * t + n, :], backT[:, t * P:(t + 1) * P], slot_out[:, n * 512:(n + 1) * 512],
                                   start=True, stop=True)
            ins.then_inc(sem["scatter"].sem, 1)

        def add_scattered(e, i):
            e.wait_ge(sem["scatter"].sem, sem["scatter"].at(i + 1))
            for t in range(T):
                e.tensor_tensor(h[:, t, :].rearrange("p (n c) -> p n c", n=2), h[:, t, :].rearrange("p (n c) -> p n c", n=2),
                                ps[:, 4 + 2 * t:6 + 2 * t, :], ALU.add).then_inc(sem["scattered"].sem, 1)

        def gather(e, i):
            e.wait_ge(sem["pick"].sem, sem["pick"].at((i + 1) * T))
            for k in range(KD):
                for t in range(T):
                    ins = e.matmul(ps[:, 4 + k // 4, (k % 4) * P:(k % 4 + 1) * P], y[:, t, k * P:(k + 1) * P], pick[:, t, :],
                                   start=(t == 0), stop=(t == T - 1))
            ins.then_inc(sem["gathered"].sem, 1)

        def gathered_hi(e, i):
            e.wait_ge(sem["gathered"].sem, sem["gathered"].at(i + 1))
            for b in range(2):
                e.copy(x_hi[:, 4 * b:4 * b + 4, 0:P], ps[:, 4 + b, :].rearrange("p (k s) -> p k s", k=4)).then_inc(sem["x_hi"].sem, 1)

        def gathered_lo(e, i):
            for b in range(2):
                e.wait_ge(sem["x_hi"].sem, sem["x_hi"].at(2 * i + b + 1))
                e.tensor_tensor(x_lo[:, 4 * b:4 * b + 4, 0:P], ps[:, 4 + b, :].rearrange("p (k s) -> p k s", k=4),
                                x_hi[:, 4 * b:4 * b + 4, 0:P].bitcast(F32), ALU.subtract).then_inc(sem["x_lo"].sem, 1)

        def run(e, turn):
            if moe is not None:
                with e.Fori(0, N_EXP - 1) as i:
                    turn(i, False)
            turn(0 if moe is None else N_EXP - 1, True)

        def prefetch(e):
            load_units(e, 0, range(RING))

        def sync_pass(e):
            if sem is not first:
                prefetch(e)
            run(e, lambda i, last: load_units(e, i, range(RING, N_UNITS + (0 if last else RING))))
            if sem is not first:
                e.wait_ge(sem["split_lo"].sem, sem["split_lo"].at(split_lo_at(N_EXP - 1, N_UNITS - 1)))

        def scalar_pass(e):
            def turn(i, last):
                for n in range(1, N_UNITS + 1):
                    if n < N_UNITS or not last:
                        split_hi(e, i, n)
                    if n == 1 and moe is not None:
                        leave(e, i)
                    if n in hidden_after:
                        silu(e, i, hidden_after[n])
                    if n in transposed_after:
                        hiddenT_hi(e, i, transposed_after[n])
                if not last:
                    gathered_hi(e, i + 1)
            split_hi(e, 0, 0)
            if moe is not None:
                e.wait_ge(sem["acc_cleared"].sem, sem["acc_cleared"].at(1))
                gathered_hi(e, 0)
            run(e, turn)
            if moe is not None:
                leave(e, N_EXP)

        def vector_pass(e):
            def turn(i, last):
                if moe is not None:
                    back_for(e, bass.ds(i, 1))
                for n in range(1, N_UNITS + 1):
                    if n < N_UNITS or not last:
                        split_lo(e, i, n)
                    if n in hidden_after:
                        hidden(e, i, hidden_after[n])
                        if n == AT[("G", 0)] + 2 and moe is not None:
                            add_scattered(e, i)
                            if not last:
                                pick_for(e, bass.ds(i + 2, 1))
                    if n in transposed_after:
                        hiddenT_lo(e, i, transposed_after[n])
                if not last:
                    gathered_lo(e, i + 1)
            if moe is not None:
                pick_for(e, slice(1, 2))
                e.memset(ps[:, 2:4, :], 0.0).then_inc(sem["acc_cleared"].sem, 1)
            split_lo(e, 0, 0)
            if moe is not None:
                gathered_lo(e, 0)
            run(e, turn)
            if moe is None:
                e.wait_ge(sem["unit_used"].sem, sem["unit_used"].at(unit_used_at(0, N_UNITS - 1)))
                for t in range(T):
                    e.tensor_tensor(h[:, t, :].rearrange("p (n c) -> p n c", n=2), h[:, t, :].rearrange("p (n c) -> p n c", n=2),
                                    ps[:, bZ[t]:bZ[t] + 2, :], ALU.add)
            else:
                back_for(e, slice(N_EXP, N_EXP + 1))
                add_scattered(e, N_EXP)

        def tensor_pass(e):
            def turn(i, last):
                if moe is not None:
                    transpose_back(e, i)
                    e.wait_ge(sem["x_lo"].sem, sem["x_lo"].at(2 * i + 2))
                for n, (kind, c) in enumerate(UNITS):
                    if n == N_UNITS - 1 and not last:
                        e.wait_ge(sem["scattered"].sem, sem["scattered"].at((i + 1) * T))
                        gather(e, i + 1)
                    unit_product(e, i, n)
                    if (kind, c) == ("G", 0) and moe is not None:
                        scatter(e, i)
                    if (kind, c) == ("U", 1):
                        transpose_hidden(e, i, 0)
                    if kind == "D" and c < CH - 1:
                        transpose_hidden(e, i, c + 1)
            e.nop().then_inc(sem["unit_used"].sem, RING)
            if moe is not None:
                gather(e, 0)
            run(e, turn)
            if moe is not None:
                transpose_back(e, N_EXP)
                scatter(e, N_EXP)

        def passes(e, one_pass, between=None):
            nonlocal sem
            sem = first
            one_pass(e)
            if moe is None:
                return
            crowded = e.value_load(over[0:1, 0:1], min_val=0, max_val=1)
            with e.If(crowded > 0):
                e.wait_ge(first["scattered"].sem, first["scattered"].at((N_EXP + 1) * T))
                if between is not None:
                    between()
                sem = second
                one_pass(e)
            sem = first

        def launch():
            with nc.Block() as block:
                @block.sync
                def _(e):
                    passes(e, sync_pass)
                    load_next(e, lambda n: e.wait_ge(first["split_lo"].sem, first["split_lo"].at(split_lo_at(0 if moe is None else N_EXP - 1, N_UNITS - RING + n // 2))))

                @block.scalar
                def _(e):
                    passes(e, scalar_pass)

                @block.vector
                def _(e):
                    def next_slots():
                        e.tensor_scalar(rank[:, :, :], rank[:, :, :], -float(P), None, ALU.add).then_inc(first["acc_cleared"].sem, 1)
                        e.wait_ge(first["acc_cleared"].sem, first["acc_cleared"].at(2))
                    passes(e, vector_pass, next_slots)

                @block.tensor
                def _(e):
                    passes(e, tensor_pass)
            if moe is None:
                finished(ffn_raw0=16 * N_UNITS // RING, ffn_raw1=16 * N_UNITS // RING, ffn_raw2=16 * N_UNITS // RING,
                         ffn_split_hi=Q, ffn_split_lo=Q, ffn_unit_used=N_UNITS + RING, ffn_silu=CH * T, ffn_hid=CH * T,
                         ffn_hid_T=CH * T, ffn_hidT_hi=CH * T, ffn_hidT_lo=CH * T, ffn_load_due=N_UNITS - RING)

        return prefetch, launch

    _, load_embed, launch_embed = embed(0)
    prefetch, dense_swiglu = swiglu({"U": a["w_up_d"][0], "G": a["w_gate_d"][0], "D": a["w_down_d"][0]}, "dense",
                                    load_next=load_embed)
    norm_T(ROW_FFN, True, load=prefetch)
    dense_swiglu()
    if stop == "ffn0":
        return dump()

    launch_embed()
    if stop == "ple0":
        return dump()

    PAD = max(WINDOWS)
    t6 = inside(arena, arena_n)
    w_pool = t6("w_pool", (P, 4, 2, 256))
    scale_b = t6("scale_b", (P, D))
    inv_pos = t6("inv_pos", (P, 4, SEQ))
    win = [t6(f"win{n}", (P, KD, PAD + SEQ)) for n in range(3)]
    pooled = t6("pooled", (P, KD, SEQ))

    def load_pool(e):
        s = sig("pool_loaded")
        for g in range(4):
            e.dma_start(w_pool[:, g, :, :], a["w_pool"][0, g].rearrange("(k p) n -> p k n", p=P)).then_inc(s.sem, 16)
        e.dma_start(scale_b[:, :], a["scale_pool"].partition_broadcast(P)[:, 0, :]).then_inc(s.sem, 16)
        e.dma_start(inv_pos[:, :, :], a["c_invpos"].partition_broadcast(P)).then_inc(s.sem, 16)

    norm_T(ROW_MIX + KD, False, yT=yT, load=load_pool)
    with nc.Block() as block:
        @block.vector
        def _(e):
            link = linker(e, "dve_step")
            for w in win:
                link(e.memset(w[:, :, 0:PAD], 0.0))
            link(e.tensor_copy(win[0][:, :, PAD:], yT[:, :, :]))
            e.wait_ge(sig("pool_loaded").sem, sig("pool_loaded").at(16 * 6))
            src = 0
            for g in range(4):
                step, dst = 1 << g, 1 + g % 2
                link(e.tensor_tensor(win[dst][:, 2 * g:, PAD:], win[src][:, 2 * g:, PAD:],
                                     win[src][:, 2 * g:, PAD - step:PAD + SEQ - step], ALU.add))
                link(e.tensor_tensor(pooled[:, 2 * g:2 * g + 2, :], win[dst][:, 2 * g:2 * g + 2, PAD:],
                                     inv_pos[:, g, :].unsqueeze(1).to_broadcast([P, 2, SEQ]), ALU.mult))
                e.tensor_tensor(pooled[:, 2 * g:2 * g + 2, :], pooled[:, 2 * g:2 * g + 2, :],
                                yT[:, 2 * g:2 * g + 2, :], ALU.subtract).then_inc(sig("pooled").sem, 1)
                src = dst
            for b in range(4):
                c = slice((b % 2) * 512, (b % 2 + 1) * 512)
                e.wait_ge(sig("pool_mm").sem, sig("pool_mm").at(b + 1))
                link(e.tensor_tensor(y[:, b // 2, c], ps[:, 4 + b, :], scale_b[:, c], ALU.mult))
                e.tensor_tensor(h[:, b // 2, c], h[:, b // 2, c], y[:, b // 2, c], ALU.add)
            link.end()

        @block.tensor
        def _(e):
            for t in range(T):
                for g in range(4):
                    e.wait_ge(sig("pooled").sem, sig("pooled").at(g + 1))
                    for k in range(2):
                        ins = e.matmul(ps[:, 4 + 2 * t + g // 2, (g % 2) * 256:(g % 2 + 1) * 256],
                                       pooled[:, 2 * g + k, t * P:(t + 1) * P], w_pool[:, g, k, :],
                                       start=(k == 0), stop=(k == 1))
                    if g % 2:
                        ins.then_inc(sig("pool_mm").sem, 1)
    if stop == "mix1":
        return dump()

    t7 = inside(z_free_at, 4096)
    pick = t7("pick", (P, T, P))
    back = t7("back", (P, T, P))
    backT = t7("backT", (P, SEQ))
    rank = t7("rank", (P, T, N_EXP + 2))
    gate = t7("gate", (P, T, N_EXP + 2))
    iota = t7("iota", (P, P))
    t8 = inside(ring_split, 2 * RING * UNIT_B)
    w_r = t8("w_r", (P, KD, N_EXP))
    b_r = t8("b_r", (P, N_EXP))
    g_b = t8("g_b", (P, D))
    logit = t8("logit", (P, T, N_EXP))
    top_v = t8("top_v", (P, T, 8))
    top_i = t8("top_i", (P, T, 8), U32)
    top_f = t8("top_f", (P, T, 8))
    sc = t8("sc", (P, T, 8))
    oh = t8("oh", (P, T, 2, N_EXP))
    chosen = t8("chosen", (P, T, N_EXP))
    most = t8("most", (P, 1))
    over = place("over", (P, 1), I32, offset=over_at)

    w_moe = {"U": a["w_up_m"][0], "G": a["w_gate_m"][0], "D": a["w_down_m"][0]}
    moe_small = (pick, back, backT, rank, gate, iota, over)
    _, load_embed, launch_embed = embed(1)
    prefetch_moe, moe_swiglu = swiglu(w_moe, "moe", moe_small, load_next=load_embed)

    def load_router(e):
        s = sig("router_loaded")
        e.dma_start(w_r[:, :, :], a["w_router"][0].rearrange("(k p) n -> p k n", p=P)).then_inc(s.sem, 16)
        e.dma_start(b_r[:, :], a["b_router"].partition_broadcast(P)[:, 0, :]).then_inc(s.sem, 16)
        e.dma_start(g_b[:, :], a["norm_ffn"][1:2].partition_broadcast(P)[:, 0, :]).then_inc(s.sem, 16)
        e.dma_start(iota[:, :], a["c_iota"].partition_broadcast(P)[:, 0, :]).then_inc(s.sem, 16)
        prefetch_moe(e)

    norm_T(ROW_FFN + KD, False, yT=yT, load=load_router)
    with nc.Block() as block:
        @block.tensor
        def _(e):
            e.wait_ge(sig("router_loaded").sem, sig("router_loaded").at(64))
            for t in range(T):
                for k in range(KD):
                    ins = e.matmul(ps[:, t, 0:N_EXP], yT[:, k, t * P:(t + 1) * P], w_r[:, k, :],
                                   start=(k == 0), stop=(k == KD - 1))
                ins.then_inc(sig("logit").sem, 1)
            e.wait_ge(sig("chosen").sem, sig("chosen").at(T))
            e.matmul(ps[:, 2, 0:N_EXP], before[:, :], chosen[:, 0, :], start=True, stop=True)
            e.matmul(ps[:, 3, 0:N_EXP], ones[:, :], chosen[:, 0, :], start=True, stop=False)
            e.matmul(ps[:, 3, 0:N_EXP], before[:, :], chosen[:, 1, :], start=False, stop=True)
            e.matmul(ps[:, 4, 0:N_EXP], ones[:, :], chosen[:, 0, :], start=True, stop=False)
            e.matmul(ps[:, 4, 0:N_EXP], ones[:, :], chosen[:, 1, :], start=False, stop=True).then_inc(sig("ranks").sem, 1)

        @block.scalar
        def _(e):
            e.wait_ge(sig("gap").sem, sig("gap").at(1))
            e.activation(sc[:, :, 1], sc[:, :, 0], ACT.Exp).then_inc(sig("gap_exp").sem, 1)

        @block.vector
        def _(e):
            link = linker(e, "dve_step")
            e.wait_ge(sig("router_loaded").sem, sig("router_loaded").at(64))
            link(e.memset(rank[:, :, :], -1.0))
            link(e.memset(gate[:, :, :], 0.0))
            for t in range(T):
                e.wait_ge(sig("logit").sem, sig("logit").at(t + 1))
                link(e.tensor_tensor(logit[:, t, :], ps[:, t, 0:N_EXP], b_r[:, :], ALU.add))
                link(e.max(top_v[:, t, :], logit[:, t, :]))
                link(e.max_index(top_i[:, t, :], top_v[:, t, :], logit[:, t, :]))
            link(e.tensor_copy(top_f[:, :, :], top_i[:, :, :]))
            e.tensor_tensor(sc[:, :, 0], top_v[:, :, 1], top_v[:, :, 0], ALU.subtract).then_inc(sig("gap").sem, 1)
            for t in range(T):
                for j in range(2):
                    link(e.tensor_scalar(oh[:, t, j, :], iota[:, 0:N_EXP], top_f[:, t, j:j + 1], None, ALU.is_equal))
                e.tensor_tensor(chosen[:, t, :], oh[:, t, 0, :], oh[:, t, 1, :], ALU.add).then_inc(sig("chosen").sem, 1)
            e.wait_ge(sig("gap_exp").sem, sig("gap_exp").at(1))
            link(e.tensor_scalar(sc[:, :, 2], sc[:, :, 1], 1.0, None, ALU.add))
            link(e.reciprocal(sc[:, :, 3], sc[:, :, 2]))
            link(e.tensor_tensor(sc[:, :, 4], sc[:, :, 3], sc[:, :, 1], ALU.mult))
            e.wait_ge(sig("ranks").sem, sig("ranks").at(1))
            for t in range(T):
                e1 = slice(1, N_EXP + 1)
                link(e.tensor_scalar(gate[:, t, e1], oh[:, t, 0, :], sc[:, t, 3:4], None, ALU.mult))
                link(e.scalar_tensor_tensor(out=gate[:, t, e1], in0=oh[:, t, 1, :], scalar=sc[:, t, 4:5], in1=gate[:, t, e1],
                                            op0=ALU.mult, op1=ALU.add))
                link(e.scalar_tensor_tensor(out=rank[:, t, e1], in0=ps[:, 2 + t, 0:N_EXP], scalar=1.0, in1=chosen[:, t, :],
                                            op0=ALU.add, op1=ALU.mult))
                link(e.tensor_scalar(rank[:, t, e1], rank[:, t, e1], -1.0, None, ALU.add))
            link(e.tensor_reduce(most[:, :], ps[:, 4, 0:N_EXP], AX_X, ALU.max))
            link(e.tensor_scalar(over[:, :], most[:, :], float(P), None, ALU.is_gt))
            for t in range(T):
                e.tensor_tensor(y[:, t, :], y[:, t, :], g_b[:, :], ALU.mult)
            link.end()

    moe_swiglu()
    if stop == "ffn1":
        return dump()
    launch_embed()

_INS = ['x', 'p', 'norm_mix', 'norm_ffn', 'w_in_e', 'b_gate_e', 'conv_a', 'norm_h_a', 'norm_q_b', 'norm_k_b',
        'norm_kv_b', 'w_uk_b', 'w_uv_b', 'w_out_e', 'rel_bias', 'w_pool', 'scale_pool', 'w_gate_d', 'w_up_d',
        'w_down_d', 'w_router', 'b_router', 'w_gate_m', 'w_up_m', 'w_down_m', 'w_ple', 'w_ple_gate', 'norm_ple']


def kernel(**inputs):
    import numpy as _np
    import concourse.bacc as _bacc
    from concourse import mybir as _mybir
    from concourse.bass_utils import run_bass_kernel_spmd as _run

    nc = _bacc.Bacc("TRN2", target_bir_lowering=False, num_devices=1)
    arrays, args = {}, {}
    given = {name: _np.ascontiguousarray(inputs[name]) for name in _INS}
    given.update(constants())
    for name, v in given.items():
        arrays[f"in_{name}"] = v
        args[name] = nc.dram_tensor(f"in_{name}", v.shape, _mybir.dt.from_np(v.dtype), kind="ExternalInput").ap()
    out = nc.dram_tensor("out_0", (1, SEQ, D), _mybir.dt.float32, kind="ExternalOutput").ap()
    build(nc, args, out)
    r = _run(nc, [arrays], core_ids=[0])
    return r.results[0]["out_0"]
```

```python
import math

import numpy as np
import concourse.bass as bass
from concourse import mybir

F32 = mybir.dt.float32
F32R = mybir.dt.float32r
I32 = mybir.dt.int32
U32 = mybir.dt.uint32
ALU = mybir.AluOpType
ACT = mybir.ActivationFunctionType
AX_X = mybir.AxisListType.X

P = 128
D = 1024
KD = D // P
SEQ = 256
T = SEQ // P
EPS = 1e-6
A_HEADS, A_DK = 4, 128
B_HEADS, B_DH, B_LATENT = 8, 64, 128
TOPK = 64
BUCKETS, MAX_DIST = 32, 128
OFF_AQ, OFF_AV, OFF_AO, OFF_AI, OFF_AF = 0, 1024, 1536, 2048, 2052
OFF_BQ, OFF_BC, OFF_QI, OFF_KI, OFF_WI, D_IN = 2056, 2568, 2696, 3208, 3272, 3280
CONV = 4
WINDOWS = (2, 4, 8, 16)
F_FF = 3584
N_EXP = 8
N_LAYERS = 2
PLE = 256
FC = 512
N_CH = F_FF // FC
NEG = -1e30
ACAUSAL, TAKEN = -3.0e38, -3.3e38
BIAS_W = 384

UNITS = [("U", 0), ("G", 0)]
for _c in range(1, N_CH):
    UNITS += [("U", _c), ("G", _c), ("D", _c - 1)]
UNITS.append(("D", N_CH - 1))
N_UNITS = len(UNITS)
AT = {u: n for n, u in enumerate(UNITS)}
RING = 3
QUARTERS = 4
assert N_UNITS % RING == 0


class Signal:

    def __init__(self, nc, name):
        self.sem, self.base = nc.alloc_semaphore(name), 0

    def at(self, n):
        return n + self.base

    def past(self, n):
        self.base += n


def constants():
    d = np.arange(SEQ)
    exact = BUCKETS // 2
    log = np.log(np.maximum(d, 1).astype(np.float32) / np.float32(exact)) / np.float32(math.log(MAX_DIST / exact))
    large = np.minimum(exact + (log * (BUCKETS - exact)).astype(np.int32), BUCKETS - 1)
    bucket = np.where(d < exact, d, large)
    bias_onehot = np.zeros((BUCKETS, BIAS_W), np.float32)
    for j in range(SEQ):
        bias_onehot[bucket[SEQ - 1 - j], j] = 1.0
    select = np.zeros((A_HEADS, A_HEADS * P), np.float32)
    for hd in range(A_HEADS):
        select[hd, hd * P:(hd + 1) * P] = 1.0
    halves = np.zeros((P, 2), np.float32)
    halves[:B_DH, 0] = 1.0
    halves[B_DH:, 1] = 1.0
    pos = np.arange(1, SEQ + 1, dtype=np.float32)
    inv = np.stack([np.float32(1.0) / np.minimum(pos, np.float32(w)) for w in WINDOWS])
    return {
        "c_ident": np.eye(P, dtype=np.float32),
        "c_before": np.triu(np.ones((P, P), np.float32), 1),
        "c_bias": bias_onehot,
        "c_select": select,
        "c_halves": halves,
        "c_invpos": inv.astype(np.float32),
        "c_iota": np.arange(P, dtype=np.float32)[None, :],
    }


def build(nc, a, out):
    limit = nc.sbuf_usable_end
    bottom = -(-nc.sbuf_base // 64) * 64
    at = [bottom]

    def place(name, shape, dtype=F32, offset=None):
        n = int(np.prod(shape[1:])) * 4
        if offset is None:
            offset, at[0] = at[0], at[0] + -(-n // 64) * 64
        assert offset % 4 == 0 and offset + n <= limit, (name, offset, n, limit)
        return nc.alloc_sbuf_tensor_at(name, tuple(shape), dtype, offset=offset)

    def region(size):
        o = at[0]
        at[0] += size
        assert at[0] <= limit, (at[0], limit)
        return o

    def inside(base, size):
        o = [base]

        def put(name, shape, dtype=F32):
            n = -(-int(np.prod(shape[1:])) * 4 // 64) * 64
            t = place(name, shape, dtype, offset=o[0])
            o[0] += n
            assert o[0] <= base + size, (name, o[0] - base, size)
            return t
        put.next = lambda: o[0]
        return put

    h = place("h", (P, T, D))
    ident = place("ident", (P, P))
    before = place("before", (P, P))
    ones = place("ones", (P, P))
    gains = place("gains", (P, P))
    stat = place("stat", (P, 64))
    bias_i = place("bias_i", (A_HEADS, 1))
    bias_f = place("bias_f", (A_HEADS, 1))
    eps_col = place("eps_col", (P, 1))
    one_col = place("one_col", (P, 1))
    over_at = region(64)
    y = place("y", (P, T, D))

    X_B, HID_B = 2 * KD * SEQ * 4, 3 * T * FC * 4
    FFN_B = X_B + HID_B + 2 * D * 4
    ffn_small = region(FFN_B)
    put = inside(ffn_small, FFN_B)
    x_hi = put("x_hi", (P, KD, SEQ), F32R)
    x_lo = put("x_lo", (P, KD, SEQ), F32R)
    hid = [put(f"hid{t}", (P, FC)) for t in range(T)]
    hidT_hi = [put(f"hidT_hi{t}", (P, 4, P), F32R) for t in range(T)]
    hidT_lo = [put(f"hidT_lo{t}", (P, 4, P), F32R) for t in range(T)]
    slot_out = put("slot_out", (P, D))
    experts_at = ffn_small + X_B + HID_B + D * 4

    UNIT = D * FC // P
    UNIT_B = UNIT * 4
    ring_raw = region(RING * UNIT_B)
    ring_split = region(2 * RING * UNIT_B)
    raw = [place(f"raw{s}", (P, UNIT), offset=ring_raw + s * UNIT_B) for s in range(RING)]
    w_hi = [place(f"w_hi{s}", (P, UNIT), F32R, offset=ring_split + 2 * s * UNIT_B) for s in range(RING)]
    w_lo = [place(f"w_lo{s}", (P, UNIT), F32R, offset=ring_split + (2 * s + 1) * UNIT_B) for s in range(RING)]
    arena, arena_n = ring_raw, 3 * RING * UNIT_B

    ps = nc.alloc_psum_tensor("ps", (P, 8, 512), F32)

    signals = {}

    def sig(name):
        if name not in signals:
            signals[name] = Signal(nc, name)
        return signals[name]

    def finished(**counts):
        for name, n in counts.items():
            sig(name).past(n)

    def linker(eng, name):
        s = sig(name)
        count = [0]

        def link(ins):
            count[0] += 1
            ins.then_inc(s.sem, 1)
            eng.wait_ge(s.sem, s.at(count[0]))

        link.end = lambda: s.past(count[0])
        return link

    ROW_MIX, ROW_FFN, ROW_PLE, ROW_CONV, ROW_GQ, ROW_GK = 0, 16, 32, 48, 80, 81
    N_ROWS = 82

    LIN = 2048
    MIX_RAW, MIX_SPLIT = 3, 3
    mix_at = arena + (MIX_RAW + 2 * MIX_SPLIT) * LIN * 4
    t1 = inside(mix_at, arena + arena_n - mix_at)
    qk = t1("qk", (P, 8, SEQ))
    v_ones = t1("v_ones", (P, T, A_HEADS, 129))
    ao = t1("ao", (P, T, 512))
    qi = t1("qi", (P, 4, SEQ))
    bqT = t1("bqT", (P, 4, SEQ))
    NARROW = B_LATENT + B_DH + 8 + 2 * A_HEADS
    narrow = t1("narrow", (P, T, NARROW))
    bc, ki, wi = narrow[:, :, 0:B_LATENT], narrow[:, :, B_LATENT:B_LATENT + B_DH], narrow[:, :, B_LATENT + B_DH:NARROW - 2 * A_HEADS]
    ki_twice = t1("ki_twice", (P, T, 2, B_DH))
    ki2 = t1("ki2", (P, SEQ))
    gate_i = t1("gate_i", (A_HEADS, SEQ))
    gate_f = t1("gate_f", (A_HEADS, SEQ))
    w_uk = t1("w_uk", (P, B_DH))
    w_uv = t1("w_uv", (P, B_HEADS, B_DH))
    sel_h = t1("sel_h", (A_HEADS, A_HEADS * P))
    halves = t1("halves", (P, 2))
    g1 = t1("g1", (A_HEADS, SEQ))
    g2 = t1("g2", (A_HEADS, SEQ))
    g3 = t1("g3", (A_HEADS, SEQ))
    g4 = t1("g4", (A_HEADS, SEQ))
    cols = t1("cols", (P, T, 8))
    WT_AT = t1.next()
    wT = t1("wT", (P, A_HEADS, 384))
    small = t1("small", (P, 96))
    msmall = t1("msmall", (P, 48))
    kb2 = t1("kb2", (P, T, P))
    kbT = t1("kbT", (P, SEQ))
    lat = t1("lat", (P, T, B_LATENT))
    latT = t1("latT", (P, SEQ))
    vu = t1("vu", (P, T, 512))
    isc = t1("isc", (P, T, SEQ))
    top8 = t1("top8", (P, 8))
    most_mask = t1("most_mask", (P, P))
    neg_mask = t1("neg_mask", (P, P))
    rel8 = t1("rel8", (BUCKETS, B_HEADS))
    bias_rows = place("bias_rows", (P, B_HEADS, BIAS_W), offset=t1.next())
    big = t1("big", (P, B_HEADS, SEQ))
    probT = t1("probT", (P, 16, P))
    rel_wide = place("rel_wide", (BUCKETS, B_HEADS, P), offset=WT_AT)
    bias_oh = place("bias_oh", (BUCKETS, BIAS_W), offset=WT_AT + B_HEADS * P * 4)
    t2 = inside(ffn_small + X_B, FFN_B - X_B)
    conv_in = t2("conv_in", (P, 8, CONV - 1 + SEQ))
    bias_toe = t2("bias_toe", (P, B_HEADS, SEQ))
    params = t2("params", (P, P))
    gh_b = t2("gh_b", (P, 512))
    gkv_b = t2("gkv_b", (P, B_LATENT))
    yT = place("yT", (P, KD, SEQ), offset=ffn_small)
    hcat = y
    scratch_b = nc.dram_tensor("bias_scratch", [P * B_HEADS * BIAS_W], F32)
    w_in_v = a["w_in_e"][0].rearrange("(k p) n -> p k n", p=P)
    w_out_v = a["w_out_e"][0].rearrange("(k p) n -> p k n", p=P)

    HALVES = 2

    class Stream:

        def __init__(self, tag, n_raw, raw_at, n_split, split_at):
            self.n_raw, self.n_split = n_raw, n_split
            b = LIN * 4
            self.raw = [place(f"{tag}_raw{s}", (P, LIN), offset=raw_at + s * b) for s in range(n_raw)]
            self.hi = [place(f"{tag}_hi{s}", (P, LIN), F32R, offset=split_at + 2 * s * b) for s in range(n_split)]
            self.lo = [place(f"{tag}_lo{s}", (P, LIN), F32R, offset=split_at + (2 * s + 1) * b) for s in range(n_split)]
            self.landed = [sig(f"w_landed{s}") for s in range(n_raw)]
            self.hi_made, self.lo_made, self.used = sig("w_hi_made"), sig("w_lo_made"), sig("w_used")
            self.dmas = {}
            self.shape = {}

        def load(self, e, n, parts):
            if n >= self.n_raw:
                e.wait_ge(self.lo_made.sem, self.lo_made.at((n - self.n_raw + 1) * HALVES))
            for lo, hi, src, k in parts:
                dst = self.raw[n % self.n_raw][:, :].rearrange("p (k n) -> p k n", k=k)[:, :, lo:hi]
                e.dma_start(dst, src).then_inc(self.landed[n % self.n_raw].sem, 16)

        def halves(self, n):
            k, w = self.shape.get(n, (KD, 256))
            for q in range(HALVES):
                yield [x[:, :].rearrange("p (k n) -> p k n", k=k)[:, q * k // 2:(q + 1) * k // 2, 0:w]
                       for x in (self.raw[n % self.n_raw], self.hi[n % self.n_split], self.lo[n % self.n_split])]

        def make_hi(self, e, n):
            s = n % self.n_raw
            e.wait_ge(self.landed[s].sem, self.landed[s].at(16 * sum(self.dmas.get(m, 1) for m in range(s, n + 1, self.n_raw))))
            if n >= self.n_split:
                e.wait_ge(self.used.sem, self.used.at(n - self.n_split + 1))
            for raw_, hi, _ in self.halves(n):
                e.copy(hi, raw_).then_inc(self.hi_made.sem, 1)

        def make_lo(self, e, n):
            for q, (raw_, hi, lo) in enumerate(self.halves(n)):
                e.wait_ge(self.hi_made.sem, self.hi_made.at(n * HALVES + q + 1))
                e.tensor_tensor(lo, raw_, hi.bitcast(F32), ALU.subtract).then_inc(self.lo_made.sem, 1)

        def over(self, units):
            for s in range(self.n_raw):
                self.landed[s].past(16 * sum(self.dmas.get(m, 1) for m in range(s, units, self.n_raw)))
            self.hi_made.past(units * HALVES)
            self.lo_made.past(units * HALVES)
            self.used.past(units)

        def half_ready(self, e, n, q):
            e.wait_ge(self.lo_made.sem, self.lo_made.at(n * HALVES + q + 1))

        def parts(self, n, k):
            return [w[n % self.n_split][:, :].rearrange("p (k n) -> p k n", k=k) for w in (self.hi, self.lo)]

        def by_token(self, e, n, bank, width=256, ks=range(KD)):
            wh, wl = self.parts(n, KD)
            for t in range(T):
                dst = ps[:, bank, t * 256:t * 256 + width] if len(ks) == KD else ps[:, bank[t], 0:width]
                for k in ks:
                    if t == 0 and k % 4 == 0:
                        self.half_ready(e, n, k // 4)
                    tok = slice(t * P, (t + 1) * P)
                    ins = three_passes(e, dst, x_hi[:, k, tok], x_lo[:, k, tok], wh[:, k, 0:width], wl[:, k, 0:width],
                                       k == 0, k == KD - 1)
            if KD - 1 in ks:
                ins.then_inc(self.used.sem, 1)

        def by_channel(self, e, n, bank):
            wh, wl = self.parts(n, KD)
            for j in range(2):
                for k in range(KD):
                    if j == 0 and k % 4 == 0:
                        self.half_ready(e, n, k // 4)
                    ch = slice(j * P, (j + 1) * P)
                    ins = three_passes(e, ps[:, bank, j * SEQ:(j + 1) * SEQ], wh[:, k, ch], wl[:, k, ch],
                                       x_hi[:, k, :], x_lo[:, k, :], k == 0, k == KD - 1)
            ins.then_inc(self.used.sem, 1)

    def three_passes(e, dst, xh, xl, wh, wl, first, last):
        e.matmul(dst, xh, wh, start=first, stop=False)
        e.matmul(dst, xh, wl, start=False, stop=False)
        return e.matmul(dst, xl, wh, start=False, stop=last)

    def norm_T(row, split, yT=None, load=None):
        dst = x_hi if split else yT
        with nc.Block() as block:
            @block.sync
            def _(e):
                load(e)

            @block.scalar
            def _(e):
                e.activation(stat[:, 6:7], eps_col[:, :], ACT.Sqrt)
                for t in range(T):
                    e.activation(y[:, t, :], h[:, t, :], ACT.Square, accum_out=stat[:, t:t + 1]).then_inc(sig("squares").sem, 1)
                e.wait_ge(sig("squares").sem, sig("squares").at(T))
                e.activation(stat[:, 2:4], stat[:, 0:2], ACT.Sqrt, bias=eps_col[:, :], scale=1.0 / D).then_inc(sig("rms").sem, 1)
                for b in range(4):
                    e.wait_ge(sig("y_T").sem, sig("y_T").at(b + 1))
                    for k in (2 * b, 2 * b + 1):
                        ins = e.activation(dst[:, k, :], ps[:, b, (k % 2) * SEQ:(k % 2 + 1) * SEQ], ACT.Copy,
                                           scale=gains[:, row + k:row + k + 1])
                    ins.then_inc(sig("yT_hi").sem, 1)

            @block.vector
            def _(e):
                link = linker(e, "dve_step")
                e.wait_ge(sig("rms").sem, sig("rms").at(1))
                link(e.reciprocal(stat[:, 4:6], stat[:, 2:4]))
                for t in range(T):
                    e.tensor_scalar(y[:, t, :], h[:, t, :], stat[:, 4 + t:5 + t], None, ALU.mult).then_inc(sig("y_ready").sem, 1)
                if split:
                    for b in range(4):
                        e.wait_ge(sig("yT_hi").sem, sig("yT_hi").at(b + 1))
                        for k in (2 * b, 2 * b + 1):
                            e.scalar_tensor_tensor(out=x_lo[:, k, :], in0=ps[:, b, (k % 2) * SEQ:(k % 2 + 1) * SEQ],
                                                   scalar=gains[:, row + k:row + k + 1],
                                                   in1=x_hi[:, k, :].bitcast(F32), op0=ALU.mult, op1=ALU.subtract)
                link.end()

            @block.tensor
            def _(e):
                e.wait_ge(sig("y_ready").sem, sig("y_ready").at(T))
                for b in range(4):
                    for k in (2 * b, 2 * b + 1):
                        for t in range(T):
                            o = (k % 2) * SEQ + t * P
                            ins = e.transpose(ps[:, b, o:o + P], y[:, t, k * P:(k + 1) * P], ident[:, :])
                    ins.then_inc(sig("y_T").sem, 1)
        finished(squares=T, rms=1, y_ready=T, y_T=4, yT_hi=4)

    QI, AQ, BQ, AV, AO, WO, MIX_UNITS = 1, 3, 7, 9, 11, 13, 17
    mix = Stream("mix", MIX_RAW, arena, MIX_SPLIT, arena + MIX_RAW * LIN * 4)
    mix.shape[0], mix.dmas[0] = (KD, NARROW), 3
    column = {}
    for first_unit, n_units, off in ((QI, 2, OFF_QI), (AQ, 4, OFF_AQ), (BQ, 2, OFF_BQ), (AV, 2, OFF_AV), (AO, 2, OFF_AO)):
        for j in range(n_units):
            column[first_unit + j] = off + 256 * j

    def load_mix_unit(e, n):
        if n == 0:
            mix.load(e, 0, [(0, B_LATENT, w_in_v[:, :, OFF_BC:OFF_BC + B_LATENT], KD),
                            (B_LATENT, B_LATENT + B_DH + 8, w_in_v[:, :, OFF_KI:D_IN], KD),
                            (B_LATENT + B_DH + 8, NARROW, w_in_v[:, :, OFF_AI:OFF_AI + 8], KD)])
        elif n < WO:
            mix.load(e, n, [(0, 256, w_in_v[:, :, column[n]:column[n] + 256], KD)])
        else:
            mix.load(e, n, [(0, 256, w_out_v[:, :, (n - WO) * 256:(n - WO + 1) * 256], KD)])

    def bank_of(hd):
        return 2 * (hd // 4) + hd % 2, (hd // 2 % 2) * SEQ

    GQK = stat[:, 8:9]
    rstd_q = small[:, 48:64]
    rden_b = small[:, 80:88]
    den, rden = msmall[:, 0:8], msmall[:, 8:16]
    q_sq = y[:, :, 0:512].rearrange("p t (j s) -> p t j s", j=2)
    N_PARAM_DMAS = 3 + 1 + 4
    N_TABLE_DMAS = 4
    PV = (1, 2)
    PROB_BANKS = ((2, 3), (4, 5, 6, 7))
    HCAT_BANKS = (0, 1, 5, 6)
    OUT_BANKS = ((3, 7), (0, 1), 4, 2)

    with nc.Block() as block:
        @block.sync
        def _(e):
            for t in range(T):
                e.dma_start(h[:, t, :], a["x"][0, t * P:(t + 1) * P, :]).then_inc(sig("x_loaded").sem, 16)
            e.dma_start(ident[:, :], a["c_ident"]).then_inc(sig("ident_loaded").sem, 16)
            s = sig("param_loaded")
            for row, name in ((ROW_MIX, "norm_mix"), (ROW_FFN, "norm_ffn"), (ROW_PLE, "norm_ple")):
                e.dma_start(params[row:row + 16, :], a[name].rearrange("l (k p) -> (l k) p", p=P)).then_inc(s.sem, 16)
            e.dma_start(params[ROW_CONV:ROW_CONV + 32, :],
                        a["conv_a"][0].rearrange("j (k p) -> (j k) p", p=P)).then_inc(s.sem, 16)
            for row, name in ((ROW_GQ, "norm_q_b"), (ROW_GK, "norm_k_b")):
                for half in range(2):
                    e.dma_start(params[row:row + 1, half * B_DH:(half + 1) * B_DH], a[name]).then_inc(s.sem, 16)
            load_mix_unit(e, 0)
            s = sig("table_loaded")
            e.dma_start(rel8[:, :], a["rel_bias"]).then_inc(s.sem, 16)
            e.dma_start(bias_oh[:, :], a["c_bias"]).then_inc(s.sem, 16)
            b8 = a["b_gate_e"].rearrange("a (g n) -> g n a", g=2)
            e.dma_start(bias_i[:, :], b8[0]).then_inc(s.sem, 16)
            e.dma_start(bias_f[:, :], b8[1]).then_inc(s.sem, 16)
            load_mix_unit(e, 1)
            load_mix_unit(e, 2)
            s = sig("mix_loaded")
            e.dma_start(gkv_b[:, :], a["norm_kv_b"].partition_broadcast(P)[:, 0, :]).then_inc(s.sem, 16)
            e.dma_start(w_uk[:, :], a["w_uk_b"][0]).then_inc(s.sem, 16)
            e.dma_start(w_uv[:, :, :], a["w_uv_b"][0].rearrange("h c d -> c h d")).then_inc(s.sem, 16)
            e.dma_start(halves[:, :], a["c_halves"]).then_inc(s.sem, 16)
            e.dma_start(sel_h[:, :], a["c_select"]).then_inc(s.sem, 16)
            e.dma_start(gh_b[:, :], a["norm_h_a"].partition_broadcast(P)[:, 0, :]).then_inc(s.sem, 16)
            e.dma_start(before[:, :], a["c_before"]).then_inc(s.sem, 16)
            load_mix_unit(e, 3)
            load_mix_unit(e, 4)
            e.wait_ge(sig("bias_rows").sem, sig("bias_rows").at(B_HEADS))
            e.dma_start(scratch_b[:].rearrange("(p x) -> p x", p=P),
                        bias_rows[:, :, :].rearrange("p a b -> p (a b)")).then_inc(sig("bias_out").sem, 16)
            load_mix_unit(e, 5)
            e.wait_ge(sig("bias_out").sem, sig("bias_out").at(16))
            x = B_HEADS * BIAS_W - 1
            skewed = scratch_b[P - 1:P - 1 + P * x].rearrange("(p x) -> p x", x=x)
            for hd in range(B_HEADS):
                e.dma_start(bias_toe[:, hd, :], skewed[:, hd * BIAS_W:hd * BIAS_W + SEQ]).then_inc(sig("bias_in").sem, 16)
            for n in range(6, MIX_UNITS):
                load_mix_unit(e, n)

        @block.gpsimd
        def _(e):
            link = linker(e, "pool_step")
            link(e.memset(most_mask[:, :], -ACAUSAL))
            link(e.memset(neg_mask[:, :], 0.0))
            for m, fill in ((most_mask, ACAUSAL), (neg_mask, NEG)):
                e.affine_select(out=m[:, :], in_=m[:, :], pattern=[[-1, P]], compare_op=ALU.is_ge, fill=fill,
                                base=0, channel_multiplier=1).then_inc(sig("masks").sem, 1)
            e.wait_ge(sig("w_exp").sem, sig("w_exp").at(A_HEADS))
            for c in (0, SEQ):
                e.affine_select(out=wT[:, :, c:c + P], in_=wT[:, :, c:c + P], pattern=[[0, A_HEADS], [1, P]],
                                compare_op=ALU.is_ge, fill=0.0, base=0, channel_multiplier=-1).then_inc(sig("w_masked").sem, 1)
            e.wait_ge(sig("mix_loaded").sem, sig("mix_loaded").at(16 * 7))
            e.wait_ge(sig("proj_out").sem, sig("proj_out").at(WO))
            for t in range(T):
                e.tensor_tensor(ao[:, t, :], ao[:, t, :], gh_b[:, :], ALU.mult).then_inc(sig("ao_scaled").sem, 1)
            link.end()

        @block.scalar
        def _(e):
            e.wait_ge(sig("consts").sem, sig("consts").at(1))
            e.activation(stat[:, 6:7], eps_col[:, :], ACT.Sqrt)
            for t in range(T):
                e.wait_ge(sig("x_loaded").sem, sig("x_loaded").at(16 * T))
                e.activation(y[:, t, :], h[:, t, :], ACT.Square, accum_out=stat[:, t:t + 1]).then_inc(sig("squares").sem, 1)
            e.wait_ge(sig("squares").sem, sig("squares").at(T))
            e.activation(stat[:, 2:4], stat[:, 0:2], ACT.Sqrt, bias=eps_col[:, :], scale=1.0 / D).then_inc(sig("rms").sem, 1)
            mix.make_hi(e, 0)
            e.wait_ge(sig("gains").sem, sig("gains").at(1))
            for b in range(4):
                e.wait_ge(sig("y_T").sem, sig("y_T").at(b + 1))
                for k in (2 * b, 2 * b + 1):
                    ins = e.activation(x_hi[:, k, :], ps[:, 2 + b, (k % 2) * SEQ:(k % 2 + 1) * SEQ], ACT.Copy,
                                       scale=gains[:, ROW_MIX + k:ROW_MIX + k + 1])
                ins.then_inc(sig("yT_hi").sem, 1)
            for n in range(1, 3):
                mix.make_hi(e, n)

            def projected(n):
                e.wait_ge(mix.used.sem, mix.used.at(n + 1))
                return ps[:, n % 2, :]

            def relu_index(t):
                for b in range(4):
                    e.wait_ge(sig("idx_mm").sem, sig("idx_mm").at(2 * t + b // 2 + 1))
                    hd = 4 * (b // 2) + b % 2
                    e.activation(big[:, hd:hd + 3:2, 0:P * (t + 1)],
                                 ps[:, 4 + b, :].rearrange("p (j s) -> p j s", j=2)[:, :, 0:P * (t + 1)],
                                 ACT.Relu).then_inc(sig("idx_relu").sem, 1)

            def probabilities(t):
                S = P * (t + 1)
                e.wait_ge(sig("nmax").sem, sig("nmax").at(t + 1))
                for hd in range(B_HEADS):
                    ins = e.activation(big[:, hd, 0:S], big[:, hd, 0:S], ACT.Exp, bias=small[:, 64 + hd:65 + hd],
                                       accum_out=small[:, 72 + hd:73 + hd])
                ins.then_inc(sig("probs").sem, 1)

            def probabilities_T(t):
                for g in range(2 * (t + 1)):
                    e.wait_ge(sig("probT_mm").sem, sig("probT_mm").at(2 * t + g + 1))
                    e.copy(probT[:, 4 * g:4 * g + 4, :],
                           ps[:, PROB_BANKS[t][g], :].rearrange("p (j s) -> p j s", j=4)).then_inc(sig("probT").sem, 1)

            def silu(chunks):
                for c in chunks:
                    e.wait_ge(sig("conv").sem, sig("conv").at(c + 1))
                    e.activation(qk[:, c, :], qk[:, c, :], ACT.Silu).then_inc(sig("qk").sem, 1)

            def decay_weights(heads):
                for hd in heads:
                    e.wait_ge(sig("mB_mm").sem, sig("mB_mm").at(hd // 2 * 2 + 2))
                    mB = ps[:, 2, (hd % 2) * SEQ:(hd % 2 + 1) * SEQ]
                    e.activation(wT[:, hd, 0:SEQ], mB, ACT.Exp, bias=cols[:, 0, hd:hd + 1], scale=-1.0)
                    e.activation(wT[:, hd, SEQ:384], mB[:, P:SEQ], ACT.Exp, bias=cols[:, 1, hd:hd + 1],
                                 scale=-1.0).then_inc(sig("w_exp").sem, 1)

            p = projected(0)
            e.copy(narrow[:, :, :], p.rearrange("p (t n) -> p t n", t=T)[:, :, 0:NARROW]).then_inc(sig("proj_out").sem, 1)
            e.wait_ge(sig("proj_out").sem, sig("proj_out").at(1))
            for t in range(T):
                e.activation(isc[:, 0, t * P:(t + 1) * P], bc[:, t, :], ACT.Square,
                             accum_out=small[:, t:t + 1]).then_inc(sig("lat_sq").sem, 1)
            e.wait_ge(sig("lat_sq").sem, sig("lat_sq").at(T))
            e.activation(small[:, 2:4], small[:, 0:2], ACT.Sqrt, bias=eps_col[:, :],
                         scale=1.0 / B_LATENT).then_inc(sig("lat_rms").sem, 1)
            for hd in range(4):
                e.wait_ge(sig("bias_mm").sem, sig("bias_mm").at(hd + 1))
                e.copy(bias_rows[:, hd, :], ps[:, 4 + hd, 0:BIAS_W]).then_inc(sig("bias_rows").sem, 1)
            mix.make_hi(e, 3)
            p = projected(1)
            e.copy(qi[:, 0:2, :], p.rearrange("p (j s) -> p j s", j=2)).then_inc(sig("proj_out").sem, 1)
            e.wait_ge(sig("kiT_mm").sem, sig("kiT_mm").at(1))
            e.copy(ki2[:, :], ps[:, 2, 0:SEQ]).then_inc(sig("ki2").sem, 1)
            e.wait_ge(sig("latT_mm").sem, sig("latT_mm").at(1))
            e.copy(latT[:, :], ps[:, 3, 0:SEQ]).then_inc(sig("latT").sem, 1)
            for hd in range(4, B_HEADS):
                e.wait_ge(sig("bias_mm").sem, sig("bias_mm").at(hd + 1))
                e.copy(bias_rows[:, hd, :], ps[:, hd, 0:BIAS_W]).then_inc(sig("bias_rows").sem, 1)
            mix.make_hi(e, 4)
            p = projected(2)
            e.copy(qi[:, 2:4, :], p.rearrange("p (j s) -> p j s", j=2)).then_inc(sig("proj_out").sem, 1)
            e.wait_ge(sig("uv_mm").sem, sig("uv_mm").at(1))
            for t in range(T):
                e.activation(isc[:, 0, t * B_DH:(t + 1) * B_DH], ps[:, 3, SEQ + t * B_DH:SEQ + (t + 1) * B_DH], ACT.Square,
                             accum_out=small[:, 8 + t:9 + t]).then_inc(sig("k_sq").sem, 1)
            e.wait_ge(sig("k_sq").sem, sig("k_sq").at(T))
            e.activation(small[:, 10:12], small[:, 8:10], ACT.Sqrt, bias=eps_col[:, :],
                         scale=1.0 / B_DH).then_inc(sig("k_rms").sem, 1)
            for t in range(T):
                e.copy(vu[:, t, :], ps[:, 4 + t, :]).then_inc(sig("vu").sem, 1)
            e.wait_ge(sig("gates_mm").sem, sig("gates_mm").at(1))
            e.activation(gate_f[:, :], ps[0:A_HEADS, 2, SEQ:2 * SEQ], ACT.Identity, bias=bias_f[:, :]).then_inc(sig("gate_in").sem, 1)
            e.activation(gate_i[:, :], ps[0:A_HEADS, 2, 0:SEQ], ACT.Identity, bias=bias_i[:, :]).then_inc(sig("gate_in").sem, 1)
            mix.make_hi(e, 5)
            def squares(heads):
                for hd in heads:
                    e.wait_ge(sig("h_raw").sem, sig("h_raw").at(hd + 1))
                    for t in range(T):
                        e.activation(wT[:, hd, t * P:(t + 1) * P], hcat[:, t, hd * P:(hd + 1) * P], ACT.Square,
                                     accum_out=msmall[:, 24 + 2 * hd + t:25 + 2 * hd + t]).then_inc(sig("h_sq").sem, 1)

            def conv_input(n):
                p = projected(n)
                c = 2 * (n - AQ)
                e.copy(conv_in[:, c:c + 2, CONV - 1:], p.rearrange("p (j s) -> p j s", j=2)).then_inc(sig("proj_out").sem, 1)

            conv_input(3)
            e.wait_ge(sig("bias_out").sem, sig("bias_out").at(16))
            relu_index(0)
            e.wait_ge(sig("kbT_mm").sem, sig("kbT_mm").at(1))
            e.activation(kbT[:, :], ps[:, 3, 0:SEQ], ACT.Copy, scale=GQK).then_inc(sig("kbT").sem, 1)
            mix.make_hi(e, 6)
            e.wait_ge(sig("absf").sem, sig("absf").at(1))
            e.activation(g1[:, :], g1[:, :], ACT.Exp, scale=-1.0).then_inc(sig("exp_f").sem, 1)
            e.wait_ge(sig("exp_f").sem, sig("exp_f").at(1))
            e.activation(g1[:, :], g1[:, :], ACT.Ln, bias=one_col[0:A_HEADS, :]).then_inc(sig("softplus").sem, 1)
            conv_input(4)
            mix.make_hi(e, 7)
            e.wait_ge(sig("isc").sem, sig("isc").at(1))
            relu_index(1)
            conv_input(5)
            mix.make_hi(e, 8)
            conv_input(6)
            mix.make_hi(e, 9)
            e.wait_ge(sig("gate_cols").sem, sig("gate_cols").at(1))
            e.copy(cols[:, :, :], ps[:, 3, 400:416].rearrange("p (t n) -> p t n", t=T)).then_inc(sig("cols").sem, 1)
            e.wait_ge(sig("cols").sem, sig("cols").at(1))
            e.activation(msmall[:, 16:24].rearrange("p (h t) -> p t h", t=T), cols[:, :, 4:8], ACT.Exp)
            decay_weights((0, 1))
            for n in (7, 8):
                p = projected(n)
                e.copy(bqT[:, 2 * (n - BQ):2 * (n - BQ) + 2, :], p.rearrange("p (j s) -> p j s", j=2)).then_inc(sig("proj_out").sem, 1)
                mix.make_hi(e, n + 3)
                if n == 7:
                    decay_weights((2, 3))
            e.wait_ge(sig("proj_out").sem, sig("proj_out").at(9))
            e.activation(q_sq, bqT[:, :, :].rearrange("p (t j) s -> p t j s", j=2), ACT.Square).then_inc(sig("q_sq").sem, 1)
            e.wait_ge(sig("q_sq_mm").sem, sig("q_sq_mm").at(1))
            e.activation(small[:, 32:48], ps[:, 3, 384:400], ACT.Sqrt, bias=eps_col[:, :],
                         scale=1.0 / B_DH).then_inc(sig("q_rms").sem, 1)
            silu(range(8))
            for n in (9, 10):
                p = projected(n)
                for t in range(T):
                    ins = e.copy(v_ones[:, t, 2 * (n - AV):2 * (n - AV) + 2, 0:P],
                                 p[:, t * SEQ:(t + 1) * SEQ].rearrange("p (h d) -> p h d", h=2))
                ins.then_inc(sig("proj_out").sem, 1)
                mix.make_hi(e, n + 3)
            probabilities(0)
            for n in (11, 12):
                p = projected(n)
                e.activation(ao[:, :, (n - AO) * 256:(n - AO + 1) * 256], p.rearrange("p (t n) -> p t n", t=T),
                             ACT.Sigmoid).then_inc(sig("proj_out").sem, 1)
                mix.make_hi(e, n + 3)
                if n == 11:
                    probabilities_T(0)
                    probabilities(1)
            squares((0, 1))
            probabilities_T(1)
            squares((2, 3))
            e.wait_ge(sig("h_sq").sem, sig("h_sq").at(8))
            e.activation(msmall[:, 32:40], msmall[:, 24:32], ACT.Sqrt, bias=eps_col[:, :], scale=1.0 / P).then_inc(sig("h_rms").sem, 1)
            for b in range(4):
                e.wait_ge(sig("hcat_T").sem, sig("hcat_T").at(b + 1))
                bank = HCAT_BANKS[b]
                e.copy(x_hi[:, 2 * b:2 * b + 2, :], ps[:, bank, :].rearrange("p (j s) -> p j s", j=2)).then_inc(sig("hT_hi").sem, 1)
            mix.make_hi(e, 16)

        @block.vector
        def _(e):
            link = linker(e, "dve_step")
            link(e.memset(ones[:, :], 1.0))
            link(e.memset(one_col[:, :], 1.0))
            e.memset(eps_col[:, :], EPS).then_inc(sig("consts").sem, 1)
            link(e.memset(conv_in[:, :, 0:CONV - 1], 0.0))
            link(e.memset(v_ones[:, :, :, P:P + 1], 1.0))
            e.wait_ge(sig("rms").sem, sig("rms").at(1))
            link(e.reciprocal(stat[:, 4:6], stat[:, 2:4]))
            for t in range(T):
                e.tensor_scalar(y[:, t, :], h[:, t, :], stat[:, 4 + t:5 + t], None, ALU.mult).then_inc(sig("y_ready").sem, 1)
            e.wait_ge(sig("params_T").sem, sig("params_T").at(1))
            e.tensor_copy(gains[:, 0:N_ROWS], ps[:, 6, 0:N_ROWS]).then_inc(sig("gains").sem, 1)
            mix.make_lo(e, 0)
            for b in range(4):
                e.wait_ge(sig("yT_hi").sem, sig("yT_hi").at(b + 1))
                for k in (2 * b, 2 * b + 1):
                    ins = e.scalar_tensor_tensor(out=x_lo[:, k, :], in0=ps[:, 2 + b, (k % 2) * SEQ:(k % 2 + 1) * SEQ],
                                                 scalar=gains[:, ROW_MIX + k:ROW_MIX + k + 1],
                                                 in1=x_hi[:, k, :].bitcast(F32), op0=ALU.mult, op1=ALU.subtract)
                ins.then_inc(sig("yT_lo").sem, 1)
            e.wait_ge(sig("table_loaded").sem, sig("table_loaded").at(16 * N_TABLE_DMAS))
            e.tensor_copy(rel_wide[:, :, :], rel8[:, :].unsqueeze(2).to_broadcast([BUCKETS, B_HEADS, P])).then_inc(sig("rel_wide").sem, 1)
            for n in range(1, 3):
                mix.make_lo(e, n)
            link(e.scalar_tensor_tensor(out=GQK, in0=gains[:, ROW_GQ:ROW_GQ + 1], scalar=B_DH ** -0.5,
                                        in1=gains[:, ROW_GK:ROW_GK + 1], op0=ALU.mult, op1=ALU.mult))
            e.wait_ge(sig("proj_out").sem, sig("proj_out").at(1))
            e.tensor_copy(ki_twice[:, :, :, :], ki.unsqueeze(2).to_broadcast([P, T, 2, B_DH])).then_inc(sig("ki_twice").sem, 1)
            e.wait_ge(sig("mix_loaded").sem, sig("mix_loaded").at(16 * 7))
            e.wait_ge(sig("lat_rms").sem, sig("lat_rms").at(1))
            link(e.reciprocal(small[:, 4:6], small[:, 2:4]))
            for t in range(T):
                ins = e.scalar_tensor_tensor(out=lat[:, t, :], in0=bc[:, t, :], scalar=small[:, 4 + t:5 + t],
                                             in1=gkv_b[:, :], op0=ALU.mult, op1=ALU.mult)
            ins.then_inc(sig("lat").sem, 1)
            mix.make_lo(e, 3)
            mix.make_lo(e, 4)
            e.wait_ge(sig("k_rms").sem, sig("k_rms").at(1))
            link(e.reciprocal(small[:, 12:14], small[:, 10:12]))
            for t in range(T):
                for half in range(2):
                    ins = e.tensor_scalar(kb2[:, t, half * B_DH:(half + 1) * B_DH], ps[:, 3, SEQ + t * B_DH:SEQ + (t + 1) * B_DH],
                                          small[:, 12 + t:13 + t], None, ALU.mult)
            ins.then_inc(sig("kb").sem, 1)
            e.wait_ge(sig("gate_in").sem, sig("gate_in").at(2))
            e.scalar_tensor_tensor(out=g1[:, :], in0=gate_f[:, :], scalar=-1.0, in1=gate_f[:, :],
                                   op0=ALU.mult, op1=ALU.max).then_inc(sig("absf").sem, 1)
            mix.make_lo(e, 5)
            mix.make_lo(e, 6)

            def index_sum(t):
                S = P * (t + 1)
                last = slice(S - P, S)
                for hd in range(B_HEADS):
                    e.wait_ge(sig("idx_relu").sem, sig("idx_relu").at(4 * t + bank_of(hd)[0] + 1))
                    w = wi[:, t, hd:hd + 1]
                    if hd == 0:
                        ins = e.tensor_scalar(isc[:, t, 0:S], big[:, 0, 0:S], w, None, ALU.mult)
                    else:
                        ins = e.scalar_tensor_tensor(out=isc[:, t, 0:S], in0=big[:, hd, 0:S], scalar=w, in1=isc[:, t, 0:S],
                                                     op0=ALU.mult, op1=ALU.add)
                    link(ins)
                e.nop().then_inc(sig("isc").sem, 1)
                e.wait_ge(sig("masks").sem, sig("masks").at(2))
                link(e.tensor_tensor(isc[:, t, last], isc[:, t, last], most_mask[:, :], ALU.min))

            def top_keys(t):
                S = P * (t + 1)
                last = slice(S - P, S)
                for _r in range(TOPK // 8):
                    link(e.max(top8[:, :], isc[:, t, 0:S]))
                    link(e.match_replace(isc[:, t, 0:S], top8[:, :], isc[:, t, 0:S], TAKEN))
                link(e.tensor_scalar(isc[:, t, 0:S], isc[:, t, 0:S], (ACAUSAL + TAKEN) / 2, NEG, ALU.is_gt, ALU.mult))
                link(e.tensor_tensor(isc[:, t, last], isc[:, t, last], neg_mask[:, :], ALU.min))

            def masked_logits(t):
                S = P * (t + 1)
                for hd in range(B_HEADS):
                    b, c = bank_of(hd)
                    e.wait_ge(sig("logit_mm").sem, sig("logit_mm").at(2 * t + hd // 4 + 1))
                    link(e.scalar_tensor_tensor(out=big[:, hd, 0:S], in0=ps[:, 4 + b, c:c + S],
                                                scalar=rstd_q[:, 8 * t + hd:8 * t + hd + 1],
                                                in1=bias_toe[:, hd, SEQ - S:SEQ], op0=ALU.mult, op1=ALU.add))
                link(e.tensor_tensor(big[:, :, 0:S], big[:, :, 0:S], isc[:, t, 0:S].unsqueeze(1).to_broadcast([P, B_HEADS, S]), ALU.add))
                e.tensor_reduce(small[:, 64:72], big[:, :, 0:S], AX_X, ALU.max, negate=True).then_inc(sig("nmax").sem, 1)

            def attention_out(t):
                if t == 1:
                    e.wait_ge(sig("probs").sem, sig("probs").at(2))
                    link(e.reciprocal(rden_b, small[:, 72:80]))
                e.wait_ge(sig("pv_mm").sem, sig("pv_mm").at(t + 1))
                e.tensor_tensor(hcat[:, t, 512:1024].rearrange("p (h d) -> p h d", h=B_HEADS),
                                ps[:, PV[t], :].rearrange("p (h d) -> p h d", h=B_HEADS),
                                rden_b.unsqueeze(2).to_broadcast([P, B_HEADS, B_DH]),
                                ALU.mult).then_inc(sig("attn_out").sem, 1)

            def conv(chunks):
                for c in chunks:
                    e.wait_ge(sig("proj_out").sem, sig("proj_out").at(AQ + c // 2 + 1))
                    w = lambda j: gains[:, ROW_CONV + 8 * j + c:ROW_CONV + 8 * j + c + 1]
                    link(e.tensor_scalar(qk[:, c, :], conv_in[:, c, 0:SEQ], w(0), None, ALU.mult))
                    for j in range(1, CONV):
                        ins = e.scalar_tensor_tensor(out=qk[:, c, :], in0=conv_in[:, c, j:j + SEQ], scalar=w(j),
                                                     in1=qk[:, c, :], op0=ALU.mult, op1=ALU.add)
                        if j < CONV - 1:
                            link(ins)
                    ins.then_inc(sig("conv").sem, 1)

            conv((0, 1))
            index_sum(0)
            mix.make_lo(e, 7)
            e.wait_ge(sig("softplus").sem, sig("softplus").at(1))
            link(e.scalar_tensor_tensor(out=g2[:, :], in0=gate_f[:, :], scalar=0.0, in1=g1[:, :], op0=ALU.min, op1=ALU.subtract))
            e.wait_ge(sig("bias_mm").sem, sig("bias_mm").at(B_HEADS))
            one_row = wT[0:A_HEADS, 0, 0:SEQ]
            link(e.memset(one_row, 1.0))
            link(e.tensor_tensor_scan(g3[:, :], one_row, g2[:, :], 0.0, ALU.mult, ALU.add))
            link(e.tensor_tensor(g1[:, :], gate_i[:, :], g3[:, :], ALU.subtract))
            link(e.tensor_tensor_scan(g2[:, :], one_row, g1[:, :], 0.0, ALU.mult, ALU.max))
            e.scalar_tensor_tensor(out=g4[:, :], in0=g3[:, :], scalar=-1.0, in1=g2[:, :],
                                   op0=ALU.mult, op1=ALU.subtract).then_inc(sig("gate_rows").sem, 1)
            top_keys(0)
            mix.make_lo(e, 8)
            conv((2, 3))
            index_sum(1)
            mix.make_lo(e, 9)
            conv((4, 5))
            mix.make_lo(e, 10)
            conv((6, 7))
            mix.make_lo(e, 11)
            e.wait_ge(sig("q_rms").sem, sig("q_rms").at(1))
            link(e.reciprocal(rstd_q, small[:, 32:48]))
            e.wait_ge(sig("bias_in").sem, sig("bias_in").at(16 * B_HEADS))
            masked_logits(0)
            mix.make_lo(e, 12)
            top_keys(1)
            e.wait_ge(sig("probT_mm").sem, sig("probT_mm").at(2))
            link(e.reciprocal(rden_b, small[:, 72:80]))
            masked_logits(1)

            def mlstm_scores(g):
                for hd in (2 * g, 2 * g + 1):
                    e.wait_ge(sig("qk_mm").sem, sig("qk_mm").at(hd + 1))
                    e.scalar_tensor_tensor(out=wT[:, hd, :], in0=ps[:, 2 + hd % 2, 0:384], scalar=A_DK ** -0.5,
                                           in1=wT[:, hd, :], op0=ALU.mult, op1=ALU.mult).then_inc(sig("scores").sem, 1)

            def mlstm_out(g):
                e.wait_ge(sig("num_mm").sem, sig("num_mm").at(2 * g + 2))
                d4, r4 = den[:, 4 * g:4 * g + 4], rden[:, 4 * g:4 * g + 4]
                link(e.tensor_copy(d4.rearrange("p (h t) -> p h t", t=T),
                                   ps[:, 2:4, 0:258].rearrange("p h (t d) -> p h t d", t=T)[:, :, :, P]))
                link(e.scalar_tensor_tensor(out=r4, in0=d4, scalar=-1.0, in1=d4, op0=ALU.mult, op1=ALU.max))
                link(e.tensor_tensor(r4, r4, msmall[:, 16 + 4 * g:20 + 4 * g], ALU.max))
                link(e.reciprocal(d4, r4))
                for hd in (2 * g, 2 * g + 1):
                    for t in range(T):
                        ins = e.tensor_scalar(hcat[:, t, hd * P:(hd + 1) * P], ps[:, 2 + hd % 2, t * 129:t * 129 + P],
                                              den[:, 2 * hd + t:2 * hd + t + 1], None, ALU.mult)
                    ins.then_inc(sig("h_raw").sem, 1)

            e.wait_ge(sig("w_masked").sem, sig("w_masked").at(2))
            mlstm_scores(0)
            attention_out(0)
            mix.make_lo(e, 13)
            mlstm_out(0)
            mlstm_scores(1)
            mix.make_lo(e, 14)
            mlstm_out(1)
            mix.make_lo(e, 15)
            e.wait_ge(sig("h_rms").sem, sig("h_rms").at(1))
            link(e.reciprocal(msmall[:, 40:48], msmall[:, 32:40]))
            e.wait_ge(sig("ao_scaled").sem, sig("ao_scaled").at(T))
            for hd in range(A_HEADS):
                for t in range(T):
                    c = slice(hd * P, (hd + 1) * P)
                    ins = e.scalar_tensor_tensor(out=hcat[:, t, c], in0=hcat[:, t, c], scalar=msmall[:, 40 + 2 * hd + t:41 + 2 * hd + t],
                                                 in1=ao[:, t, c], op0=ALU.mult, op1=ALU.mult)
                ins.then_inc(sig("h_out").sem, 1)
            attention_out(1)
            for b in range(4):
                e.wait_ge(sig("hT_hi").sem, sig("hT_hi").at(b + 1))
                bank = HCAT_BANKS[b]
                e.tensor_tensor(x_lo[:, 2 * b:2 * b + 2, :], ps[:, bank, :].rearrange("p (j s) -> p j s", j=2),
                                x_hi[:, 2 * b:2 * b + 2, :].bitcast(F32), ALU.subtract).then_inc(sig("hT_lo").sem, 1)
            mix.make_lo(e, 16)
            for n in range(WO, MIX_UNITS):
                e.wait_ge(mix.used.sem, mix.used.at(n + 1))
                c = slice((n - WO) * 256, (n - WO + 1) * 256)
                b = OUT_BANKS[n - WO]
                if n < WO + 2:
                    for t in range(T):
                        e.tensor_tensor(h[:, t, c], h[:, t, c], ps[:, b[t], 0:256], ALU.add)
                else:
                    e.tensor_tensor(h[:, :, c], h[:, :, c], ps[:, b, :].rearrange("p (t n) -> p t n", t=T), ALU.add)
            link.end()

        @block.tensor
        def _(e):
            e.wait_ge(sig("ident_loaded").sem, sig("ident_loaded").at(16))
            e.wait_ge(sig("param_loaded").sem, sig("param_loaded").at(16 * N_PARAM_DMAS))
            e.transpose(ps[:, 6, 0:N_ROWS], params[0:N_ROWS, :], ident[0:N_ROWS, 0:N_ROWS]).then_inc(sig("params_T").sem, 1)
            e.wait_ge(sig("y_ready").sem, sig("y_ready").at(T))
            for b in range(4):
                for k in (2 * b, 2 * b + 1):
                    for t in range(T):
                        o = (k % 2) * SEQ + t * P
                        ins = e.transpose(ps[:, 2 + b, o:o + P], y[:, t, k * P:(k + 1) * P], ident[:, :])
                ins.then_inc(sig("y_T").sem, 1)

            def project(n):
                if n >= 2:
                    e.wait_ge(sig("proj_out").sem, sig("proj_out").at(n - 1))
                if n == 0:
                    mix.by_token(e, 0, 0, width=NARROW)
                elif n < AV:
                    mix.by_channel(e, n, n % 2)
                else:
                    mix.by_token(e, n, n % 2)

            def bias_table(heads):
                for hd in heads:
                    e.matmul(ps[:, 4 + hd % 4, 0:BIAS_W], rel_wide[:, hd, :], bias_oh[:, :], start=True,
                             stop=True).then_inc(sig("bias_mm").sem, 1)

            def index_scores(t):
                S = P * (t + 1)
                if t:
                    e.wait_ge(sig("idx_relu").sem, sig("idx_relu").at(4))
                for hd in range(B_HEADS):
                    b, c = bank_of(hd)
                    part = slice((hd % 2) * B_DH, (hd % 2 + 1) * B_DH)
                    ins = e.matmul(ps[:, 4 + b, c:c + S], qi[part, hd // 2, t * P:(t + 1) * P], ki2[part, 0:S],
                                   start=True, stop=True)
                    if hd % 4 == 3:
                        ins.then_inc(sig("idx_mm").sem, 1)

            def logits(t):
                S = P * (t + 1)
                if t == 0:
                    e.wait_ge(sig("idx_relu").sem, sig("idx_relu").at(8))
                else:
                    e.wait_ge(sig("nmax").sem, sig("nmax").at(1))
                for hd in range(B_HEADS):
                    b, c = bank_of(hd)
                    part = slice((hd % 2) * B_DH, (hd % 2 + 1) * B_DH)
                    ins = e.matmul(ps[:, 4 + b, c:c + S], bqT[part, hd // 2, t * P:(t + 1) * P], kbT[part, 0:S],
                                   start=True, stop=True)
                    if hd % 4 == 3:
                        ins.then_inc(sig("logit_mm").sem, 1)

            def probabilities_T(t):
                e.wait_ge(sig("probs").sem, sig("probs").at(t + 1))
                for n in range(8 * (t + 1)):
                    hd, k = n // (t + 1), n % (t + 1)
                    ins = e.transpose(ps[:, PROB_BANKS[t][n // 4], (n % 4) * P:(n % 4 + 1) * P], big[:, hd, k * P:(k + 1) * P], ident[:, :])
                    if n % 4 == 3:
                        ins.then_inc(sig("probT_mm").sem, 1)

            def attend(t):
                for n in range(8 * (t + 1)):
                    hd, k = n // (t + 1), n % (t + 1)
                    if n % 4 == 0:
                        e.wait_ge(sig("probT").sem, sig("probT").at(2 * t + n // 4 + 1))
                    ins = e.matmul(ps[:, PV[t], hd * B_DH:(hd + 1) * B_DH], probT[:, n, :], vu[:, k, hd * B_DH:(hd + 1) * B_DH],
                                   start=(k == 0), stop=(k == t))
                ins.then_inc(sig("pv_mm").sem, 1)

            e.wait_ge(sig("yT_lo").sem, sig("yT_lo").at(4))
            project(0)
            e.wait_ge(sig("rel_wide").sem, sig("rel_wide").at(1))
            bias_table(range(4))
            project(1)
            e.wait_ge(sig("ki_twice").sem, sig("ki_twice").at(1))
            for t in range(T):
                ins = e.transpose(ps[:, 2, t * P:(t + 1) * P], ki_twice[:, t, :, :].rearrange("p g d -> p (g d)"), ident[:, :])
            ins.then_inc(sig("kiT_mm").sem, 1)
            e.wait_ge(sig("lat").sem, sig("lat").at(1))
            for t in range(T):
                ins = e.transpose(ps[:, 3, t * P:(t + 1) * P], lat[:, t, :], ident[:, :])
            ins.then_inc(sig("latT_mm").sem, 1)
            e.wait_ge(sig("bias_rows").sem, sig("bias_rows").at(4))
            bias_table(range(4, B_HEADS))
            project(2)
            e.wait_ge(sig("latT").sem, sig("latT").at(1))
            e.wait_ge(sig("bias_rows").sem, sig("bias_rows").at(6))
            for t in range(T):
                e.matmul(ps[:, 3, SEQ + t * B_DH:SEQ + (t + 1) * B_DH], latT[:, t * P:(t + 1) * P], w_uk[:, :], start=True, stop=True)
                ins = e.matmul(ps[:, 4 + t, :], latT[:, t * P:(t + 1) * P], w_uv[:, :, :].rearrange("p h d -> p (h d)"),
                               start=True, stop=True)
            ins.then_inc(sig("uv_mm").sem, 1)
            e.wait_ge(sig("ki2").sem, sig("ki2").at(1))
            for g in range(2):
                for t in range(T):
                    c = NARROW - 2 * A_HEADS + g * A_HEADS
                    ins = e.transpose(ps[0:A_HEADS, 2, g * SEQ + t * P:g * SEQ + (t + 1) * P], narrow[:, t, c:c + A_HEADS], ident[:, :])
            ins.then_inc(sig("gates_mm").sem, 1)
            project(3)
            e.wait_ge(sig("bias_rows").sem, sig("bias_rows").at(B_HEADS))
            e.wait_ge(sig("vu").sem, sig("vu").at(T))
            index_scores(0)
            e.wait_ge(sig("kb").sem, sig("kb").at(1))
            for t in range(T):
                ins = e.transpose(ps[:, 3, t * P:(t + 1) * P], kb2[:, t, :], ident[:, :])
            ins.then_inc(sig("kbT_mm").sem, 1)
            project(4)
            index_scores(1)
            project(5)
            project(6)
            e.wait_ge(sig("gate_rows").sem, sig("gate_rows").at(1))
            for t in range(T):
                o = 400 + 8 * t
                e.transpose(ps[:, 3, o:o + 4], g1[:, t * P:(t + 1) * P], ident[0:A_HEADS, 0:A_HEADS])
                ins = e.transpose(ps[:, 3, o + 4:o + 8], g4[:, t * P:(t + 1) * P], ident[0:A_HEADS, 0:A_HEADS])
            ins.then_inc(sig("gate_cols").sem, 1)
            for hd in range(A_HEADS):
                if hd == 2:
                    project(7)
                    e.wait_ge(sig("w_exp").sem, sig("w_exp").at(2))
                e.matmul(ps[:, 2, hd % 2 * SEQ:(hd % 2 + 1) * SEQ], sel_h[:, hd * P:(hd + 1) * P], g2[:, :], start=True,
                         stop=True).then_inc(sig("mB_mm").sem, 1)
            project(8)
            project(9)
            e.wait_ge(sig("q_sq").sem, sig("q_sq").at(1))
            e.wait_ge(sig("cols").sem, sig("cols").at(1))
            for t in range(T):
                for j in range(4):
                    o = 384 + 8 * t + 2 * j
                    ins = e.matmul(ps[:, 3, o:o + 2], q_sq[:, j // 2, j % 2, t * P:(t + 1) * P], halves[:, :], start=True, stop=True)
            ins.then_inc(sig("q_sq_mm").sem, 1)
            logits(0)
            project(10)
            project(11)
            logits(1)
            e.wait_ge(sig("w_exp").sem, sig("w_exp").at(A_HEADS))
            probabilities_T(0)
            e.wait_ge(sig("proj_out").sem, sig("proj_out").at(12))
            attend(0)

            def mlstm_scores(g):
                for hd in (2 * g, 2 * g + 1):
                    if g == 0:
                        e.wait_ge(sig("qk").sem, sig("qk").at(8))
                    else:
                        e.wait_ge(sig("h_raw").sem, sig("h_raw").at(hd - 1))
                    e.matmul(ps[:, 2 + hd % 2, 0:SEQ], qk[:, 4 + hd, 0:P], qk[:, hd, :], start=True, stop=True)
                    e.matmul(ps[:, 2 + hd % 2, SEQ:384], qk[:, 4 + hd, P:SEQ], qk[:, hd, P:SEQ], start=True,
                             stop=True).then_inc(sig("qk_mm").sem, 1)

            def mlstm_values(g):
                e.wait_ge(sig("proj_out").sem, sig("proj_out").at(AV + 2))
                for hd in (2 * g, 2 * g + 1):
                    b = 2 + hd % 2
                    e.wait_ge(sig("scores").sem, sig("scores").at(hd + 1))
                    e.matmul(ps[:, b, 0:129], wT[:, hd, 0:P], v_ones[:, 0, hd, :], start=True, stop=True)
                    e.matmul(ps[:, b, 129:258], wT[:, hd, P:SEQ], v_ones[:, 0, hd, :], start=True, stop=False)
                    e.matmul(ps[:, b, 129:258], wT[:, hd, SEQ:384], v_ones[:, 1, hd, :], start=False,
                             stop=True).then_inc(sig("num_mm").sem, 1)

            def transpose_out(b):
                for k in (2 * b, 2 * b + 1):
                    for t in range(T):
                        o = (k % 2) * SEQ + t * P
                        ins = e.transpose(ps[:, HCAT_BANKS[b], o:o + P], hcat[:, t, k * P:(k + 1) * P], ident[:, :])
                ins.then_inc(sig("hcat_T").sem, 1)

            mlstm_scores(0)
            project(12)
            mlstm_values(0)
            mlstm_scores(1)
            probabilities_T(1)
            mlstm_values(1)
            e.wait_ge(sig("h_raw").sem, sig("h_raw").at(A_HEADS))
            attend(1)
            e.wait_ge(sig("h_out").sem, sig("h_out").at(A_HEADS))
            transpose_out(0)
            transpose_out(1)
            e.wait_ge(sig("attn_out").sem, sig("attn_out").at(T))
            transpose_out(2)
            transpose_out(3)
            e.wait_ge(sig("hT_lo").sem, sig("hT_lo").at(2))
            for n in range(WO, WO + 2):
                mix.by_token(e, n, OUT_BANKS[n - WO], ks=range(0, 4))
            e.wait_ge(sig("hT_lo").sem, sig("hT_lo").at(4))
            for n in range(WO, WO + 2):
                mix.by_token(e, n, OUT_BANKS[n - WO], ks=range(4, KD))
            for n in range(WO + 2, MIX_UNITS):
                mix.by_token(e, n, OUT_BANKS[n - WO])
    mix.over(MIX_UNITS)
    finished(squares=T, rms=1, y_ready=T, y_T=4, yT_hi=4, yT_lo=4)

    def embed(layer):
        tag = f"ple{layer}"
        ws = Stream(tag, 5, ring_raw, 2, ring_split)
        ws.shape[0] = (2, D)
        t5 = inside(ring_split + 4 * LIN * 4, 2 * RING * UNIT_B - 4 * LIN * 4)
        p_in = t5(f"p_in_{tag}", (P, T, PLE))
        p_hi = t5(f"p_hi_{tag}", (P, 2, SEQ), F32R)
        p_lo = t5(f"p_lo_{tag}", (P, 2, SEQ), F32R)
        emb = t5(f"emb_{tag}", (P, T, D))
        sg = t5(f"sg_{tag}", (P, 4, 512))
        row = ROW_PLE + KD * layer

        def load(e, free=None):
            for n in range(5):
                if free is not None:
                    free(n)
                if n == 0:
                    ws.load(e, 0, [(0, D, a["w_ple"][layer].rearrange("(k p) n -> p k n", p=P), 2)])
                else:
                    ws.load(e, n, [(0, 256, a["w_ple_gate"][layer][:, (n - 1) * 256:n * 256].rearrange("(k p) n -> p k n", p=P), KD)])

        def launch():
            with nc.Block() as block:
                @block.sync
                def _(e):
                    e.dma_start(p_in[:, :, :], a["p"][layer, 0].rearrange("(t p) n -> p t n", p=P)).then_inc(sig("p_loaded").sem, 16)
                    if layer == N_LAYERS - 1:
                        for b in range(4):
                            e.wait_ge(sig("embedded").sem, sig("embedded").at(2 * b + 2))
                            e.dma_start(out[0, :, b * 256:(b + 1) * 256].rearrange("(t p) n -> p t n", p=P),
                                        h[:, :, b * 256:(b + 1) * 256]).then_inc(sig("out").sem, 16)
                        e.wait_ge(sig("out").sem, sig("out").at(64))

                @block.scalar
                def _(e):
                    e.activation(stat[:, 6:7], eps_col[:, :], ACT.Sqrt)
                    for t in range(T):
                        e.activation(y[:, t, :], h[:, t, :], ACT.Square, accum_out=stat[:, t:t + 1]).then_inc(sig("squares").sem, 1)
                    e.wait_ge(sig("squares").sem, sig("squares").at(T))
                    e.activation(stat[:, 2:4], stat[:, 0:2], ACT.Sqrt, bias=eps_col[:, :], scale=1.0 / D).then_inc(sig("rms").sem, 1)
                    ws.make_hi(e, 0)
                    e.wait_ge(sig("p_T").sem, sig("p_T").at(1))
                    e.copy(p_hi[:, :, :], ps[:, 4, :].rearrange("p (k s) -> p k s", k=2)).then_inc(sig("p_hi").sem, 1)
                    for b in range(4):
                        e.wait_ge(sig("y_T").sem, sig("y_T").at(b + 1))
                        for k in (2 * b, 2 * b + 1):
                            ins = e.activation(x_hi[:, k, :], ps[:, b, (k % 2) * SEQ:(k % 2 + 1) * SEQ], ACT.Copy,
                                               scale=gains[:, row + k:row + k + 1])
                        ins.then_inc(sig("yT_hi").sem, 1)
                    ws.make_hi(e, 1)
                    e.wait_ge(ws.used.sem, ws.used.at(1))
                    for t in range(T):
                        e.copy(emb[:, t, :].rearrange("p (n c) -> p n c", n=2), ps[:, 4 + 2 * t:6 + 2 * t, :]).then_inc(sig("emb").sem, 1)
                    for n in range(2, 5):
                        ws.make_hi(e, n)
                        e.wait_ge(ws.used.sem, ws.used.at(n))
                        e.activation(sg[:, n - 2, :], ps[:, n - 2, :], ACT.Sigmoid).then_inc(sig("gate_sig").sem, 1)
                    e.wait_ge(ws.used.sem, ws.used.at(5))
                    e.activation(sg[:, 3, :], ps[:, 3, :], ACT.Sigmoid).then_inc(sig("gate_sig").sem, 1)

                @block.vector
                def _(e):
                    link = linker(e, "dve_step")
                    e.wait_ge(sig("rms").sem, sig("rms").at(1))
                    link(e.reciprocal(stat[:, 4:6], stat[:, 2:4]))
                    for t in range(T):
                        e.tensor_scalar(y[:, t, :], h[:, t, :], stat[:, 4 + t:5 + t], None, ALU.mult).then_inc(sig("y_ready").sem, 1)
                    ws.make_lo(e, 0)
                    e.wait_ge(sig("p_hi").sem, sig("p_hi").at(1))
                    e.tensor_tensor(p_lo[:, :, :], ps[:, 4, :].rearrange("p (k s) -> p k s", k=2),
                                    p_hi[:, :, :].bitcast(F32), ALU.subtract).then_inc(sig("p_lo").sem, 1)
                    for b in range(4):
                        e.wait_ge(sig("yT_hi").sem, sig("yT_hi").at(b + 1))
                        for k in (2 * b, 2 * b + 1):
                            ins = e.scalar_tensor_tensor(out=x_lo[:, k, :], in0=ps[:, b, (k % 2) * SEQ:(k % 2 + 1) * SEQ],
                                                         scalar=gains[:, row + k:row + k + 1],
                                                         in1=x_hi[:, k, :].bitcast(F32), op0=ALU.mult, op1=ALU.subtract)
                        ins.then_inc(sig("yT_lo").sem, 1)
                    for n in range(1, 5):
                        ws.make_lo(e, n)
                    for b in range(4):
                        e.wait_ge(sig("gate_sig").sem, sig("gate_sig").at(b + 1))
                        e.wait_ge(sig("emb").sem, sig("emb").at(T))
                        c = slice(b * 256, (b + 1) * 256)
                        link(e.tensor_tensor(sg[:, b, :].rearrange("p (t n) -> p t n", t=T),
                                             sg[:, b, :].rearrange("p (t n) -> p t n", t=T), emb[:, :, c], ALU.mult))
                        e.tensor_tensor(h[:, :, c], h[:, :, c], sg[:, b, :].rearrange("p (t n) -> p t n", t=T),
                                        ALU.add).then_inc(sig("embedded").sem, 2)
                    link.end()

                @block.tensor
                def _(e):
                    e.wait_ge(sig("p_loaded").sem, sig("p_loaded").at(16))
                    for k in range(2):
                        for t in range(T):
                            ins = e.transpose(ps[:, 4, k * SEQ + t * P:k * SEQ + (t + 1) * P], p_in[:, t, k * P:(k + 1) * P],
                                              ident[:, :])
                    ins.then_inc(sig("p_T").sem, 1)
                    e.wait_ge(sig("y_ready").sem, sig("y_ready").at(T))
                    for b in range(4):
                        for k in (2 * b, 2 * b + 1):
                            for t in range(T):
                                o = (k % 2) * SEQ + t * P
                                ins = e.transpose(ps[:, b, o:o + P], y[:, t, k * P:(k + 1) * P], ident[:, :])
                        ins.then_inc(sig("y_T").sem, 1)
                    e.wait_ge(sig("p_lo").sem, sig("p_lo").at(1))
                    wh, wl = ws.parts(0, 2)
                    for t in range(T):
                        for n in range(2):
                            for k in range(2):
                                ws.half_ready(e, 0, k)
                                ins = three_passes(e, ps[:, 4 + 2 * t + n, :], p_hi[:, k, t * P:(t + 1) * P],
                                                   p_lo[:, k, t * P:(t + 1) * P], wh[:, k, n * 512:(n + 1) * 512],
                                                   wl[:, k, n * 512:(n + 1) * 512], k == 0, k == 1)
                    ins.then_inc(ws.used.sem, 1)
                    e.wait_ge(sig("yT_lo").sem, sig("yT_lo").at(4))
                    for n in range(1, 5):
                        ws.by_token(e, n, n - 1)
            finished(squares=T, rms=1, y_ready=T, y_T=4, yT_hi=4, yT_lo=4, p_loaded=16, p_T=1, p_hi=1, p_lo=1, emb=T, gate_sig=4,
                     embedded=8)
            ws.over(5)
        return ws, load, launch

    Q = N_UNITS * QUARTERS
    CH = N_CH

    def swiglu(weights, tag, moe=None, load_next=None):
        tiles = T if moe is None else 1
        bU, bG, bZ = ([0, 1], [2, 3], [4, 6]) if moe is None else ([0], [1], [2])
        names = ["raw0", "raw1", "raw2", "split_hi", "split_lo", "unit_used", "silu", "hid", "hid_T", "hidT_hi",
                 "hidT_lo", "acc_out", "load_due"]
        if moe is not None:
            names += ["pick", "gathered", "x_hi", "x_lo", "back", "back_T", "backT", "scatter", "scattered", "acc_cleared"]
        sem = {k: sig(f"ffn_{k}") for k in names}
        first = sem
        second = None if moe is None else {k: sig(f"more_{k}") for k in names}

        hidden_after = {AT[("G", c)] + 2: c for c in range(CH)}
        transposed_after = {AT[("G", c)] + 3: c for c in range(CH)}

        def split_lo_at(i, n, q=QUARTERS - 1):
            return i * Q + n * QUARTERS + q + 1


        def unit_used_at(i, n):
            return i * N_UNITS + RING + n + 1

        def chunk_at(i, c, t=None):
            return i * (CH * tiles) + c * tiles + (tiles if t is None else t + 1)

        def slot(n):
            return n % RING

        def load_units(e, i, units):
            for n in units:
                kind, c = UNITS[n % N_UNITS]
                w = weights[kind] if moe is None else weights[kind][i + n // N_UNITS]
                if kind == "D":
                    src = w[c * FC:(c + 1) * FC, :].rearrange("(j p) n -> p j n", p=P)
                    dst = raw[slot(n)][:, :].rearrange("p (j n) -> p j n", j=4)
                else:
                    src = w[:, c * FC:(c + 1) * FC].rearrange("(k p) n -> p k n", p=P)
                    dst = raw[slot(n)][:, :].rearrange("p (k n) -> p k n", k=KD)
                if n >= RING:
                    e.wait_ge(sem["split_lo"].sem, sem["split_lo"].at(split_lo_at(i, n - RING)))
                    e.sem_inc(sem["load_due"].sem, 1)
                e.dma_start(dst, src).then_inc(sem[f"raw{slot(n)}"].sem, 16)

        def split_hi(e, i, n):
            e.wait_ge(sem[f"raw{slot(n)}"].sem, sem[f"raw{slot(n)}"].at(i * (16 * N_UNITS // RING) + 16 * (n // RING + 1)))
            e.wait_ge(sem["unit_used"].sem, sem["unit_used"].at(unit_used_at(i, n - RING)))
            for q in range(QUARTERS):
                c = slice(q * 1024, (q + 1) * 1024)
                e.copy(w_hi[slot(n)][:, c], raw[slot(n)][:, c]).then_inc(sem["split_hi"].sem, 1)

        def split_lo(e, i, n):
            for q in range(QUARTERS):
                c = slice(q * 1024, (q + 1) * 1024)
                e.wait_ge(sem["split_hi"].sem, sem["split_hi"].at(i * Q + n * QUARTERS + q + 1))
                e.tensor_tensor(w_lo[slot(n)][:, c], raw[slot(n)][:, c], w_hi[slot(n)][:, c].bitcast(F32),
                                ALU.subtract).then_inc(sem["split_lo"].sem, 1)

        def unit_product(e, i, n):
            kind, c = UNITS[n]
            if kind == "U" and c > 0:
                e.wait_ge(sem["hid"].sem, sem["hid"].at(chunk_at(i, c - 1)))
            if kind == "G" and c > 0:
                e.wait_ge(sem["hidT_lo"].sem, sem["hidT_lo"].at(chunk_at(i, c - 1)))
            if kind == "D":
                e.wait_ge(sem["hidT_lo"].sem, sem["hidT_lo"].at(chunk_at(i, c)))
                if c == 0 and moe is not None:
                    e.wait_ge(sem["acc_out"].sem, sem["acc_out"].at(i + 1))
            wh, wl = w_hi[slot(n)], w_lo[slot(n)]
            for t in range(tiles):
                for q in range(QUARTERS):
                    if t == 0:
                        e.wait_ge(sem["split_lo"].sem, sem["split_lo"].at(split_lo_at(i, n, q)))
                    for m in range(2):
                        cols_ = slice((2 * q + m) * 512, (2 * q + m + 1) * 512)
                        if kind == "D":
                            ins = three_passes(e, ps[:, bZ[t] + m, :], hidT_hi[t][:, q, :], hidT_lo[t][:, q, :],
                                               wh[:, cols_], wl[:, cols_], c == 0 and q == 0, c == CH - 1 and q == QUARTERS - 1)
                        else:
                            k = 2 * q + m
                            ins = three_passes(e, ps[:, (bU if kind == "U" else bG)[t], :],
                                               x_hi[:, k, t * P:(t + 1) * P], x_lo[:, k, t * P:(t + 1) * P],
                                               wh[:, cols_], wl[:, cols_], k == 0, k == KD - 1)
            ins.then_inc(sem["unit_used"].sem, 1)

        def transpose_hidden(e, i, c):
            for t in range(tiles):
                e.wait_ge(sem["hid"].sem, sem["hid"].at(chunk_at(i, c, t)))
                for j in range(4):
                    ins = e.transpose(ps[:, bG[t], j * P:(j + 1) * P], hid[t][:, j * P:(j + 1) * P], ident[:, :])
                ins.then_inc(sem["hid_T"].sem, 1)

        def silu(e, i, c):
            e.wait_ge(sem["unit_used"].sem, sem["unit_used"].at(unit_used_at(i, AT[("G", c)])))
            for t in range(tiles):
                e.activation(hid[t][:, :], ps[:, bG[t], :], ACT.Silu).then_inc(sem["silu"].sem, 1)

        def hidden(e, i, c):
            for t in range(tiles):
                e.wait_ge(sem["silu"].sem, sem["silu"].at(chunk_at(i, c, t)))
                e.tensor_tensor(hid[t][:, :], hid[t][:, :], ps[:, bU[t], :], ALU.mult).then_inc(sem["hid"].sem, 1)

        def hiddenT_hi(e, i, c):
            for t in range(tiles):
                e.wait_ge(sem["hid_T"].sem, sem["hid_T"].at(chunk_at(i, c, t)))
                e.copy(hidT_hi[t][:, :, :], ps[:, bG[t], :].rearrange("p (j s) -> p j s", j=4)).then_inc(sem["hidT_hi"].sem, 1)

        def hiddenT_lo(e, i, c):
            for t in range(tiles):
                e.wait_ge(sem["hidT_hi"].sem, sem["hidT_hi"].at(chunk_at(i, c, t)))
                e.tensor_tensor(hidT_lo[t][:, :, :], ps[:, bG[t], :].rearrange("p (j s) -> p j s", j=4),
                                hidT_hi[t][:, :, :].bitcast(F32), ALU.subtract).then_inc(sem["hidT_lo"].sem, 1)

        def pick_for(e, col):
            for t in range(T):
                e.tensor_scalar(pick[:, t, :], iota[:, :], rank[:, t, col], None, ALU.is_equal).then_inc(sem["pick"].sem, 1)

        def back_for(e, col):
            for t in range(T):
                e.tensor_scalar(back[:, t, :], iota[:, :], rank[:, t, col], gate[:, t, col], ALU.is_equal,
                                ALU.mult).then_inc(sem["back"].sem, 1)

        def transpose_back(e, i):
            e.wait_ge(sem["back"].sem, sem["back"].at((i + 1) * T))
            for t in range(T):
                ins = e.transpose(ps[:, 6, t * P:(t + 1) * P], back[:, t, :], ident[:, :])
            ins.then_inc(sem["back_T"].sem, 1)

        def leave(e, i):
            e.wait_ge(sem["unit_used"].sem, sem["unit_used"].at(unit_used_at(i, -1)))
            e.copy(slot_out[:, :].rearrange("p (n c) -> p n c", n=2), ps[:, 2:4, :]).then_inc(sem["acc_out"].sem, 1)
            e.wait_ge(sem["back_T"].sem, sem["back_T"].at(i + 1))
            e.copy(backT[:, :], ps[:, 6, 0:SEQ]).then_inc(sem["backT"].sem, 1)

        def scatter(e, i):
            e.wait_ge(sem["acc_out"].sem, sem["acc_out"].at(i + 1))
            e.wait_ge(sem["backT"].sem, sem["backT"].at(i + 1))
            for t in range(T):
                for n in range(2):
                    ins = e.matmul(ps[:, 4 + 2 * t + n, :], backT[:, t * P:(t + 1) * P], slot_out[:, n * 512:(n + 1) * 512],
                                   start=True, stop=True)
            ins.then_inc(sem["scatter"].sem, 1)

        def add_scattered(e, i):
            e.wait_ge(sem["scatter"].sem, sem["scatter"].at(i + 1))
            for t in range(T):
                e.tensor_tensor(h[:, t, :].rearrange("p (n c) -> p n c", n=2), h[:, t, :].rearrange("p (n c) -> p n c", n=2),
                                ps[:, 4 + 2 * t:6 + 2 * t, :], ALU.add).then_inc(sem["scattered"].sem, 1)

        def gather(e, i):
            e.wait_ge(sem["pick"].sem, sem["pick"].at((i + 1) * T))
            for k in range(KD):
                for t in range(T):
                    ins = e.matmul(ps[:, 4 + k // 4, (k % 4) * P:(k % 4 + 1) * P], y[:, t, k * P:(k + 1) * P], pick[:, t, :],
                                   start=(t == 0), stop=(t == T - 1))
            ins.then_inc(sem["gathered"].sem, 1)

        def gathered_hi(e, i):
            e.wait_ge(sem["gathered"].sem, sem["gathered"].at(i + 1))
            for b in range(2):
                e.copy(x_hi[:, 4 * b:4 * b + 4, 0:P], ps[:, 4 + b, :].rearrange("p (k s) -> p k s", k=4)).then_inc(sem["x_hi"].sem, 1)

        def gathered_lo(e, i):
            for b in range(2):
                e.wait_ge(sem["x_hi"].sem, sem["x_hi"].at(2 * i + b + 1))
                e.tensor_tensor(x_lo[:, 4 * b:4 * b + 4, 0:P], ps[:, 4 + b, :].rearrange("p (k s) -> p k s", k=4),
                                x_hi[:, 4 * b:4 * b + 4, 0:P].bitcast(F32), ALU.subtract).then_inc(sem["x_lo"].sem, 1)

        def run(e, turn):
            if moe is not None:
                with e.Fori(0, N_EXP - 1) as i:
                    turn(i, False)
            turn(0 if moe is None else N_EXP - 1, True)

        def prefetch(e):
            load_units(e, 0, range(RING))

        class begin:

            def sync(e):
                load_units(e, 0, range(RING, RING + 1))

            def scalar(e, n):
                split_hi(e, 0, n)

            def vector(e, n):
                split_lo(e, 0, n)

            def tensor(e):
                e.nop().then_inc(sem["unit_used"].sem, RING)

        def sync_pass(e):
            if sem is not first:
                prefetch(e)
            if sem is not first or moe is None:
                begin.sync(e)
            load_units(e, 0, range(RING + 1, 2 * RING))
            run(e, lambda i, last: load_units(e, i, range(2 * RING, N_UNITS + (0 if last else 2 * RING))))
            if sem is not first:
                e.wait_ge(sem["split_lo"].sem, sem["split_lo"].at(split_lo_at(N_EXP - 1, N_UNITS - 1)))

        def scalar_pass(e):
            def turn(i, last):
                for n in range(RING, N_UNITS + RING):
                    if n == N_UNITS + 1 and not last:
                        gathered_hi(e, i + 1)
                    if n == N_UNITS + 2 and moe is not None:
                        leave(e, i + 1)
                    if n < N_UNITS or not last:
                        split_hi(e, i, n)
                    if n in hidden_after:
                        silu(e, i, hidden_after[n])
                    if n in transposed_after:
                        hiddenT_hi(e, i, transposed_after[n])
            if sem is not first or moe is None:
                begin.scalar(e, 0)
                begin.scalar(e, 1)
            if moe is not None:
                gathered_hi(e, 0)
            if sem is not first or moe is None:
                begin.scalar(e, 2)
            if moe is not None:
                e.wait_ge(sem["acc_cleared"].sem, sem["acc_cleared"].at(1))
                leave(e, 0)
            run(e, turn)

        def vector_pass(e):
            def turn(i, last):
                for n in range(RING, N_UNITS + RING):
                    if n == N_UNITS + 1 and not last:
                        gathered_lo(e, i + 1)
                    if n == N_UNITS + 1 and moe is not None:
                        back_for(e, bass.ds(i + 1, 1))
                    if n < N_UNITS or not last:
                        split_lo(e, i, n)
                    if n in hidden_after:
                        hidden(e, i, hidden_after[n])
                        if n == AT[("G", 0)] + 2 and moe is not None:
                            add_scattered(e, i)
                            if not last:
                                pick_for(e, bass.ds(i + 2, 1))
                    if n in transposed_after:
                        hiddenT_lo(e, i, transposed_after[n])
            if moe is not None:
                back_for(e, slice(0, 1))
                pick_for(e, slice(1, 2))
            if sem is not first or moe is None:
                begin.vector(e, 0)
            begin.vector(e, 1)
            if moe is not None:
                e.memset(ps[:, 2:4, :], 0.0).then_inc(sem["acc_cleared"].sem, 1)
                gathered_lo(e, 0)
            begin.vector(e, 2)
            run(e, turn)
            if moe is None:
                e.wait_ge(sem["unit_used"].sem, sem["unit_used"].at(unit_used_at(0, N_UNITS - 1)))
                for t in range(T):
                    e.tensor_tensor(h[:, t, :].rearrange("p (n c) -> p n c", n=2), h[:, t, :].rearrange("p (n c) -> p n c", n=2),
                                    ps[:, bZ[t]:bZ[t] + 2, :], ALU.add)
            else:
                add_scattered(e, N_EXP)

        def tensor_pass(e):
            def turn(i, last):
                if moe is not None:
                    transpose_back(e, i)
                    e.wait_ge(sem["x_lo"].sem, sem["x_lo"].at(2 * i + 2))
                for n, (kind, c) in enumerate(UNITS):
                    if n == N_UNITS - 1 and not last:
                        e.wait_ge(sem["scattered"].sem, sem["scattered"].at((i + 1) * T))
                        gather(e, i + 1)
                    unit_product(e, i, n)
                    if (kind, c) == ("G", 0) and moe is not None:
                        scatter(e, i)
                    if (kind, c) == ("U", 1):
                        transpose_hidden(e, i, 0)
                    if kind == "D" and c < CH - 1:
                        transpose_hidden(e, i, c + 1)
            if sem is not first or moe is None:
                begin.tensor(e)
            if moe is not None:
                gather(e, 0)
            run(e, turn)
            if moe is not None:
                transpose_back(e, N_EXP)
                scatter(e, N_EXP)

        def passes(e, one_pass, between=None):
            nonlocal sem
            sem = first
            one_pass(e)
            if moe is None:
                return
            crowded = e.value_load(over[0:1, 0:1], min_val=0, max_val=1)
            with e.If(crowded > 0):
                e.wait_ge(first["scattered"].sem, first["scattered"].at((N_EXP + 1) * T))
                if between is not None:
                    between()
                sem = second
                one_pass(e)
            sem = first

        def launch():
            with nc.Block() as block:
                @block.sync
                def _(e):
                    passes(e, sync_pass)
                    turns = 1 if moe is None else N_EXP

                    def free(n):
                        e.wait_ge(first["split_lo"].sem, first["split_lo"].at(split_lo_at(turns - 1, N_UNITS - RING + n // 2)))
                    load_next(e, free)

                @block.scalar
                def _(e):
                    passes(e, scalar_pass)

                @block.vector
                def _(e):
                    def next_slots():
                        e.tensor_scalar(rank[:, :, :], rank[:, :, :], -float(P), None, ALU.add).then_inc(first["acc_cleared"].sem, 1)
                        e.wait_ge(first["acc_cleared"].sem, first["acc_cleared"].at(2))
                    passes(e, vector_pass, next_slots)

                @block.tensor
                def _(e):
                    passes(e, tensor_pass)
            if moe is None:
                finished(ffn_raw0=16 * N_UNITS // RING, ffn_raw1=16 * N_UNITS // RING, ffn_raw2=16 * N_UNITS // RING,
                         ffn_split_hi=Q, ffn_split_lo=Q, ffn_unit_used=N_UNITS + RING, ffn_silu=CH * T, ffn_hid=CH * T,
                         ffn_hid_T=CH * T, ffn_hidT_hi=CH * T, ffn_hidT_lo=CH * T, ffn_load_due=N_UNITS - RING)

        return prefetch, begin, launch

    _, load_embed, launch_embed = embed(0)
    prefetch, _, dense_swiglu = swiglu({"U": a["w_up_d"][0], "G": a["w_gate_d"][0], "D": a["w_down_d"][0]}, "dense",
                                    load_next=load_embed)
    norm_T(ROW_FFN, True, load=prefetch)
    dense_swiglu()

    launch_embed()

    t7 = inside(experts_at, D * 4)
    pick = t7("pick", (P, T, P))
    back = t7("back", (P, T, P))
    backT = t7("backT", (P, SEQ))
    rank = t7("rank", (P, T, N_EXP + 2))
    gate = t7("gate", (P, T, N_EXP + 2))
    iota = t7("iota", (P, P))
    over = place("over", (P, 1), I32, offset=over_at)

    w_moe = {"U": a["w_up_m"][0], "G": a["w_gate_m"][0], "D": a["w_down_m"][0]}
    moe_small = (pick, back, backT, rank, gate, iota, over)
    _, load_embed, launch_embed = embed(1)
    load_experts, begin_experts, moe_swiglu = swiglu(w_moe, "moe", moe_small, load_next=load_embed)


    PAD = max(WINDOWS)
    t6 = inside(ring_split, 2 * RING * UNIT_B)
    w_pool = t6("w_pool", (P, 4, 2, 256))
    scale_b = t6("scale_b", (P, D))
    inv_pos = t6("inv_pos", (P, 4, PAD))
    win = [t6(f"win{n}", (P, KD, PAD + SEQ)) for n in range(3)]
    pooled = t6("pooled", (P, KD, SEQ))

    def load_pool(e):
        s = sig("pool_loaded")
        for g in range(4):
            e.dma_start(w_pool[:, g, :, :], a["w_pool"][0, g].rearrange("(k p) n -> p k n", p=P)).then_inc(s.sem, 16)
        e.dma_start(scale_b[:, :], a["scale_pool"].partition_broadcast(P)[:, 0, :]).then_inc(s.sem, 16)
        e.dma_start(inv_pos[:, :, :], a["c_invpos"][:, 0:PAD].partition_broadcast(P)).then_inc(s.sem, 16)
        load_experts(e)

    normed = win[0][:, :, PAD:]
    norm_T(ROW_MIX + KD, False, yT=normed, load=load_pool)
    with nc.Block() as block:
        @block.vector
        def _(e):
            link = linker(e, "dve_step")
            for w in win:
                link(e.memset(w[:, :, 0:PAD], 0.0))
            e.wait_ge(sig("pool_loaded").sem, sig("pool_loaded").at(16 * 6))
            src = 0
            for g in range(4):
                step, dst, ch, cut = 1 << g, 1 + g % 2, slice(2 * g, 2 * g + 2), WINDOWS[g] - 1
                link(e.tensor_tensor(win[dst][:, 2 * g:, PAD:], win[src][:, 2 * g:, PAD:],
                                     win[src][:, 2 * g:, PAD - step:PAD + SEQ - step], ALU.add))
                link(e.tensor_tensor(pooled[:, ch, 0:cut], win[dst][:, ch, PAD:PAD + cut],
                                     inv_pos[:, g, 0:cut].unsqueeze(1).to_broadcast([P, 2, cut]), ALU.mult))
                e.scalar_tensor_tensor(out=pooled[:, ch, cut:], in0=win[dst][:, ch, PAD + cut:], scalar=1.0 / WINDOWS[g],
                                       in1=normed[:, ch, cut:], op0=ALU.mult, op1=ALU.subtract)
                e.tensor_tensor(pooled[:, ch, 0:cut], pooled[:, ch, 0:cut], normed[:, ch, 0:cut],
                                ALU.subtract).then_inc(sig("pooled").sem, 1)
                src = dst
            for half in range(2):
                c = slice(half * 512, (half + 1) * 512)
                e.wait_ge(sig("pool_mm").sem, sig("pool_mm").at(half + 1))
                for t in range(T):
                    e.tensor_tensor(h[:, t, c], h[:, t, c], ps[:, 4 + 2 * t + half, :], ALU.add)
            link.end()

        @block.gpsimd
        def _(e):
            e.wait_ge(sig("pool_loaded").sem, sig("pool_loaded").at(16 * 6))
            for g in range(4):
                e.tensor_tensor(w_pool[:, g, :, :], w_pool[:, g, :, :],
                                scale_b[:, g * 256:(g + 1) * 256].unsqueeze(1).to_broadcast([P, 2, 256]),
                                ALU.mult).then_inc(sig("w_scaled").sem, 1)

        @block.tensor
        def _(e):
            for g in range(4):
                e.wait_ge(sig("w_scaled").sem, sig("w_scaled").at(g + 1))
                e.wait_ge(sig("pooled").sem, sig("pooled").at(g + 1))
                for t in range(T):
                    for k in range(2):
                        ins = e.matmul(ps[:, 4 + 2 * t + g // 2, (g % 2) * 256:(g % 2 + 1) * 256],
                                       pooled[:, 2 * g + k, t * P:(t + 1) * P], w_pool[:, g, k, :],
                                       start=(k == 0), stop=(k == 1))
                if g % 2:
                    ins.then_inc(sig("pool_mm").sem, 1)

    t8 = inside(ffn_small + X_B, HID_B)
    w_r = t8("w_r", (P, KD, N_EXP))
    b_r = t8("b_r", (P, N_EXP))
    g_b = t8("g_b", (P, D))
    logit = t8("logit", (P, T, N_EXP))
    top_v = t8("top_v", (P, T, 8))
    top_i = t8("top_i", (P, T, 8), U32)
    top_f = t8("top_f", (P, T, 8))
    sc = t8("sc", (P, T, 8))
    oh = t8("oh", (P, T, 2, N_EXP))
    chosen = t8("chosen", (P, T, N_EXP))
    most = t8("most", (P, 1))
    def load_router(e):
        s = sig("router_loaded")
        e.dma_start(w_r[:, :, :], a["w_router"][0].rearrange("(k p) n -> p k n", p=P)).then_inc(s.sem, 16)
        e.dma_start(b_r[:, :], a["b_router"].partition_broadcast(P)[:, 0, :]).then_inc(s.sem, 16)
        e.dma_start(g_b[:, :], a["norm_ffn"][1:2].partition_broadcast(P)[:, 0, :]).then_inc(s.sem, 16)
        e.dma_start(iota[:, :], a["c_iota"].partition_broadcast(P)[:, 0, :]).then_inc(s.sem, 16)

    norm_T(ROW_FFN + KD, False, yT=yT, load=load_router)
    with nc.Block() as block:
        @block.sync
        def _(e):
            begin_experts.sync(e)

        @block.gpsimd
        def _(e):
            e.wait_ge(sig("router_loaded").sem, sig("router_loaded").at(64))
            for t in range(T):
                e.tensor_tensor(y[:, t, :], y[:, t, :], g_b[:, :], ALU.mult)

        @block.tensor
        def _(e):
            begin_experts.tensor(e)
            e.wait_ge(sig("router_loaded").sem, sig("router_loaded").at(64))
            for t in range(T):
                for k in range(KD):
                    ins = e.matmul(ps[:, t, 0:N_EXP], yT[:, k, t * P:(t + 1) * P], w_r[:, k, :],
                                   start=(k == 0), stop=(k == KD - 1))
                ins.then_inc(sig("logit").sem, 1)
            e.wait_ge(sig("chosen").sem, sig("chosen").at(T))
            e.matmul(ps[:, 2, 0:N_EXP], before[:, :], chosen[:, 0, :], start=True, stop=True)
            e.matmul(ps[:, 3, 0:N_EXP], ones[:, :], chosen[:, 0, :], start=True, stop=False)
            e.matmul(ps[:, 3, 0:N_EXP], before[:, :], chosen[:, 1, :], start=False, stop=True)
            e.matmul(ps[:, 4, 0:N_EXP], ones[:, :], chosen[:, 0, :], start=True, stop=False)
            e.matmul(ps[:, 4, 0:N_EXP], ones[:, :], chosen[:, 1, :], start=False, stop=True).then_inc(sig("ranks").sem, 1)

        @block.scalar
        def _(e):
            begin_experts.scalar(e, 0)
            e.wait_ge(sig("gap").sem, sig("gap").at(1))
            e.activation(sc[:, :, 1], sc[:, :, 0], ACT.Exp).then_inc(sig("gap_exp").sem, 1)
            for n in range(1, RING):
                begin_experts.scalar(e, n)

        @block.vector
        def _(e):
            link = linker(e, "dve_step")
            e.wait_ge(sig("router_loaded").sem, sig("router_loaded").at(64))
            link(e.memset(rank[:, :, :], -1.0))
            link(e.memset(gate[:, :, :], 0.0))
            begin_experts.vector(e, 0)
            for t in range(T):
                e.wait_ge(sig("logit").sem, sig("logit").at(t + 1))
                link(e.tensor_tensor(logit[:, t, :], ps[:, t, 0:N_EXP], b_r[:, :], ALU.add))
                link(e.max(top_v[:, t, :], logit[:, t, :]))
                link(e.max_index(top_i[:, t, :], top_v[:, t, :], logit[:, t, :]))
            link(e.tensor_copy(top_f[:, :, :], top_i[:, :, :]))
            e.tensor_tensor(sc[:, :, 0], top_v[:, :, 1], top_v[:, :, 0], ALU.subtract).then_inc(sig("gap").sem, 1)
            for t in range(T):
                for j in range(2):
                    link(e.tensor_scalar(oh[:, t, j, :], iota[:, 0:N_EXP], top_f[:, t, j:j + 1], None, ALU.is_equal))
                e.tensor_tensor(chosen[:, t, :], oh[:, t, 0, :], oh[:, t, 1, :], ALU.add).then_inc(sig("chosen").sem, 1)
            e.wait_ge(sig("gap_exp").sem, sig("gap_exp").at(1))
            link(e.tensor_scalar(sc[:, :, 2], sc[:, :, 1], 1.0, None, ALU.add))
            link(e.reciprocal(sc[:, :, 3], sc[:, :, 2]))
            link(e.tensor_tensor(sc[:, :, 4], sc[:, :, 3], sc[:, :, 1], ALU.mult))
            e.wait_ge(sig("ranks").sem, sig("ranks").at(1))
            for t in range(T):
                e1 = slice(1, N_EXP + 1)
                link(e.tensor_scalar(gate[:, t, e1], oh[:, t, 0, :], sc[:, t, 3:4], None, ALU.mult))
                link(e.scalar_tensor_tensor(out=gate[:, t, e1], in0=oh[:, t, 1, :], scalar=sc[:, t, 4:5], in1=gate[:, t, e1],
                                            op0=ALU.mult, op1=ALU.add))
                link(e.scalar_tensor_tensor(out=rank[:, t, e1], in0=ps[:, 2 + t, 0:N_EXP], scalar=1.0, in1=chosen[:, t, :],
                                            op0=ALU.add, op1=ALU.mult))
                link(e.tensor_scalar(rank[:, t, e1], rank[:, t, e1], -1.0, None, ALU.add))
            link(e.tensor_reduce(most[:, :], ps[:, 4, 0:N_EXP], AX_X, ALU.max))
            link(e.tensor_scalar(over[:, :], most[:, :], float(P), None, ALU.is_gt))
            link.end()

    moe_swiglu()
    launch_embed()

_INS = ['x', 'p', 'norm_mix', 'norm_ffn', 'w_in_e', 'b_gate_e', 'conv_a', 'norm_h_a', 'norm_q_b', 'norm_k_b',
        'norm_kv_b', 'w_uk_b', 'w_uv_b', 'w_out_e', 'rel_bias', 'w_pool', 'scale_pool', 'w_gate_d', 'w_up_d',
        'w_down_d', 'w_router', 'b_router', 'w_gate_m', 'w_up_m', 'w_down_m', 'w_ple', 'w_ple_gate', 'norm_ple']


def kernel(**inputs):
    import numpy as _np
    import concourse.bacc as _bacc
    from concourse import mybir as _mybir
    from concourse.bass_utils import run_bass_kernel_spmd as _run

    nc = _bacc.Bacc("TRN2", target_bir_lowering=False, num_devices=1)
    arrays, args = {}, {}
    given = {name: _np.ascontiguousarray(inputs[name]) for name in _INS}
    given.update(constants())
    for name, v in given.items():
        arrays[f"in_{name}"] = v
        args[name] = nc.dram_tensor(f"in_{name}", v.shape, _mybir.dt.from_np(v.dtype), kind="ExternalInput").ap()
    out = nc.dram_tensor("out_0", (1, SEQ, D), _mybir.dt.float32, kind="ExternalOutput").ap()
    build(nc, args, out)
    r = _run(nc, [arrays], core_ids=[0])
    return r.results[0]["out_0"]
```
